# Optimizing a Trainium2 kernel written in Bass

```python
import math
import jax, jax.numpy as jnp
from jax import lax
import numpy as np

D_MODEL = 1024
BATCH = 1
SEQ = 512
DEPTH = 2
DEC_BATCH = 8
DEC_SEQ = 1
PAST_LEN = 2048
PAGE_SIZE = 128

N_A_LAYERS = DEPTH // 2
N_B_LAYERS = DEPTH - N_A_LAYERS
H_A = 4
DK_A = D_MODEL // 2 // H_A
DV_A = D_MODEL // H_A
QK_A = H_A * DK_A
VW_A = H_A * DV_A
GATE_RANK = 16
GATE_TAU = 16.0
GLA_CHUNK = 32
IN_A = 2 * QK_A + 2 * VW_A + GATE_RANK
H_B = 8
DH_B = D_MODEL // (2 * H_B)
DV_B = 2 * DH_B
KW_B = H_B * 2 * DH_B
VW_B = H_B * DV_B
Q_BLOCK = 128
N_EXPERTS = 16
N_GROUPS = 4
EXPERTS_PER_GROUP = N_EXPERTS // N_GROUPS
TOP_K = 2
D_FF_EXPERT = D_MODEL // 2
DEEPNORM_ALPHA = (2.0 * DEPTH) ** 0.25
DEEPNORM_BETA = (8.0 * DEPTH) ** -0.25
LN_EPS = 1e-5
RMS_EPS = 1e-6
NEG_BIG = -1e30

kernel_name = 'yoco_gla_diffattn_grouped_moe_step'

def layer_norm(x, g, b):
    xf = x.astype(jnp.float32)
    mu = jnp.mean(xf, axis=-1, keepdims=True)
    var = jnp.mean(jnp.square(xf - mu), axis=-1, keepdims=True)
    y = (xf - mu) * lax.rsqrt(var + LN_EPS) * g.astype(jnp.float32) + b.astype(jnp.float32)
    return y.astype(x.dtype)

def rms_norm(x, g):
    xf = x.astype(jnp.float32)
    y = xf * lax.rsqrt(jnp.mean(jnp.square(xf), axis=-1, keepdims=True) + RMS_EPS) * g.astype(jnp.float32)
    return y.astype(x.dtype)

def modulate(x, shift, scale):
    return x * (1.0 + scale[:, None, :]) + shift[:, None, :]

def alibi_slopes():
    return jnp.asarray([2.0 ** (-8.0 * (i + 1) / H_B) for i in range(H_B)], jnp.float32)

def gla_project(xm, w_in, w_gate_up, b_gate):
    n, t, _ = xm.shape
    p = xm @ w_in
    q, k, v, r, gd = jnp.split(p, [QK_A, 2 * QK_A, 2 * QK_A + VW_A, 2 * QK_A + 2 * VW_A], axis=-1)
    g = jax.nn.log_sigmoid(gd @ w_gate_up + b_gate) / GATE_TAU
    heads = lambda a: a.reshape(n, t, H_A, -1).transpose(0, 2, 1, 3)
    return heads(q) * (DK_A ** -0.5), heads(k), heads(v), heads(g), r.reshape(n, t, H_A, DV_A)

def gla_chunked(q, k, v, g, s0):
    b_, h_, t_, _ = q.shape
    nc = t_ // GLA_CHUNK
    to_chunks = lambda a: a.reshape(b_, h_, nc, GLA_CHUNK, a.shape[-1]).transpose(2, 0, 1, 3, 4)
    causal = jnp.tril(jnp.ones((GLA_CHUNK, GLA_CHUNK), bool))[:, :, None]

    def step(s, xs):
        qc, kc, vc, gc = xs
        cum = jnp.cumsum(gc, axis=2)
        inter = jnp.einsum('bhtk,bhkv->bhtv', qc * jnp.exp(cum), s)
        diff = cum[:, :, :, None, :] - cum[:, :, None, :, :]
        decay = jnp.exp(jnp.where(causal, diff, -jnp.inf))
        attn = jnp.einsum('bhtk,bhsk,bhtsk->bhts', qc, kc, decay)
        intra = jnp.einsum('bhts,bhsv->bhtv', attn, vc)
        last = cum[:, :, -1:, :]
        s_new = jnp.exp(last[:, :, 0])[..., None] * s + jnp.einsum('bhsk,bhsv->bhkv', kc * jnp.exp(last - cum), vc)
        return s_new, inter + intra

    s_fin, o = lax.scan(step, s0, (to_chunks(q), to_chunks(k), to_chunks(v), to_chunks(g)))
    o = o.transpose(1, 2, 0, 3, 4).reshape(b_, h_, t_, DV_A)
    return o, s_fin

def gla_recurrent(q, k, v, g, s0):
    def step(s, xs):
        qt, kt, vt, gt = xs
        s = jnp.exp(gt)[..., None] * s + kt[..., None] * vt[..., None, :]
        return s, jnp.einsum('bhk,bhkv->bhv', qt, s)
    mv = lambda a: jnp.moveaxis(a, 2, 0)
    s_fin, o = lax.scan(step, s0, (mv(q), mv(k), mv(v), mv(g)))
    return o.transpose(1, 2, 0, 3), s_fin

def gla_output(o, r, gn, w_o):
    n, _, t, _ = o.shape
    o = rms_norm(o.transpose(0, 2, 1, 3), gn) * jax.nn.silu(r)
    return o.reshape(n, t, VW_A) @ w_o

def diff_lambda(lq1, lk1, lq2, lk2, lam_init):
    f = lambda a: a.astype(jnp.float32)
    return jnp.exp(jnp.sum(f(lq1) * f(lk1))) - jnp.exp(jnp.sum(f(lq2) * f(lk2))) + lam_init

def diff_attn_prompt(q, k, v, lam):
    b_, t_ = q.shape[:2]
    nb = t_ // Q_BLOCK
    slopes = alibi_slopes()
    kf = k.astype(jnp.float32)
    k1, k2 = kf[..., :DH_B], kf[..., DH_B:]
    vf = v.astype(jnp.float32)
    kpos = jnp.arange(t_)
    qb = q.reshape(b_, nb, Q_BLOCK, H_B, 2 * DH_B).transpose(1, 0, 2, 3, 4)

    def block(xs):
        qblk, i = xs
        qf = qblk.astype(jnp.float32)
        qpos = i * Q_BLOCK + jnp.arange(Q_BLOCK)
        dist = (qpos[:, None] - kpos[None, :]).astype(jnp.float32)
        bias = jnp.where(dist >= 0, -slopes[:, None, None] * dist, -jnp.inf)
        p1 = jax.nn.softmax(jnp.einsum('bqhd,bkhd->bhqk', qf[..., :DH_B], k1) + bias, axis=-1)
        p2 = jax.nn.softmax(jnp.einsum('bqhd,bkhd->bhqk', qf[..., DH_B:], k2) + bias, axis=-1)
        return jnp.einsum('bhqk,bkhv->bqhv', p1 - lam * p2, vf)

    o = lax.map(block, (qb, jnp.arange(nb)))
    return o.transpose(1, 0, 2, 3, 4).reshape(b_, t_, H_B, DV_B)

def diff_attn_sample(q, k_new, v_new, cache_k, cache_v, page_table, lam):
    db, s_ = q.shape[:2]
    n_pages = page_table.shape[1]
    slopes = alibi_slopes()
    qf = q.astype(jnp.float32)
    q1, q2 = qf[..., :DH_B], qf[..., DH_B:]
    qpos = PAST_LEN + jnp.arange(s_)

    def online(m, l, a, s, vf):
        m_new = jnp.maximum(m, jnp.max(s, axis=-1))
        corr = jnp.exp(m - m_new)
        p = jnp.exp(s - m_new[..., None])
        return m_new, l * corr + jnp.sum(p, axis=-1), a * corr[..., None] + jnp.einsum('bhqk,bkhv->bhqv', p, vf)

    def update(carry, k, v, bias):
        m1, l1, a1, m2, l2, a2 = carry
        kf, vf = k.astype(jnp.float32), v.astype(jnp.float32)
        s1 = jnp.einsum('bqhd,bkhd->bhqk', q1, kf[..., :DH_B]) + bias
        s2 = jnp.einsum('bqhd,bkhd->bhqk', q2, kf[..., DH_B:]) + bias
        m1, l1, a1 = online(m1, l1, a1, s1, vf)
        m2, l2, a2 = online(m2, l2, a2, s2, vf)
        return (m1, l1, a1, m2, l2, a2)

    def page_step(carry, xs):
        phys, j = xs
        kpos = j * PAGE_SIZE + jnp.arange(PAGE_SIZE)
        dist = (qpos[:, None] - kpos[None, :]).astype(jnp.float32)
        bias = -slopes[:, None, None] * dist
        return update(carry, cache_k[phys], cache_v[phys], bias), None

    m0 = jnp.full((db, H_B, s_), NEG_BIG, jnp.float32)
    l0 = jnp.zeros((db, H_B, s_), jnp.float32)
    a0 = jnp.zeros((db, H_B, s_, DV_B), jnp.float32)
    carry, _ = lax.scan(page_step, (m0, l0, a0, m0, l0, a0), (page_table.T, jnp.arange(n_pages)))
    dist = (qpos[:, None] - qpos[None, :]).astype(jnp.float32)
    bias = jnp.where(dist >= 0, -slopes[:, None, None] * dist, -jnp.inf)
    m1, l1, a1, m2, l2, a2 = update(carry, k_new, v_new, bias)
    o = a1 / l1[..., None] - lam * (a2 / l2[..., None])
    return o.transpose(0, 2, 1, 3)

def diff_output(o, subln, lam_init, w_o):
    n, t = o.shape[:2]
    o = rms_norm(o, subln) * (1.0 - lam_init)
    return o.reshape(n, t, VW_B).astype(w_o.dtype) @ w_o

def shared_kv(x, c, w_ada_kv, b_ada_kv, w_kv):
    n, t, _ = x.shape
    sh, sc = jnp.split(c @ w_ada_kv + b_ada_kv, 2, axis=-1)
    kv = modulate(x, sh, sc) @ w_kv
    return kv[..., :KW_B].reshape(n, t, H_B, 2 * DH_B), kv[..., KW_B:].reshape(n, t, H_B, DV_B)

def moe_ffn(xm, w_router, b_router, w_gate, w_up, w_down):
    shp = xm.shape
    xt = xm.reshape(-1, D_MODEL)
    probs = jax.nn.softmax((xt @ w_router + b_router).astype(jnp.float32), axis=-1)
    pg = probs.reshape(-1, N_GROUPS, EXPERTS_PER_GROUP)
    gscore = jnp.sum(lax.top_k(pg, TOP_K)[0], axis=-1)
    gidx = jnp.argmax(gscore, axis=-1)
    in_group = jnp.take_along_axis(pg, gidx[:, None, None], axis=1)[:, 0]
    vals, idx = lax.top_k(in_group, TOP_K)
    wts = vals / jnp.sum(vals, axis=-1, keepdims=True)
    eidx = gidx[:, None] * EXPERTS_PER_GROUP + idx
    comb = jnp.sum(jax.nn.one_hot(eidx, N_EXPERTS, dtype=jnp.float32) * wts[..., None], axis=1).astype(xt.dtype)
    y = jnp.zeros_like(xt)
    for e in range(N_EXPERTS):
        h = jax.nn.silu(xt @ w_gate[e]) * (xt @ w_up[e])
        y = y + comb[:, e:e + 1] * (h @ w_down[e])
    return y.reshape(shp)

def setup_inputs(seed: int = 0) -> dict:
    key = jax.random.key(seed)
    ks = iter(jax.random.split(key, 48))
    nrm = lambda shape, scale: scale * jax.random.normal(next(ks), shape, jnp.float32)
    n_pages = PAST_LEN // PAGE_SIZE
    n_pool = (DEC_BATCH * n_pages * 5) // 4
    d_s = D_MODEL ** -0.5
    beta = DEEPNORM_BETA
    col_a = jnp.concatenate([jnp.ones((2 * QK_A,)), jnp.full((VW_A,), beta), jnp.ones((VW_A + GATE_RANK,))])
    col_kv = jnp.concatenate([jnp.ones((KW_B,)), jnp.full((VW_B,), beta)])
    perm = jax.random.permutation(next(ks), n_pool)[:DEC_BATCH * n_pages]
    return {
        'x_prompt': nrm((BATCH, SEQ, D_MODEL), 1.0),
        'x_sample': nrm((DEC_BATCH, DEC_SEQ, D_MODEL), 1.0),
        'c_prompt': nrm((BATCH, D_MODEL), 1.0),
        'c_sample': nrm((DEC_BATCH, D_MODEL), 1.0),
        'state_gla': nrm((N_A_LAYERS, DEC_BATCH, H_A, DK_A, DV_A), 0.5),
        'cache_k': nrm((n_pool, PAGE_SIZE, H_B, 2 * DH_B), 1.0),
        'cache_v': nrm((n_pool, PAGE_SIZE, H_B, DV_B), 1.0),
        'page_table': perm.reshape(DEC_BATCH, n_pages).astype(jnp.int32),
        'w_ada': nrm((DEPTH, D_MODEL, 6 * D_MODEL), 0.5 * d_s),
        'b_ada': nrm((DEPTH, 6 * D_MODEL), 0.02),
        'ln_mix_g': 1.0 + nrm((DEPTH, D_MODEL), 0.02),
        'ln_mix_b': nrm((DEPTH, D_MODEL), 0.02),
        'ln_ffn_g': 1.0 + nrm((DEPTH, D_MODEL), 0.02),
        'ln_ffn_b': nrm((DEPTH, D_MODEL), 0.02),
        'w_in_a': nrm((N_A_LAYERS, D_MODEL, IN_A), d_s) * col_a,
        'w_gate_up_a': nrm((N_A_LAYERS, GATE_RANK, QK_A), GATE_RANK ** -0.5),
        'b_gate_a': nrm((N_A_LAYERS, QK_A), 0.5),
        'gn_a': 1.0 + nrm((N_A_LAYERS, DV_A), 0.02),
        'w_o_a': nrm((N_A_LAYERS, VW_A, D_MODEL), beta * VW_A ** -0.5),
        'w_ada_kv': nrm((D_MODEL, 2 * D_MODEL), 0.5 * d_s),
        'b_ada_kv': nrm((2 * D_MODEL,), 0.02),
        'w_kv': nrm((D_MODEL, KW_B + VW_B), d_s) * col_kv,
        'w_q_b': nrm((N_B_LAYERS, D_MODEL, KW_B), d_s),
        'lam_q1': nrm((N_B_LAYERS, DH_B), 0.1),
        'lam_k1': nrm((N_B_LAYERS, DH_B), 0.1),
        'lam_q2': nrm((N_B_LAYERS, DH_B), 0.1),
        'lam_k2': nrm((N_B_LAYERS, DH_B), 0.1),
        'subln_b': 1.0 + nrm((N_B_LAYERS, DV_B), 0.02),
        'w_o_b': nrm((N_B_LAYERS, VW_B, D_MODEL), beta * VW_B ** -0.5),
        'w_router': nrm((D_MODEL, N_EXPERTS), d_s),
        'b_router': nrm((N_EXPERTS,), 0.01),
        'w_exp_gate': nrm((DEPTH, N_EXPERTS, D_MODEL, D_FF_EXPERT), d_s),
        'w_exp_up': nrm((DEPTH, N_EXPERTS, D_MODEL, D_FF_EXPERT), beta * d_s),
        'w_exp_down': nrm((DEPTH, N_EXPERTS, D_FF_EXPERT, D_MODEL), beta * D_FF_EXPERT ** -0.5),
    }

def reference(x_prompt, x_sample, c_prompt, c_sample, state_gla, cache_k, cache_v, page_table,
              w_ada, b_ada, ln_mix_g, ln_mix_b, ln_ffn_g, ln_ffn_b,
              w_in_a, w_gate_up_a, b_gate_a, gn_a, w_o_a,
              w_ada_kv, b_ada_kv, w_kv,
              w_q_b, lam_q1, lam_k1, lam_q2, lam_k2, subln_b, w_o_b,
              w_router, b_router, w_exp_gate, w_exp_up, w_exp_down):

    def run(x, c, prompt):
        n, t, _ = x.shape
        gla_states = []
        k_sh = None
        v_sh = None
        for l in range(DEPTH):
            sh1, sc1, g1, sh2, sc2, g2 = jnp.split(c @ w_ada[l] + b_ada[l], 6, axis=-1)
            xm = modulate(x, sh1, sc1)
            if l < N_A_LAYERS:
                q, k, v, g, r = gla_project(xm, w_in_a[l], w_gate_up_a[l], b_gate_a[l])
                if prompt:
                    s0 = jnp.zeros((n, H_A, DK_A, DV_A), x.dtype)
                    o, s_fin = gla_chunked(q, k, v, g, s0)
                else:
                    o, s_fin = gla_recurrent(q, k, v, g, state_gla[l])
                gla_states.append(s_fin)
                mix = gla_output(o, r, gn_a[l], w_o_a[l])
            else:
                lb = l - N_A_LAYERS
                lam_init = 0.8 - 0.6 * math.exp(-0.3 * l)
                lam = diff_lambda(lam_q1[lb], lam_k1[lb], lam_q2[lb], lam_k2[lb], lam_init)
                q = (xm @ w_q_b[lb]).reshape(n, t, H_B, 2 * DH_B) * (DH_B ** -0.5)
                if prompt:
                    o = diff_attn_prompt(q, k_sh, v_sh, lam)
                else:
                    o = diff_attn_sample(q, k_sh, v_sh, cache_k, cache_v, page_table, lam)
                mix = diff_output(o, subln_b[lb], lam_init, w_o_b[lb]).astype(x.dtype)
            x = layer_norm(DEEPNORM_ALPHA * x + g1[:, None, :] * mix, ln_mix_g[l], ln_mix_b[l])
            xm = modulate(x, sh2, sc2)
            ff = moe_ffn(xm, w_router, b_router, w_exp_gate[l], w_exp_up[l], w_exp_down[l])
            x = layer_norm(DEEPNORM_ALPHA * x + g2[:, None, :] * ff, ln_ffn_g[l], ln_ffn_b[l])
            if l == N_A_LAYERS - 1:
                k_sh, v_sh = shared_kv(x, c, w_ada_kv, b_ada_kv, w_kv)
        return x, jnp.stack(gla_states), k_sh, v_sh

    y_prompt, s_prompt, k_prompt, v_prompt = run(x_prompt, c_prompt, True)
    y_sample, s_sample, k_sample, v_sample = run(x_sample, c_sample, False)
    bp, tp = x_prompt.shape[:2]
    k_prompt_pages = k_prompt.reshape(bp, tp // PAGE_SIZE, PAGE_SIZE, H_B, 2 * DH_B)
    v_prompt_pages = v_prompt.reshape(bp, tp // PAGE_SIZE, PAGE_SIZE, H_B, DV_B)
    return (y_prompt, y_sample, s_prompt, s_sample, k_prompt_pages, v_prompt_pages, k_sample, v_sample)


_drawn_inputs = setup_inputs


def setup_inputs(seed=0):
    import zlib

    import numpy as np

    out = dict(_drawn_inputs(seed))
    spreads = {}
    factors = {'gn_a': 8.0,
     'lam_q1': 5.151,
     'lam_k1': 3.691,
     'lam_q2': 3.549,
     'lam_k2': 8.0,
     'subln_b': 87.381,
     'b_router': 8.0}
    for name, (base, spread) in spreads.items():
        noise = np.random.default_rng([zlib.crc32(name.encode()), seed]).standard_normal(out[name].shape)
        drawn = base * np.exp(spread * noise) if base else spread * noise
        out[name] = __import__('jax').numpy.asarray(drawn.astype(out[name].dtype))
    for name, factor in factors.items():
        out[name] = (out[name] * factor).astype(out[name].dtype)
    return out
```

```python
import math
from contextlib import ExitStack, nullcontext

import numpy as np
import concourse.bass as bass
from concourse import mybir

F32 = mybir.dt.float32
I32 = mybir.dt.int32
ALU = mybir.AluOpType
ACT = mybir.ActivationFunctionType
AX = mybir.AxisListType

P = 128
D = 1024
KT = D // P
SEQ, NS = 512, 8
TOK = SEQ + NS
TILES = [(i, P) for i in range(SEQ // P)] + [(SEQ // P, NS)]
NTT = len(TILES)
PAST, PAGE = 2048, 128
PAGES = PAST // PAGE
HA, DKA, DVA, CH = 4, 128, 256, 32
HB, DHB, DVB = 8, 64, 128
NE, NG, EPG, FF = 16, 4, 4, 512
DEPTH = 2
ALPHA = (2.0 * DEPTH) ** 0.25
LN_EPS, RMS_EPS, NEG = 1e-5, 1e-6, -1e30
LAM_INIT = 0.8 - 0.6 * math.exp(-0.3 * 1)
TAU = 16.0
SLOT_TILES = (2 * TOK + NE * (P - 1)) // P
SLOTS = SLOT_TILES * P
NVEC = 6 * DEPTH + 2


held = []


def m_semaphore(nc, name):
    s = nc.alloc_semaphore(name=name)
    held.append(s)
    return nullcontext(s)


def end_of_layer(nc):
    nc.all_engine_barrier()
    nc.clear_and_free_semaphores(list(held))
    held.clear()
    nc.all_engine_barrier()


class Mem:
    pass


def rows_of(ap3, i, n):
    return ap3[0:n, i, :]


def allocate(nc, ctx):
    m = Mem()

    def sb(name, shape, dt=F32):
        return ctx.enter_context(nc.sbuf_tensor(name, shape, dt))

    m.x = sb("x_res", [P, NTT, D])
    m.xt = sb("xt", [P, KT, TOK])
    m.mod = sb("mod", [P, 2, 3, D])
    m.lnr = sb("lnr", [P, 2, D])
    m.ident = sb("ident", [P, P])
    m.ones = sb("ones", [P, P])
    m.mv = sb("mv", [P, NTT, 2])
    m.st6 = sb("st6", [P, 2, 6])
    m.rs = sb("rs", [P, 2, NTT])
    m.dest = sb("dest", [P, 2, NTT], I32)
    m.wts = sb("wts", [P, 2, NTT])
    m.idx = sb("idx", [P, SLOT_TILES], I32)
    m.texp = sb("texp", [1, SLOT_TILES], I32)
    m.small = sb("small", [P, 512])
    m.W = sb("arena_w", [P, 24576])
    m.R = sb("arena_r", [P, 10240])
    m.ps = [ctx.enter_context(nc.psum_tensor(f"ps{i}", [P, 512], F32)) for i in range(8)]
    m.psd = lambda n: m.ps[n]
    m.modD = nc.dram_tensor("mod_rows", (NVEC, NS + 1, D), F32).ap()
    m.xmD = nc.dram_tensor("xm_rows", (TOK, D), F32).ap()
    m.yD = [nc.dram_tensor(f"y_rows{l}", (SLOTS, D), F32).ap() for l in range(DEPTH)]
    m.idxD = [nc.dram_tensor(f"slot_token{l}", (SLOTS, 1), I32).ap() for l in range(DEPTH)]
    m.qsD = nc.dram_tensor("q_sample_rows", (NS, D), F32).ap()
    m.newD = [nc.dram_tensor(f"new_{n}_rows", (NS, D), F32).ap() for n in ("k", "v")]
    m.osD = nc.dram_tensor("o_sample_rows", (NS, D), F32).ap()
    return m


def view(t, off, *shape):
    n = int(np.prod(shape))
    v = t[:, off:off + n]
    if len(shape) == 2:
        return v.rearrange("p (a b) -> p a b", b=shape[1])
    if len(shape) == 3:
        return v.rearrange("p (a b c) -> p a b c", b=shape[1], c=shape[2])
    return v


def stage_constants(nc, ctx, m):
    s_z = ctx.enter_context(m_semaphore(nc, "const_filled"))
    with nc.Block() as block:
        @block.gpsimd
        def _(g):
            nc.gpsimd.memset(m.ident[:, :], 0.0).then_inc(s_z, 1)
            nc.gpsimd.memset(m.ones[:, :], 1.0)
            nc.gpsimd.memset(m.mv[:, :, :], 1.0)
            g.wait_ge(s_z, 1)
            nc.gpsimd.affine_select(out=m.ident[:, :], in_=m.ident[:, :], compare_op=ALU.not_equal, fill=1.0,
                                    base=0, pattern=[[-1, P]], channel_multiplier=1)


def stage_ada(nc, ctx, m, a):
    sem = lambda n: ctx.enter_context(m_semaphore(nc, n))
    c_in, ct_ps, ct_ok = sem("ada_c_in"), sem("ada_ct_ps"), sem("ada_ct_ok")
    w_in = [sem(f"ada_w_in{u}") for u in range(2)]
    b_in = [sem(f"ada_b_in{u}") for u in range(2)]
    mm, ev = sem("ada_mm"), sem("ada_ev")
    st = [sem(f"ada_stored{u}") for u in range(2)]
    crow = m.R[0:NS + 1, 0:D]
    ct = view(m.R, D, KT, NS + 1)
    w = [view(m.W, u * KT * D, KT, D) for u in range(2)]
    brow = [m.R[0:NS + 1, (2 + u) * D:(3 + u) * D] for u in range(2)]
    out = [m.R[0:NS + 1, (4 + u) * D:(5 + u) * D] for u in range(2)]
    pw = [a["w_ada"][l].rearrange("(p k) (v n) -> v p k n", k=KT, n=D) for l in range(DEPTH)]
    pw.append(a["w_ada_kv"].rearrange("(p k) (v n) -> v p k n", k=KT, n=D))
    pb = [a["b_ada"][l].rearrange("(v n) -> v n", n=D) for l in range(DEPTH)]
    pb.append(a["b_ada_kv"].rearrange("(v n) -> v n", n=D))
    parts = [(0, 0, 3), (1, 6, 3), (2, 12, 1)]
    with nc.Block() as block:
        @block.sync
        def _(sp):
            sp.dma_start(crow[0:NS, :], a["c_sample"]).then_inc(c_in, 16)
            sp.dma_start(m.R[NS:NS + 1, 0:D], a["c_prompt"]).then_inc(c_in, 16)

            def load(src, i, u, n2):
                sp.dma_start(w[u], pw[src][bass.ds(2 * i + u, 1)].rearrange("a p k n -> p (a k) n")).then_inc(w_in[u], 16)
                sp.dma_start(brow[u], pb[src][bass.ds(2 * i + u, 1)].to_broadcast([NS + 1, D])).then_inc(b_in[u], 16)

            for src, v0, pairs in parts:
                if src == 0:
                    for u in range(2):
                        load(src, 0, u, 0)
                lo = 1 if src == 0 else 0

                def body(i):
                    for u in range(2):
                        sp.wait_ge(mm, 2 * i + (v0 + u - 1))
                        sp.wait_ge(ev, 2 * i + (v0 + u - 1))
                        load(src, i, u, 0)
                if pairs - lo > 1:
                    with sp.Fori(lo, pairs) as i:
                        body(i)
                else:
                    body(lo)
            for u in range(2):
                sp.wait_ge(st[u], 16 * NVEC // 2)

        @block.tensor
        def _(pe):
            pe.wait_ge(c_in, 32)
            for k in range(KT):
                last = nc.tensor.transpose(m.ps[0][:, k * 16:k * 16 + NS + 1],
                                           crow.rearrange("b (p k) -> b k p", k=KT)[:, k, :],
                                           m.ident[0:NS + 1, 0:NS + 1])
            last.then_inc(ct_ps, 1)
            pe.wait_ge(ct_ok, 1)

            def body(i, v0):
                for u in range(2):
                    pe.wait_ge(w_in[u], 16 * i + 8 * v0 + 16)
                    if not (v0 == 0 and isinstance(i, int) and i == 0):
                        pe.wait_ge(ev, 2 * i + (v0 + u - 1))
                    for n in range(2):
                        for k in range(KT):
                            last = nc.tensor.matmul(m.ps[2 * u + n][0:NS + 1, :], ct[:, k, :],
                                                    w[u][:, k, n * 512:(n + 1) * 512],
                                                    start=(k == 0), stop=(k == KT - 1))
                    last.then_inc(mm, 1)
            for src, v0, pairs in parts:
                if src == 0:
                    body(0, 0)
                    with pe.Fori(1, pairs) as i:
                        body(i, v0)
                elif pairs > 1:
                    with pe.Fori(0, pairs) as i:
                        body(i, v0)
                else:
                    body(0, v0)

        @block.vector
        def _(v):
            v.wait_ge(ct_ps, 1)
            nc.vector.tensor_copy(ct, m.ps[0][:, 0:16 * KT].rearrange("p (k c) -> p k c", c=16)[:, :, 0:NS + 1]).then_inc(ct_ok, 1)

            def body(i, v0):
                for u in range(2):
                    v.wait_ge(mm, 2 * i + (v0 + u + 1))
                    v.wait_ge(b_in[u], 16 * i + 8 * v0 + 16)
                    if not (v0 == 0 and isinstance(i, int) and i == 0):
                        v.wait_ge(st[u], 16 * i + 8 * v0)
                    for n in range(2):
                        c = slice(n * 512, (n + 1) * 512)
                        last = nc.vector.tensor_tensor(out[u][:, c], m.ps[2 * u + n][0:NS + 1, :], brow[u][:, c], ALU.add)
                    last.then_inc(ev, 1)
            body(0, 0)
            with v.Fori(1, 3) as i:
                body(i, 0)
            with v.Fori(0, 3) as i:
                body(i, 6)
            body(0, 12)

        @block.scalar
        def _(s):
            def body(i, v0):
                for u in range(2):
                    s.wait_ge(ev, 2 * i + (v0 + u + 1))
                    s.dma_start(m.modD[bass.ds(2 * i + (v0 + u), 1)].rearrange("a b n -> (a b) n"), out[u]).then_inc(st[u], 16)
            with s.Fori(0, NVEC // 2) as i:
                body(i, 0)


def stage_modulate(nc, ctx, m, name, vec, nvec, load_x=None, keep_rows=False):
    sem = lambda n: ctx.enter_context(m_semaphore(nc, f"{name}_{n}"))
    mod_in, x_in, xm_ok, tr, cp = (sem(n) for n in ("mod_in", "x_in", "xm_ok", "transposed", "copied"))
    rows_out = [sem(f"rows_out{u}") for u in range(2)]
    xm = [m.R[:, u * D:(u + 1) * D] for u in range(2)]
    with nc.Block() as block:
        @block.sync
        def _(sp):
            sp.dma_start(m.mod[:, 0, 0:nvec, :], m.modD[vec:vec + nvec, NS, :].partition_broadcast(P)).then_inc(mod_in, 16)
            sp.dma_start(m.mod[0:NS, 1, 0:nvec, :], m.modD[vec:vec + nvec, 0:NS, :].rearrange("v b n -> b v n")).then_inc(mod_in, 16)
            if load_x is not None:
                sp.dma_start(m.x[:, 0:NTT - 1, :], load_x[0].rearrange("b (i p) n -> p (b i) n", p=P)).then_inc(x_in, 16)
                sp.dma_start(m.x[0:NS, NTT - 1, :], load_x[1].rearrange("b s n -> (b s) n")).then_inc(x_in, 16)
            if keep_rows:
                for i, r in TILES:
                    sp.wait_ge(xm_ok, i + 1)
                    sp.dma_start(m.xmD[i * P:i * P + r, :], xm[i % 2][0:r, :]).then_inc(rows_out[i % 2], 16)
                for u in range(2):
                    sp.wait_ge(rows_out[u], 16 * ((NTT + 1 - u) // 2))

        @block.vector
        def _(v):
            v.wait_ge(mod_in, 32)
            nc.vector.tensor_scalar(m.mod[:, 0, 1, :], m.mod[:, 0, 1, :], 1.0, None, ALU.add)
            nc.vector.tensor_scalar(m.mod[0:NS, 1, 1, :], m.mod[0:NS, 1, 1, :], 1.0, None, ALU.add)
            if load_x is not None:
                v.wait_ge(x_in, 32)
            v.drain()
            for i, r in TILES:
                kind = i // (NTT - 1)
                if i >= 2:
                    v.wait_ge(tr, i - 1)
                    if keep_rows:
                        v.wait_ge(rows_out[i % 2], 16 * (i // 2))
                nc.vector.tensor_tensor(xm[i % 2][0:r, :], m.x[0:r, i, :], m.mod[0:r, kind, 1, :], ALU.mult)
                v.drain()
                nc.vector.tensor_tensor(xm[i % 2][0:r, :], xm[i % 2][0:r, :], m.mod[0:r, kind, 0, :], ALU.add).then_inc(xm_ok, 1)

        @block.tensor
        def _(pe):
            for i, r in TILES:
                pe.wait_ge(xm_ok, i + 1)
                if i >= 2:
                    pe.wait_ge(cp, i - 1)
                for k in range(KT):
                    last = nc.tensor.transpose(m.ps[4 * (i % 2) + k // 4][:, (k % 4) * P:(k % 4) * P + r],
                                               xm[i % 2][0:r, :].rearrange("t (p k) -> t k p", k=KT)[:, k, :],
                                               m.ident[0:r, 0:r])
                last.then_inc(tr, 1)

        @block.scalar
        def _(s):
            for i, r in TILES:
                s.wait_ge(tr, i + 1)
                for n in range(2):
                    last = nc.scalar.copy(m.xt[:, 4 * n:4 * n + 4, i * P:i * P + r],
                                          m.ps[4 * (i % 2) + n][:, :].rearrange("p (k t) -> p k t", t=P)[:, :, 0:r])
                last.then_inc(cp, 1)


def stage_gla_project(nc, ctx, m, a):
    sem = lambda n: ctx.enter_context(m_semaphore(nc, f"glap_{n}"))
    w_in = [sem(f"w_in{u}") for u in range(2)]
    g_in, qk_mm, qk_ev, vr_mm, vr_ev, gd_mm, gd_ev, z_mm, z_ev, ab, ex, ln = (sem(n) for n in
        ("g_in", "qk_mm", "qk_ev", "vr_mm", "vr_ev", "gd_mm", "gd_ev", "z_mm", "z_ev", "abs", "exp", "ln"))
    m.wr = [view(m.W, u * 4096, KT, 512) for u in range(2)]
    m.v = view(m.W, 8192, NTT, D)
    m.r = view(m.W, 13312, NTT, D)
    m.q = view(m.W, 18432, HA, TOK)
    m.k = view(m.W, 18432 + HA * TOK, HA, TOK)
    m.g = view(m.R, 0, HA, TOK)
    t1 = view(m.R, HA * TOK, HA, TOK)
    wgd = view(m.R, 2 * HA * TOK, KT, 16)
    wgu = m.R[0:16, 2 * HA * TOK + 128:2 * HA * TOK + 640]
    gd = m.R[0:16, 2 * HA * TOK + 640:2 * HA * TOK + 640 + TOK]
    bg = m.small[:, 0:HA]
    w_src = a["w_in_a"][0].rearrange("(p k) n -> p k n", k=KT)
    with nc.Block() as block:
        @block.sync
        def _(sp):
            for c in range(6):
                if c >= 2:
                    if c - 2 < 2:
                        sp.wait_ge(qk_mm, HA * (c - 1))
                    else:
                        sp.wait_ge(vr_mm, NTT * (c - 3))
                sp.dma_start(m.wr[c % 2], w_src[:, :, c * 512:(c + 1) * 512]).then_inc(w_in[c % 2], 16)
                if c == 1:
                    sp.dma_start(wgd, w_src[:, :, 3072:3088]).then_inc(g_in, 16)
                    sp.dma_start(wgu, a["w_gate_up_a"][0]).then_inc(g_in, 16)
                    with nc.allow_non_contiguous_dma(reason="512 gate offsets, one per partition and head"):
                        sp.dma_start(bg, a["b_gate_a"][0].rearrange("(h p) -> p h", p=P)).then_inc(g_in, 16)

        @block.tensor
        def _(pe):
            for c in range(2):
                pe.wait_ge(w_in[c], 16)
                for h in range(HA):
                    n = c * HA + h
                    if n >= 2:
                        pe.wait_ge(qk_ev, n - 1)
                    for k in range(KT):
                        w = m.wr[c][:, k, h * P:(h + 1) * P]
                        nc.tensor.matmul(m.ps[n % 2][:, :], w, m.xt[:, k, 0:SEQ], start=(k == 0), stop=(k == KT - 1))
                        last = nc.tensor.matmul(m.ps[2 + n % 2][:, 0:NS], w, m.xt[:, k, SEQ:TOK],
                                                start=(k == 0), stop=(k == KT - 1))
                    last.then_inc(qk_mm, 1)
            pe.wait_ge(g_in, 48)
            pe.wait_ge(qk_ev, 2 * HA)
            for k in range(KT):
                nc.tensor.matmul(m.ps[0][0:16, :], wgd[:, k, :], m.xt[:, k, 0:SEQ], start=(k == 0), stop=(k == KT - 1))
                last = nc.tensor.matmul(m.ps[1][0:16, 0:NS], wgd[:, k, :], m.xt[:, k, SEQ:TOK],
                                        start=(k == 0), stop=(k == KT - 1))
            last.then_inc(gd_mm, 1)
            pe.wait_ge(gd_ev, 1)
            for h in range(HA):
                if h >= 1:
                    pe.wait_ge(z_ev, h)
                nc.tensor.matmul(m.ps[2][:, :], wgu[:, h * P:(h + 1) * P], gd[:, 0:SEQ], start=True, stop=True)
                nc.tensor.matmul(m.ps[3][:, 0:NS], wgu[:, h * P:(h + 1) * P], gd[:, SEQ:TOK],
                                 start=True, stop=True).then_inc(z_mm, 1)
            for c in range(4):
                pe.wait_ge(w_in[c % 2], 16 * (c // 2 + 2))
                for i, r in TILES:
                    n = c * NTT + i
                    if n >= 4:
                        pe.wait_ge(vr_ev, n - 3)
                    for k in range(KT):
                        last = nc.tensor.matmul(m.ps[4 + n % 4][0:r, :], m.xt[:, k, i * P:i * P + r],
                                                m.wr[c % 2][:, k, :], start=(k == 0), stop=(k == KT - 1))
                    last.then_inc(vr_mm, 1)

        @block.scalar
        def _(s):
            for n in range(2 * HA):
                s.wait_ge(qk_mm, n + 1)
                dst = (m.q, m.k)[n // HA]
                scale = DKA ** -0.5 if n < HA else 1.0
                nc.scalar.activation(dst[:, n % HA, 0:SEQ], m.ps[n % 2][:, :], ACT.Copy, scale=scale)
                nc.scalar.activation(dst[:, n % HA, SEQ:TOK], m.ps[2 + n % 2][:, 0:NS], ACT.Copy,
                                     scale=scale).then_inc(qk_ev, 1)
            s.wait_ge(z_ev, HA)
            nc.scalar.activation(t1, m.g, ACT.Abs).then_inc(ab, 1)
            s.wait_ge(ab, 1)
            nc.scalar.activation(t1, t1, ACT.Exp, scale=-1.0).then_inc(ex, 1)
            s.wait_ge(ex, 1)
            nc.scalar.activation(t1, t1, ACT.Ln, bias=1.0).then_inc(ln, 1)

        @block.vector
        def _(v):
            v.wait_ge(gd_mm, 1)
            nc.vector.tensor_copy(gd[:, 0:SEQ], m.ps[0][0:16, :])
            nc.vector.tensor_copy(gd[:, SEQ:TOK], m.ps[1][0:16, 0:NS]).then_inc(gd_ev, 1)
            for h in range(HA):
                v.wait_ge(z_mm, h + 1)
                nc.vector.tensor_scalar(m.g[:, h, 0:SEQ], m.ps[2][:, :], bg[:, h:h + 1], None, ALU.add)
                nc.vector.tensor_scalar(m.g[:, h, SEQ:TOK], m.ps[3][:, 0:NS], bg[:, h:h + 1], None, ALU.add).then_inc(z_ev, 1)
            for c in range(4):
                for i, r in TILES:
                    n = c * NTT + i
                    v.wait_ge(vr_mm, n + 1)
                    dst = (m.v, m.r)[c // 2]
                    nc.vector.tensor_copy(dst[0:r, i, (c % 2) * 512:(c % 2 + 1) * 512], m.ps[4 + n % 4][0:r, :]).then_inc(vr_ev, 1)
                if c == 1:
                    v.wait_ge(ln, 1)
                    nc.vector.tensor_scalar(m.g, m.g, 0.0, None, ALU.min)
                    v.drain()
                    nc.vector.tensor_tensor(m.g, m.g, t1, ALU.subtract)
                    v.drain()
                    nc.vector.tensor_scalar(m.g, m.g, 1.0 / TAU, None, ALU.mult)


def stage_gla_prompt(nc, ctx, m, a):
    sem = lambda n: ctx.enter_context(m_semaphore(nc, f"gla_{n}"))
    (start_ok, mask_ok, cum_ok, dif_ok, exp_ok, fac_ok, kl_tr, kl_ok, at_mm, at_ok, v_ok, ds_mm, s_ok, o_mm, o_ev, s_out) = (
        sem(n) for n in ("start_ok", "mask_ok", "cum_ok", "dif_ok", "exp_ok", "fac_ok", "kl_tr", "kl_ok", "at_mm",
                         "at_ok", "v_ok", "ds_mm", "s_ok", "o_mm", "o_ev", "s_out"))
    NCH = P // CH
    off = [HA * TOK]

    def take(*shape):
        v = view(m.R, off[0], *shape)
        off[0] += int(np.prod(shape))
        return v
    cum = take(HA, P)
    mask = take(1, P)[:, 0, :]
    dmid, dlast = take(HA, P), take(HA, P)
    emid, ekey, ecum, elast = take(HA, P), take(HA, P), take(HA, P), take(HA, P)
    kls = take(HA, P)
    ats = take(HA, CH)
    tri = take(1, CH)[:, 0, :]
    S = [view(m.W, u * D, HA, DVA) for u in range(2)]
    vs = view(m.W, 2 * D, HA, DVA)
    eend = view(m.W, 3 * D, HA, NCH)
    qe, qm, km, kl = (view(m.W, 4 * D + j * 512, HA, P) for j in range(4))
    chunks = lambda t: t.rearrange("p h (c t) -> p h c t", t=CH)
    at_ps = m.ps[0][:, 0:P].rearrange("p (h t) -> p h t", t=CH)
    kl_ps = m.ps[1][:, :].rearrange("p (h k) -> p h k", k=P)
    with nc.Block() as block:
        @block.gpsimd
        def _(g):
            nc.gpsimd.memset(mask, 1.0).then_inc(start_ok, 1)
            nc.gpsimd.memset(tri, 1.0).then_inc(start_ok, 1)
            nc.gpsimd.memset(view(m.W, 0, 1, D), 0.0).then_inc(start_ok, 1)
            g.wait_ge(start_ok, 3)
            nc.gpsimd.memset(mask.rearrange("p (c t) -> p c t", t=CH)[:, :, 0:1], 0.0).then_inc(mask_ok, 1)
            for c in range(NCH):
                g.wait_ge(mask_ok, 1 + c)
                nc.gpsimd.affine_select(out=tri[c * CH:(c + 1) * CH, :], in_=tri[c * CH:(c + 1) * CH, :],
                                        compare_op=ALU.is_ge, fill=0.0, base=0, pattern=[[1, CH]],
                                        channel_multiplier=-1).then_inc(mask_ok, 1)

        @block.vector
        def _(v):
            v.wait_ge(mask_ok, 1 + NCH)

            def body(i, first):
                tok = bass.ds(i * P, P)
                if not first:
                    v.wait_ge(exp_ok, i)
                for h in range(HA):
                    last = nc.vector.tensor_tensor_scan(cum[:, h, :], mask, m.g[:, h, tok], 0.0, ALU.mult, ALU.add)
                v.drain()
                c4 = chunks(cum)
                mid = c4[:, :, :, CH // 2 - 1:CH // 2].to_broadcast([P, HA, NCH, CH])
                end = c4[:, :, :, CH - 1:CH].to_broadcast([P, HA, NCH, CH])
                nc.vector.tensor_tensor(chunks(dmid), c4, mid, ALU.subtract)
                nc.vector.tensor_tensor(chunks(dlast), end, c4, ALU.subtract).then_inc(dif_ok, 1)
                v.wait_ge(exp_ok, i + 1)
                if not first:
                    v.wait_ge(o_mm, NCH * i)
                nc.vector.tensor_tensor(kl, m.k[:, :, tok], elast, ALU.mult)
                nc.vector.tensor_tensor(qm, m.q[:, :, tok], emid, ALU.mult)
                nc.vector.tensor_tensor(km, m.k[:, :, tok], ekey, ALU.mult)
                nc.vector.tensor_tensor(qe, m.q[:, :, tok], ecum, ALU.mult).then_inc(fac_ok, 1)
                v.wait_ge(at_mm, i + 1)
                nc.vector.tensor_tensor(ats, at_ps, tri.unsqueeze(1).to_broadcast([P, HA, CH]), ALU.mult).then_inc(at_ok, 1)
                for c in range(NCH):
                    v.wait_ge(ds_mm, NCH * i + c + 1)
                    if c >= 1:
                        v.wait_ge(o_mm, NCH * i + c)
                    for h in range(HA):
                        nc.vector.scalar_tensor_tensor(out=S[(c + 1) % 2][:, h, :], in0=S[c % 2][:, h, :],
                                                       scalar=eend[:, h, c:c + 1],
                                                       in1=m.ps[4 + 2 * (c % 2) + h // 2][:, (h % 2) * DVA:(h % 2 + 1) * DVA],
                                                       op0=ALU.mult, op1=ALU.add).then_inc(s_ok, 1)
                    v.drain()
                v.wait_ge(o_mm, NCH * i + NCH)
                for n in range(2):
                    last = nc.vector.tensor_copy(m.v[:, bass.ds(i, 1), n * 512:(n + 1) * 512].rearrange("p a n -> p (a n)"),
                                                 m.ps[2 + n][:, :])
                last.then_inc(o_ev, 1)
            body(0, True)
            with v.Fori(1, SEQ // P) as i:
                body(i, False)

        @block.scalar
        def _(s):
            def body(i, first):
                if not first:
                    s.wait_ge(o_mm, NCH * i)
                nc.scalar.copy(vs.rearrange("p h n -> p (h n)"), m.v[:, bass.ds(i, 1), :].rearrange("p a n -> p (a n)")).then_inc(v_ok, 1)
                s.wait_ge(dif_ok, i + 1)
                if not first:
                    s.wait_ge(fac_ok, i)
                    s.wait_ge(s_ok, HA * NCH * i)
                nc.scalar.activation(elast, dlast, ACT.Exp)
                nc.scalar.activation(emid, dmid, ACT.Exp)
                nc.scalar.activation(ekey, dmid, ACT.Exp, scale=-1.0)
                nc.scalar.activation(ecum, cum, ACT.Exp)
                nc.scalar.activation(eend, chunks(cum)[:, :, :, CH - 1], ACT.Exp).then_inc(exp_ok, 1)
                s.wait_ge(kl_tr, i + 1)
                nc.scalar.copy(kls, kl_ps).then_inc(kl_ok, 1)
            body(0, True)
            with s.Fori(1, SEQ // P) as i:
                body(i, False)

        @block.tensor
        def _(pe):
            def state(i, c):
                r = slice(c * CH, (c + 1) * CH)
                for h in range(HA):
                    last = nc.tensor.matmul(m.ps[4 + 2 * (c % 2) + h // 2][:, (h % 2) * DVA:(h % 2 + 1) * DVA],
                                            kls[r, h, :], vs[r, h, :], start=True, stop=True, tile_position=(c * CH, 0))
                last.then_inc(ds_mm, 1)

            def body(i, first):
                pe.wait_ge(fac_ok, i + 1)
                for h in range(HA):
                    last = nc.tensor.transpose(kl_ps[:, h, :], kl[:, h, :], m.ident[:, :])
                last.then_inc(kl_tr, 1)
                for h in range(HA):
                    for c in range(NCH):
                        r = slice(c * CH, (c + 1) * CH)
                        last = nc.tensor.matmul(at_ps[r, h, :], km[:, h, r], qm[:, h, r], start=True, stop=True,
                                                tile_position=(0, c * CH))
                last.then_inc(at_mm, 1)
                pe.wait_ge(kl_ok, i + 1)
                pe.wait_ge(v_ok, i + 1)
                pe.wait_ge(at_ok, i + 1)
                if not first:
                    pe.wait_ge(o_ev, i)
                    pe.wait_ge(s_ok, HA * NCH * i)
                state(i, 0)
                for c in range(NCH):
                    r = slice(c * CH, (c + 1) * CH)
                    if c + 1 < NCH:
                        if c >= 1:
                            pe.wait_ge(s_ok, HA * (NCH * i + c))
                        state(i, c + 1)
                    for h in range(HA):
                        o = m.ps[2 + h // 2][r, (h % 2) * DVA:(h % 2 + 1) * DVA]
                        if c >= 1:
                            pe.wait_ge(s_ok, HA * (NCH * i + c - 1) + h + 1)
                        nc.tensor.matmul(o, qe[:, h, r], S[c % 2][:, h, :], start=True, stop=False, tile_position=(0, c * CH))
                        last = nc.tensor.matmul(o, ats[r, h, :], vs[r, h, :], start=False, stop=True,
                                                tile_position=(c * CH, c * CH))
                    last.then_inc(o_mm, 1)
            body(0, True)
            with pe.Fori(1, SEQ // P) as i:
                body(i, False)

        @block.sync
        def _(sp):
            sp.wait_ge(s_ok, HA * NCH * (SEQ // P))
            sp.dma_start(a["s_prompt"].rearrange("l b h k v -> k (l b h) v"), S[0]).then_inc(s_out, 16)
            sp.wait_ge(s_out, 16)


def stage_gla_sample(nc, ctx, m, a):
    sem = lambda n: ctx.enter_context(m_semaphore(nc, f"glas_{n}"))
    st_in, eg_ok, sel_ok, dg_ok, vb_mm, s_ok, o_mm, o_out, qs_ok = (sem(n) for n in
        ("st_in", "eg_ok", "sel_ok", "dg_ok", "vb_mm", "s_ok", "o_mm", "o_out", "qs_ok"))
    st = view(m.W, 0, NS * HA, DVA)
    off = HA * TOK
    eg = view(m.R, off, HA, NS)
    qsel = view(m.R, off + 32, HA, NS * NS)
    sel = m.R[0:NS, off + 32 + HA * NS * NS:off + 32 + HA * NS * NS + NS * P]
    src = a["state_gla"].rearrange("l b h k v -> k (l b h) v")
    dst = a["s_sample"].rearrange("l b h k v -> k (l b h) v")
    with nc.Block() as block:
        @block.sync
        def _(sp):
            sp.dma_start(st, src).then_inc(st_in, 16)
            for b in range(NS):
                sp.wait_ge(s_ok, b + 1)
                sp.dma_start(dst[:, b * HA:(b + 1) * HA, :], st[:, b * HA:(b + 1) * HA, :]).then_inc(o_out, 16)
            sp.wait_ge(o_out, 16 * NS)

        @block.gpsimd
        def _(g):
            nc.gpsimd.memset(sel, 0.0).then_inc(sel_ok, 1)
            g.wait_ge(sel_ok, 1)
            nc.gpsimd.affine_select(out=sel.rearrange("r (b n) -> r b n", n=P), in_=sel.rearrange("r (b n) -> r b n", n=P),
                                    compare_op=ALU.not_equal, fill=1.0, base=0, pattern=[[-1, NS], [0, P]],
                                    channel_multiplier=1).then_inc(dg_ok, 1)

        @block.scalar
        def _(s):
            nc.scalar.activation(eg, m.g[:, :, SEQ:TOK], ACT.Exp).then_inc(eg_ok, 1)

        @block.vector
        def _(v):
            nc.vector.memset(qsel, 0.0)
            v.drain()
            nc.vector.tensor_copy(qsel[:, :, 0:NS * NS:NS + 1], m.q[:, :, SEQ:TOK]).then_inc(qs_ok, 1)
            v.wait_ge(st_in, 16)
            v.wait_ge(eg_ok, 1)
            for b in range(NS):
                for h in range(HA):
                    nc.vector.tensor_scalar(st[:, b * HA + h, :], st[:, b * HA + h, :], eg[:, h, b:b + 1], None, ALU.mult)
                v.wait_ge(vb_mm, b + 1)
                v.drain()
                for h in range(HA):
                    last = nc.vector.scalar_tensor_tensor(
                        out=st[:, b * HA + h, :], in0=m.ps[2 * (b % 2) + h // 2][:, (h % 2) * DVA:(h % 2 + 1) * DVA],
                        scalar=m.k[:, h, SEQ + b:SEQ + b + 1], in1=st[:, b * HA + h, :], op0=ALU.mult, op1=ALU.add)
                last.then_inc(s_ok, 1)
            v.wait_ge(o_mm, 1)
            for h in range(HA):
                nc.vector.tensor_copy(m.v[0:NS, NTT - 1, h * DVA:(h + 1) * DVA], m.ps[4 + h][0:NS, 0:DVA])

        @block.tensor
        def _(pe):
            pe.wait_ge(dg_ok, 1)
            pe.wait_ge(qs_ok, 1)

            def spread(b):
                if b >= 2:
                    pe.wait_ge(s_ok, b - 1)
                for n in range(2):
                    last = nc.tensor.matmul(m.ps[2 * (b % 2) + n][:, :], sel[:, b * P:(b + 1) * P],
                                            m.v[0:NS, NTT - 1, n * 512:(n + 1) * 512], start=True, stop=True)
                last.then_inc(vb_mm, 1)
            spread(0)
            for b in range(NS):
                if b + 1 < NS:
                    spread(b + 1)
                pe.wait_ge(s_ok, b + 1)
                for h in range(HA):
                    last = nc.tensor.matmul(m.ps[4 + h][0:NS, 0:DVA], qsel[:, h, b * NS:(b + 1) * NS], st[:, b * HA + h, :],
                                            start=(b == 0), stop=(b == NS - 1))
            last.then_inc(o_mm, 1)


def stage_mix_output(nc, ctx, m, name, groups, gain, gate_r, factor, w_o):
    sem = lambda n: ctx.enter_context(m_semaphore(nc, f"{name}_{n}"))
    gn_in, w_in, sq_ok, sd_ok, er_ok, row_ok, tr, cp, mm, ev = (sem(n) for n in
        ("gn_in", "w_in", "sq_ok", "sd_ok", "er_ok", "row_ok", "tr", "cp", "mm", "ev"))
    width = D // groups
    gn = m.R[:, 0:width]
    sq = [m.R[:, (1 + u) * D:(2 + u) * D] for u in range(2)]
    er = [m.R[:, (3 + u) * D:(4 + u) * D] for u in range(2)]
    ss = m.R[:, 5 * D:5 * D + NTT * groups].rearrange("p (i g) -> p i g", g=groups)
    rstd = m.R[:, 5 * D + 64:5 * D + 64 + NTT * groups].rearrange("p (i g) -> p i g", g=groups)
    w = view(m.W, 0, KT, D)
    ln = LayerNorm(nc, ctx, m, name)
    with nc.Block() as block:
        @block.sync
        def _(sp):
            sp.dma_start(gn, gain.partition_broadcast(P)).then_inc(gn_in, 16)
            sp.dma_start(w, w_o.rearrange("(p k) n -> p k n", k=KT)).then_inc(w_in, 16)

        @block.scalar
        def _(s):
            for i, r in TILES:
                if gate_r:
                    if i >= 2:
                        s.wait_ge(row_ok, i - 1)
                    nc.scalar.activation(er[i % 2][0:r, :], m.r[0:r, i, :], ACT.Exp, scale=-1.0).then_inc(er_ok, 1)
            s.wait_ge(sq_ok, NTT)
            nc.scalar.activation(rstd, ss, ACT.Sqrt, scale=1.0 / width, bias=m.small[:, 500:501]).then_inc(sd_ok, 1)
            for i, r in TILES:
                s.wait_ge(tr, i + 1)
                for n in range(2):
                    last = nc.scalar.copy(m.xt[:, 4 * n:4 * n + 4, i * P:i * P + r],
                                          m.ps[2 * (i % 2) + n][:, :].rearrange("p (k t) -> p k t", t=P)[:, :, 0:r])
                last.then_inc(cp, 1)
            ln.scalar(s)

        @block.vector
        def _(v):
            nc.vector.memset(ss, 1.0)
            nc.vector.memset(m.small[:, 500:501], RMS_EPS)
            v.wait_ge(gn_in, 16)
            if factor != 1.0:
                nc.vector.tensor_scalar(gn, gn, factor, None, ALU.mult)
            v.drain()
            for i, r in TILES:
                nc.vector.tensor_tensor(sq[i % 2][0:r, :], m.v[0:r, i, :], m.v[0:r, i, :], ALU.mult)
                v.drain()
                nc.vector.tensor_reduce(out=ss[0:r, i, :], in_=sq[i % 2][0:r, :].rearrange("p (g w) -> p g w", g=groups),
                                        axis=AX.X, op=ALU.add).then_inc(sq_ok, 1)
                if gate_r:
                    v.wait_ge(er_ok, i + 1)
                    nc.vector.tensor_scalar(er[i % 2][0:r, :], er[i % 2][0:r, :], 1.0, None, ALU.add)
                    v.drain()
                    nc.vector.reciprocal(er[i % 2][0:r, :], er[i % 2][0:r, :])
                    v.drain()
                    nc.vector.tensor_tensor(m.r[0:r, i, :], m.r[0:r, i, :], er[i % 2][0:r, :], ALU.mult).then_inc(row_ok, 1)
            v.wait_ge(sd_ok, 1)
            nc.vector.reciprocal(rstd, rstd)
            v.drain()
            ready = NTT if gate_r else 0
            for i, r in TILES:
                row = m.v[0:r, i, :].rearrange("p (g w) -> p g w", g=groups)
                nc.vector.tensor_tensor(row, row, rstd[0:r, i, :].unsqueeze(2).to_broadcast([r, groups, width]), ALU.mult)
                v.drain()
                last = nc.vector.tensor_tensor(row, row, gn[0:r, :].unsqueeze(1).to_broadcast([r, groups, width]), ALU.mult)
                if gate_r:
                    v.drain()
                    last = nc.vector.tensor_tensor(m.v[0:r, i, :], m.v[0:r, i, :], m.r[0:r, i, :], ALU.mult)
                last.then_inc(row_ok, 1)
            for i, r in TILES:
                v.wait_ge(mm, i + 1)
                ln.mixed(v, i, r, [m.ps[4 + 2 * (i % 2) + n] for n in range(2)]).then_inc(ev, 1)
                ln.stats(v, i, r)
            ln.normalize(v)

        @block.tensor
        def _(pe):
            ready = NTT if gate_r else 0
            for i, r in TILES:
                pe.wait_ge(row_ok, ready + i + 1)
                if i >= 2:
                    pe.wait_ge(cp, i - 1)
                for k in range(KT):
                    last = nc.tensor.transpose(m.ps[2 * (i % 2) + k // 4][:, (k % 4) * P:(k % 4) * P + r],
                                               m.v[0:r, i, :].rearrange("t (p k) -> t k p", k=KT)[:, k, :],
                                               m.ident[0:r, 0:r])
                last.then_inc(tr, 1)
            pe.wait_ge(w_in, 16)
            for i, r in TILES:
                pe.wait_ge(cp, i + 1)
                if i >= 2:
                    pe.wait_ge(ev, i - 1)
                for n in range(2):
                    for k in range(KT):
                        last = nc.tensor.matmul(m.ps[4 + 2 * (i % 2) + n][0:r, :], m.xt[:, k, i * P:i * P + r],
                                                w[:, k, n * 512:(n + 1) * 512], start=(k == 0), stop=(k == KT - 1))
                last.then_inc(mm, 1)


class LayerNorm:

    def __init__(self, nc, ctx, m, name):
        sem = lambda n: ctx.enter_context(m_semaphore(nc, f"{name}_ln_{n}"))
        self.nc, self.m = nc, m
        self.var_ok, self.sd_ok, self.bias_ok, self.scaled = (sem(n) for n in ("var_ok", "sd_ok", "bias_ok", "scaled"))
        self.done = sem("done")

    def mixed(self, v, i, r, halves):
        nc, m = self.nc, self.m
        for n in range(2):
            c = slice(n * 512, (n + 1) * 512)
            last = nc.vector.tensor_tensor(m.R[0:r, 6 * D + n * 512:6 * D + (n + 1) * 512], halves[n][0:r, :],
                                           m.mod[0:r, i // (NTT - 1), 2, c], ALU.mult)
        return last

    def stats(self, v, i, r):
        nc, m = self.nc, self.m
        v.drain()
        nc.vector.scalar_tensor_tensor(out=m.x[0:r, i, :], in0=m.x[0:r, i, :], scalar=ALPHA,
                                       in1=m.R[0:r, 6 * D:7 * D], op0=ALU.mult, op1=ALU.add)
        v.drain()
        for n in range(2):
            nc.vector.bn_stats(m.st6[0:r, n, :], m.x[0:r, i, n * 512:(n + 1) * 512])
        v.drain()
        nc.vector.bn_aggr(m.mv[0:r, i, :], m.st6[0:r, :, :])

    def normalize(self, v):
        nc, m = self.nc, self.m
        v.drain()
        nc.vector.memset(m.small[:, 501:502], LN_EPS)
        v.drain()
        nc.vector.tensor_copy(m.rs[:, 0, :], m.mv[:, :, 1]).then_inc(self.var_ok, 1)
        v.wait_ge(self.sd_ok, 1)
        nc.vector.reciprocal(m.rs[:, 0, :], m.rs[:, 0, :])
        v.drain()
        nc.vector.scalar_tensor_tensor(out=m.rs[:, 1, :], in0=m.mv[:, :, 0], scalar=-1.0, in1=m.rs[:, 0, :],
                                       op0=ALU.mult, op1=ALU.mult).then_inc(self.bias_ok, 1)
        for i, r in TILES:
            v.wait_ge(self.scaled, i + 1)
            nc.vector.tensor_tensor(m.x[0:r, i, :], m.x[0:r, i, :], m.lnr[0:r, 0, :], ALU.mult)
            v.drain()
            nc.vector.tensor_tensor(m.x[0:r, i, :], m.x[0:r, i, :], m.lnr[0:r, 1, :], ALU.add).then_inc(self.done, 1)

    def scalar(self, s):
        nc, m = self.nc, self.m
        s.wait_ge(self.var_ok, 1)
        nc.scalar.activation(m.rs[:, 0, :], m.rs[:, 0, :], ACT.Sqrt, bias=m.small[:, 501:502]).then_inc(self.sd_ok, 1)
        s.wait_ge(self.bias_ok, 1)
        for i, r in TILES:
            nc.scalar.activation(m.x[0:r, i, :], m.x[0:r, i, :], ACT.Identity, scale=m.rs[0:r, 0, i:i + 1],
                                 bias=m.rs[0:r, 1, i:i + 1]).then_inc(self.scaled, 1)


def stage_route(nc, ctx, m, l, a):
    sem = lambda n: ctx.enter_context(m_semaphore(nc, f"route{l}_{n}"))
    w_in, ln_in, tab, mm, ev, sel_ok, rk_mm, rk2, z_in, z_out, dst_ok, sc_out, ix_in, tri_ok, te_ok = (sem(n) for n in
        ("w_in", "ln_in", "tab", "mm", "ev", "sel_ok", "rk_mm", "rk2", "z_in", "z_out", "dst_ok", "sc_out", "ix_in",
         "tri_ok", "te_ok"))
    ex_ok = sem("ex_ok")
    off = [2 * D]

    def take(*shape):
        v = view(m.R, off[0], *shape)
        off[0] += int(np.prod(shape))
        return v
    wr, br = take(KT, NE), take(1, NE)[:, 0, :]
    L, E, O1, O2, T, RK = (take(NTT, NE) for _ in range(6))
    GS, GM = take(NTT, NG), take(NTT, NG)
    A1, A2, A3 = (take(NTT, 1)[:, :, 0] for _ in range(3))
    G3 = take(NTT, NG)
    valid = take(NTT, 1)[:, :, 0]
    tri = take(1, P)[:, 0, :]
    w16, w4 = take(1, NE)[:, 0, :], take(1, NG)[:, 0, :]
    nt, start, end, zero16 = (take(1, NE)[:, 0, :] for _ in range(4))
    tmp16 = take(1, NE)[:, 0, :]
    cmp_ = take(SLOT_TILES, NE)
    tix, tef = take(1, SLOT_TILES)[:, 0, :], take(1, SLOT_TILES)[:, 0, :]
    toki = take(1, NTT)[:, 0, :].bitcast(I32)
    zi = take(1, SLOT_TILES)[:, 0, :].bitcast(I32)
    t_e = [P, NTT, NE]
    with nc.Block() as block:
        @block.sync
        def _(sp):
            sp.dma_start(wr, a["w_router"].rearrange("(p k) n -> p k n", k=KT)).then_inc(w_in, 16)
            sp.dma_start(br, a["b_router"].partition_broadcast(P)).then_inc(w_in, 16)
            sp.dma_start(m.lnr[:, 0, :], a["ln_ffn_g"][l].partition_broadcast(P)).then_inc(ln_in, 16)
            sp.dma_start(m.lnr[:, 1, :], a["ln_ffn_b"][l].partition_broadcast(P)).then_inc(ln_in, 16)
            sp.wait_ge(z_in, 1)
            sp.dma_start(m.idxD[l].rearrange("(p t) a -> p (t a)", p=P), zi).then_inc(z_out, 16)
            sp.wait_ge(sc_out, 16 * 2 * NTT)
            with nc.allow_non_contiguous_dma(reason="slot tokens, one per partition and tile"):
                sp.dma_start(m.idx[:, :], m.idxD[l].rearrange("(t p) a -> p (t a)", p=P)).then_inc(ix_in, 16)
            sp.wait_ge(ix_in, 16)
            sp.wait_ge(ln_in, 32)

        @block.gpsimd
        def _(g):
            nc.gpsimd.memset(tri, 1.0).then_inc(tri_ok, 1)
            nc.gpsimd.memset(valid, 0.0).then_inc(tri_ok, 1)
            g.wait_ge(tri_ok, 2)
            nc.gpsimd.affine_select(out=tri, in_=tri, compare_op=ALU.is_gt, fill=0.0, base=0, pattern=[[1, P]],
                                    channel_multiplier=-1).then_inc(tab, 1)
            nc.gpsimd.memset(valid[:, 0:NTT - 1], 1.0).then_inc(tab, 1)
            nc.gpsimd.memset(valid[0:NS, NTT - 1:NTT], 1.0).then_inc(tab, 1)
            nc.gpsimd.iota(w16, pattern=[[-1, NE]], base=NE, channel_multiplier=0, allow_small_or_imprecise_dtypes=True).then_inc(tab, 1)
            nc.gpsimd.iota(w4, pattern=[[-1, NG]], base=NG, channel_multiplier=0, allow_small_or_imprecise_dtypes=True).then_inc(tab, 1)
            nc.gpsimd.iota(tix, pattern=[[1, SLOT_TILES]], base=0, channel_multiplier=0,
                           allow_small_or_imprecise_dtypes=True).then_inc(tab, 1)
            nc.gpsimd.iota(toki, pattern=[[P, NTT]], base=0, channel_multiplier=1).then_inc(tab, 1)
            nc.gpsimd.memset(zi, 0).then_inc(z_in, 1)
            g.wait_ge(z_out, 16)
            g.wait_ge(dst_ok, 1)
            g.wait_ge(tab, 7)
            for c in range(2):
                for i, r in TILES:
                    g.indirect_dma_start(out=m.idxD[l], out_offset=bass.IndirectOffsetOnAxis(ap=m.dest[0:r, c, i:i + 1], axis=0),
                                         in_=toki[0:r, i:i + 1], in_offset=None).then_inc(sc_out, 16)

        @block.tensor
        def _(pe):
            pe.wait_ge(w_in, 32)
            for i, r in TILES:
                for k in range(KT):
                    last = nc.tensor.matmul(m.ps[i][0:r, 0:NE], m.xt[:, k, i * P:i * P + r], wr[:, k, :],
                                            start=(k == 0), stop=(k == KT - 1))
            last.then_inc(mm, 1)
            pe.wait_ge(sel_ok, 1)
            pe.wait_ge(tab, 7)
            for i, r in TILES:
                for j in range(i):
                    nc.tensor.matmul(m.ps[i][:, 0:NE], m.ones[:, :], T[:, j, :], start=(j == 0), stop=False)
                nc.tensor.matmul(m.ps[i][:, 0:NE], tri, T[:, i, :], start=(i == 0), stop=True)
            for j in range(NTT):
                last = nc.tensor.matmul(m.ps[5][:, 0:NE], m.ones[:, :], T[:, j, :], start=(j == 0), stop=(j == NTT - 1))
            last.then_inc(rk_mm, 1)

        @block.scalar
        def _(s):
            s.wait_ge(ev, 1)
            nc.scalar.activation(E, L, ACT.Exp).then_inc(ex_ok, 1)

        @block.vector
        def _(v):
            V = nc.vector

            def tt(out, x, y, op):
                last = V.tensor_tensor(out, x, y, op)
                v.drain()
                return last

            def bc(x):
                return x.unsqueeze(2).to_broadcast([P, NTT, x.shape[-1] if False else NE])
            V.memset(L, 0.0)
            v.wait_ge(mm, 1)
            v.wait_ge(w_in, 32)
            v.drain()
            for i, r in TILES:
                V.tensor_tensor(L[0:r, i, :], m.ps[i][0:r, 0:NE], br[0:r, :], ALU.add)
            v.drain()
            V.tensor_reduce(out=A1, in_=L, axis=AX.X, op=ALU.max)
            v.drain()
            V.tensor_tensor(L, L, bc(A1), ALU.subtract).then_inc(ev, 1)
            v.wait_ge(ex_ok, 1)
            V.tensor_reduce(out=A2, in_=E, axis=AX.X, op=ALU.add)
            v.drain()
            V.reciprocal(A2, A2)
            v.drain()
            tt(E, E, bc(A2), ALU.mult)
            e4 = E.rearrange("p i (g e) -> p i g e", e=EPG)
            pairs = [(x, y) for x in range(EPG) for y in range(x + 1, EPG)]
            for n, (x, y) in enumerate(pairs):
                tt(G3 if n else GS, e4[:, :, :, x], e4[:, :, :, y], ALU.add)
                if n:
                    tt(GS, GS, G3, ALU.max)
            v.wait_ge(tab, 7)

            def first_of(onehot, score, best, weights, n):
                V.tensor_reduce(out=best, in_=score, axis=AX.X, op=ALU.max)
                v.drain()
                tt(onehot, score, best.unsqueeze(2).to_broadcast([P, NTT, n]), ALU.is_equal)
                tt(onehot, onehot, weights.unsqueeze(1).to_broadcast([P, NTT, n]), ALU.mult)
                V.tensor_reduce(out=A3, in_=onehot, axis=AX.X, op=ALU.max)
                v.drain()
                tt(onehot, onehot, A3.unsqueeze(2).to_broadcast([P, NTT, n]), ALU.is_equal)
            first_of(GM, GS, A1, w4, NG)
            tt(E.rearrange("p i (g e) -> p i g e", e=EPG), e4, GM.unsqueeze(3).to_broadcast([P, NTT, NG, EPG]), ALU.mult)
            tt(E.rearrange("p i (g e) -> p i g e", e=EPG), e4, GM.unsqueeze(3).to_broadcast([P, NTT, NG, EPG]), ALU.add)
            V.tensor_scalar(E, E, -1.0, None, ALU.add)
            v.drain()
            first_of(O1, E, A1, w16, NE)
            V.scalar_tensor_tensor(out=E, in0=O1, scalar=-4.0, in1=E, op0=ALU.mult, op1=ALU.add)
            v.drain()
            first_of(O2, E, A2, w16, NE)
            tt(A3, A1, A2, ALU.add)
            V.reciprocal(A3, A3)
            v.drain()
            tt(m.wts[:, 0, :], A1, A3, ALU.mult)
            tt(m.wts[:, 1, :], A2, A3, ALU.mult)
            tt(O1, O1, bc(valid), ALU.mult)
            tt(O2, O2, bc(valid), ALU.mult)
            V.tensor_tensor(T, O1, O2, ALU.add).then_inc(sel_ok, 1)
            v.wait_ge(rk_mm, 1)
            V.tensor_scalar(nt, m.ps[5][:, 0:NE], 0.0, None, ALU.is_gt)
            v.drain()
            for c in range(1, NTT):
                V.tensor_scalar(tmp16, m.ps[5][:, 0:NE], float(c * P), None, ALU.is_gt)
                v.drain()
                tt(nt, nt, tmp16, ALU.add)
            V.memset(zero16, 1.0)
            v.drain()
            V.tensor_tensor_scan(end, zero16, nt, 0.0, ALU.mult, ALU.add)
            v.drain()
            tt(start, end, nt, ALU.subtract)
            V.tensor_scalar(start, start, float(P), None, ALU.mult)
            v.drain()
            for i in range(NTT):
                V.tensor_tensor(RK[:, i, :], m.ps[i][:, 0:NE], start, ALU.add)
            v.drain()
            for c, O in enumerate((O1, O2)):
                tt(O, O, RK, ALU.mult)
                V.tensor_reduce(out=A1, in_=O, axis=AX.X, op=ALU.add)
                v.drain()
                V.tensor_copy(m.dest[:, c, :], A1).then_inc(rk2, 1)
                v.drain()
            v.nop().then_inc(dst_ok, 1)
            tt(cmp_, end.unsqueeze(1).to_broadcast([P, SLOT_TILES, NE]), tix.unsqueeze(2).to_broadcast([P, SLOT_TILES, NE]), ALU.is_le)
            V.tensor_reduce(out=tef, in_=cmp_, axis=AX.X, op=ALU.add)
            v.drain()
            V.tensor_scalar(tef, tef, float(NE - 1), None, ALU.min)
            v.drain()
            V.tensor_copy(m.texp[0:1, :], tef[0:1, :]).then_inc(te_ok, 1)


def stage_experts(nc, ctx, m, l, a):
    sem = lambda n: ctx.enter_context(m_semaphore(nc, f"moe{l}_{n}"))
    x_in, wg_in, wu_in, wd_in, y_out = ([sem(f"{n}{u}") for u in range(2)] for n in ("x_in", "wg_in", "wu_in", "wd_in", "y_out"))
    x_tr, x_cp, g_mm, u_mm, e_ok, s_ok, h_ok, h_tr, h_cp, d_mm, y_v, y_s = (sem(n) for n in
        ("x_tr", "x_cp", "g_mm", "u_mm", "e_ok", "s_ok", "h_ok", "h_tr", "h_cp", "d_mm", "y_v", "y_s"))
    NT = SLOT_TILES
    FT = FF // P
    wg = [view(m.W, u * 4096, KT, FF) for u in range(2)]
    wu = [view(m.W, 8192 + u * 4096, KT, FF) for u in range(2)]
    wd = [view(m.W, 16384 + u * 4096, FT, D) for u in range(2)]
    xg = [m.R[:, u * D:(u + 1) * D] for u in range(2)]
    xgt = [view(m.R, 2 * D + u * D, KT, P) for u in range(2)]
    ys = [m.R[:, (4 + u) * D:(5 + u) * D] for u in range(2)]
    es = [m.R[:, 6 * D + u * FF:6 * D + (u + 1) * FF] for u in range(2)]
    hs = [m.R[:, 7 * D + u * FF:7 * D + (u + 1) * FF] for u in range(2)]
    ht = [view(m.R, 8 * D + u * FF, FT, P) for u in range(2)]
    src = [a[n][l] for n in ("w_exp_gate", "w_exp_up", "w_exp_down")]
    pst = [m.ps[0], m.ps[1]]
    psg, psu, psh, psy = m.ps[2], m.ps[3], m.ps[4], [m.ps[5], m.ps[6]]

    def tiles(eng, step):
        step(0, 0, 0)
        step(0, 1, 1)
        with eng.Fori(1, NT // 2 - 1) as i:
            for u in range(2):
                step(i, u, None)
        step(NT // 2 - 1, 0, NT - 2)
        step(NT // 2 - 1, 1, NT - 1)

    with nc.Block() as block:
        @block.sync
        def _(sp):
            def step(i, u, t):
                e = sp.value_load(m.texp[0:1, bass.ds(2 * i + u, 1)], min_val=0, max_val=NE - 1)
                for w, s, done, free, k in ((wg, src[0], wg_in, g_mm, KT), (wu, src[1], wu_in, u_mm, KT), (wd, src[2], wd_in, d_mm, FT)):
                    if t is None or t >= 2:
                        sp.wait_ge(free, 2 * i + u - 1)
                    sp.dma_start(w[u].rearrange("p k n -> p (k n)"),
                                 s[bass.ds(e, 1)].rearrange("a (p k) n -> p (a k n)", k=k)).then_inc(done[u], 16)
            tiles(sp, step)

        @block.gpsimd
        def _(g):
            for t in range(NT):
                u = t % 2
                if t >= 2:
                    g.wait_ge(x_tr, t - 1)
                g.indirect_dma_start(out=xg[u], out_offset=None, in_=m.xmD,
                                     in_offset=bass.IndirectOffsetOnAxis(ap=m.idx[:, t:t + 1], axis=0)).then_inc(x_in[u], 16)

        @block.tensor
        def _(pe):
            def x_transpose(i, u, first):
                pe.wait_ge(x_in[u], 16 * i + 16)
                if not first:
                    pe.wait_ge(x_cp, 2 * i + u)
                for k in range(KT):
                    last = nc.tensor.transpose(pst[k // 4][:, (k % 4) * P:(k % 4 + 1) * P],
                                               xg[u].rearrange("t (p k) -> t k p", k=KT)[:, k, :], m.ident[:, :])
                last.then_inc(x_tr, 1)

            def h_transpose(i, u, n):
                pe.wait_ge(h_ok, n + 1)
                if not (isinstance(n, int) and n == 0):
                    pe.wait_ge(h_cp, n)
                for k in range(FT):
                    last = nc.tensor.transpose(psh[:, k * P:(k + 1) * P],
                                               hs[u].rearrange("t (p k) -> t k p", k=FT)[:, k, :], m.ident[:, :])
                last.then_inc(h_tr, 1)

            def down(u, n, wd_value):
                pe.wait_ge(h_cp, n + 1)
                pe.wait_ge(wd_in[u], wd_value)
                if not (isinstance(n, int) and n == 0):
                    pe.wait_ge(y_v, n)
                    pe.wait_ge(y_s, n)
                for c in range(2):
                    for k in range(FT):
                        last = nc.tensor.matmul(psy[c][:, :], ht[u][:, k, :], wd[u][:, k, c * 512:(c + 1) * 512],
                                                start=(k == 0), stop=(k == FT - 1))
                last.then_inc(d_mm, 1)

            def step(i, u, t):
                n = 2 * i + u
                pe.wait_ge(x_cp, n + 1)
                pe.wait_ge(wg_in[u], 16 * i + 16)
                if t != 0:
                    pe.wait_ge(s_ok, n)
                    pe.wait_ge(e_ok, n)
                for k in range(KT):
                    last = nc.tensor.matmul(psg[:, :], xgt[u][:, k, :], wg[u][:, k, :], start=(k == 0), stop=(k == KT - 1))
                last.then_inc(g_mm, 1)
                if t != 0:
                    h_transpose(None, 1 - u, n - 1)
                if t != NT - 1:
                    x_transpose(i + u, 1 - u, False)
                pe.wait_ge(wu_in[u], 16 * i + 16)
                if t != 0:
                    pe.wait_ge(h_ok, n)
                for k in range(KT):
                    last = nc.tensor.matmul(psu[:, :], xgt[u][:, k, :], wu[u][:, k, :], start=(k == 0), stop=(k == KT - 1))
                last.then_inc(u_mm, 1)
                if t != 0:
                    down(1 - u, n - 1, 16 * i + 16 * u)
            x_transpose(0, 0, True)
            tiles(pe, step)
            h_transpose(None, 1, NT - 1)
            down(1, NT - 1, 16 * (NT // 2))

        @block.scalar
        def _(s):
            def x_copy(u, n, first):
                s.wait_ge(x_tr, n + 1)
                if not first:
                    s.wait_ge(u_mm, n - 1)
                for c in range(2):
                    last = nc.scalar.copy(xgt[u][:, 4 * c:4 * c + 4, :], pst[c][:, :].rearrange("p (k t) -> p k t", t=P))
                last.then_inc(x_cp, 1)

            def h_copy(u, n, first):
                s.wait_ge(h_tr, n + 1)
                if not first:
                    s.wait_ge(d_mm, n - 1)
                nc.scalar.copy(ht[u], psh[:, :].rearrange("p (k t) -> p k t", t=P)).then_inc(h_cp, 1)

            def y_store(i, u, n, first, done):
                s.wait_ge(d_mm, n + 1)
                if not first:
                    s.wait_ge(y_out[u], done)
                nc.scalar.copy(ys[u][:, 512:1024], psy[1][:, :]).then_inc(y_s, 1)
                s.wait_ge(y_s, n + 1)
                s.wait_ge(y_v, n + 1)
                s.dma_start(m.yD[l][bass.ds(n * P, P), :], ys[u]).then_inc(y_out[u], 16)

            def step(i, u, t):
                n = 2 * i + u
                s.wait_ge(g_mm, n + 1)
                if t is None or t >= 2:
                    s.wait_ge(h_ok, n - 1)
                nc.scalar.activation(es[u], psg[:, :], ACT.Exp, scale=-1.0).then_inc(e_ok, 1)
                if t != 0:
                    h_copy(1 - u, n - 1, t in (1, 2))
                if t != NT - 1:
                    x_copy(1 - u, n + 1, t == 0)
                if t != 0:
                    y_store(None, 1 - u, n - 1, t in (1, 2), 16 * i + 16 * u - 16)
            x_copy(0, 0, True)
            tiles(s, step)
            h_copy(1, NT - 1, False)
            y_store(None, 1, NT - 1, False, 16 * (NT // 2 - 1))
            for u in range(2):
                s.wait_ge(y_out[u], 16 * (NT // 2))

        @block.vector
        def _(v):
            V = nc.vector

            def y_copy(u, n, first, done):
                v.wait_ge(d_mm, n + 1)
                if not first:
                    v.wait_ge(y_out[u], done)
                V.tensor_copy(ys[u][:, 0:512], psy[0][:, :]).then_inc(y_v, 1)

            def step(i, u, t):
                n = 2 * i + u
                v.wait_ge(e_ok, n + 1)
                V.tensor_scalar(es[u], es[u], 1.0, None, ALU.add)
                v.drain()
                V.reciprocal(es[u], es[u])
                v.drain()
                V.tensor_tensor(es[u], es[u], psg[:, :], ALU.mult).then_inc(s_ok, 1)
                v.drain()
                v.wait_ge(u_mm, n + 1)
                if t is None or t >= 2:
                    v.wait_ge(h_tr, n - 1)
                V.tensor_tensor(hs[u], es[u], psu[:, :], ALU.mult).then_inc(h_ok, 1)
                if t != 0:
                    y_copy(1 - u, n - 1, t in (1, 2), 16 * i + 16 * u - 16)
            tiles(v, step)
            y_copy(1, NT - 1, False, 16 * (NT // 2 - 1))


def stage_combine(nc, ctx, m, l, stores=None):
    sem = lambda n: ctx.enter_context(m_semaphore(nc, f"comb{l}_{n}"))
    y_in = [sem(f"y_in{u}") for u in range(2)]
    w_ok, f_ok, out = sem("w_ok"), sem("f_ok"), sem("stored")
    y = [[m.R[:, (2 * u + c) * D:(2 * u + c + 1) * D] for c in range(2)] for u in range(2)]
    ln = LayerNorm(nc, ctx, m, f"comb{l}")
    with nc.Block() as block:
        @block.gpsimd
        def _(g):
            for i, r in TILES:
                if i >= 2:
                    g.wait_ge(f_ok, i - 1)
                for c in range(2):
                    g.indirect_dma_start(out=y[i % 2][c][0:r, :], out_offset=None, in_=m.yD[l],
                                         in_offset=bass.IndirectOffsetOnAxis(ap=m.dest[0:r, c, i:i + 1], axis=0)
                                         ).then_inc(y_in[i % 2], 16)

        @block.vector
        def _(v):
            for i, r in TILES:
                v.wait_ge(y_in[i % 2], 32 * (i // 2 + 1))
                y1, y2 = y[i % 2]
                nc.vector.tensor_scalar(y1[0:r, :], y1[0:r, :], m.wts[0:r, 0, i:i + 1], None, ALU.mult)
                v.drain()
                nc.vector.scalar_tensor_tensor(out=y1[0:r, :], in0=y2[0:r, :], scalar=m.wts[0:r, 1, i:i + 1],
                                               in1=y1[0:r, :], op0=ALU.mult, op1=ALU.add)
                v.drain()
                ln.mixed(v, i, r, [y1[:, 0:512], y1[:, 512:1024]]).then_inc(f_ok, 1)
                ln.stats(v, i, r)
            ln.normalize(v)

        @block.scalar
        def _(s):
            ln.scalar(s)

        @block.sync
        def _(sp):
            if stores is not None:
                for i, r in TILES:
                    sp.wait_ge(ln.done, i + 1)
                    dst = (stores[0].rearrange("b t n -> (b t) n")[i * P:(i + 1) * P, :] if i < NTT - 1
                           else stores[1].rearrange("b s n -> (b s) n"))
                    sp.dma_start(dst, m.x[0:r, i, :]).then_inc(out, 16)
                sp.wait_ge(out, 16 * NTT)


def stage_ln_rows(nc, ctx, m, name, g, b):
    s_in = ctx.enter_context(m_semaphore(nc, f"{name}_in"))
    with nc.Block() as block:
        @block.sync
        def _(sp):
            sp.dma_start(m.lnr[:, 0, :], g.partition_broadcast(P)).then_inc(s_in, 16)
            sp.dma_start(m.lnr[:, 1, :], b.partition_broadcast(P)).then_inc(s_in, 16)
            sp.wait_ge(s_in, 32)


def wait(eng, sem, value):
    if not isinstance(value, int) or value > 0:
        eng.wait_ge(sem, value)


def stage_shared_kv(nc, ctx, m, a):
    sem = lambda n: ctx.enter_context(m_semaphore(nc, f"kv_{n}"))
    w_in = [sem(f"w_in{u}") for u in range(2)]
    mm, ev, out = sem("mm"), sem("ev"), sem("stored")
    m.kk = view(m.W, 13312, NTT, D)
    m.vv = view(m.W, 18432, NTT, D)
    w_src = a["w_kv"].rearrange("(p k) n -> p k n", k=KT)
    with nc.Block() as block:
        @block.sync
        def _(sp):
            for c in range(4):
                if c >= 2:
                    sp.wait_ge(mm, NTT * (c - 1))
                sp.dma_start(m.wr[c % 2], w_src[:, :, c * 512:(c + 1) * 512]).then_inc(w_in[c % 2], 16)
            for j, (t, name) in enumerate(((m.kk, "k"), (m.vv, "v"))):
                sp.wait_ge(ev, 2 * NTT * (j + 1))
                sp.dma_start(a[f"{name}_prompt"].rearrange("b g p h d -> p (b g) (h d)"), t[:, 0:NTT - 1, :]).then_inc(out, 16)
                sp.dma_start(a[f"{name}_sample"].rearrange("b s h d -> (b s) (h d)"), t[0:NS, NTT - 1, :]).then_inc(out, 16)
                sp.dma_start(m.newD[j], t[0:NS, NTT - 1, :]).then_inc(out, 16)
            sp.wait_ge(out, 96)

        @block.tensor
        def _(pe):
            for c in range(4):
                pe.wait_ge(w_in[c % 2], 16 * (c // 2 + 1))
                for i, r in TILES:
                    n = c * NTT + i
                    wait(pe, ev, n - 3)
                    for k in range(KT):
                        last = nc.tensor.matmul(m.ps[4 + n % 4][0:r, :], m.xt[:, k, i * P:i * P + r],
                                                m.wr[c % 2][:, k, :], start=(k == 0), stop=(k == KT - 1))
                    last.then_inc(mm, 1)

        @block.vector
        def _(v):
            for c in range(4):
                for i, r in TILES:
                    n = c * NTT + i
                    v.wait_ge(mm, n + 1)
                    nc.vector.tensor_copy((m.kk, m.vv)[c // 2][0:r, i, (c % 2) * 512:(c % 2 + 1) * 512],
                                          m.ps[4 + n % 4][0:r, :]).then_inc(ev, 1)


def stage_queries(nc, ctx, m, a):
    sem = lambda n: ctx.enter_context(m_semaphore(nc, f"q_{n}"))
    w_in = [sem(f"w_in{u}") for u in range(2)]
    mm, ev, smm, sev, qs_out, l_in, l_sum, l_exp, l_row, l_mm, tab0, tab1, tab2, tab3 = (sem(n) for n in
        ("mm", "ev", "smm", "sev", "qs_out", "l_in", "l_sum", "l_exp", "l_row", "l_mm", "tab0", "tab1", "tab2", "tab3"))
    m.qt = view(m.R, 0, HB, SEQ)
    m.dist = m.R[:, 4096:4608]
    m.slope = m.small[:, 16:16 + HB]
    m.lam = m.small[:, 32:33]
    m.coef = m.small[0:2 * HB, 33:34]
    qs = m.R[0:NS, 5120:6144]
    lrow = m.R[0:1, 6144:6400]
    lprod = m.R[0:1, 6400:6528]
    lsum = m.R[0:1, 6528:6530]
    lam1 = m.R[0:1, 6530:6531]
    odd8 = m.R[0:2 * HB, 6600:6608]
    odd1 = m.R[0:2 * HB, 6608:6609]
    w_src = a["w_q_b"][0].rearrange("(p k) n -> p k n", k=KT)
    with nc.Block() as block:
        @block.sync
        def _(sp):
            for n, name in enumerate(("lam_q1", "lam_q2", "lam_k1", "lam_k2")):
                sp.dma_start(lrow[:, n * DHB:(n + 1) * DHB], a[name]).then_inc(l_in, 16)
            for c in range(2):
                sp.dma_start(m.wr[c], w_src[:, :, c * 512:(c + 1) * 512]).then_inc(w_in[c], 16)
            sp.wait_ge(sev, 2)
            sp.dma_start(m.qsD, qs).then_inc(qs_out, 16)
            sp.wait_ge(qs_out, 16)

        @block.gpsimd
        def _(g):
            nc.gpsimd.iota(m.dist, pattern=[[1, SEQ]], base=P - SEQ, channel_multiplier=-1,
                           allow_small_or_imprecise_dtypes=True).then_inc(tab0, 1)
            g.wait_ge(tab0, 1)
            nc.gpsimd.affine_select(out=m.dist, in_=m.dist, compare_op=ALU.is_ge, fill=NEG, base=SEQ - P,
                                    pattern=[[-1, SEQ]], channel_multiplier=1).then_inc(tab1, 1)
            for h in range(HB):
                nc.gpsimd.memset(m.slope[:, h:h + 1], 2.0 ** (-8.0 * (h + 1) / HB)).then_inc(tab1, 1)
            nc.gpsimd.memset(odd8, 0.0).then_inc(tab2, 1)
            g.wait_ge(tab2, 1)
            nc.gpsimd.affine_select(out=odd8, in_=odd8, compare_op=ALU.not_equal, fill=1.0, base=-1,
                                    pattern=[[-2, HB]], channel_multiplier=1).then_inc(tab3, 1)

        @block.tensor
        def _(pe):
            for c in range(2):
                pe.wait_ge(w_in[c], 16)
                for j in range(4):
                    n = 4 * c + j
                    wait(pe, ev, n - 1)
                    for k in range(KT):
                        last = nc.tensor.matmul(m.ps[n % 2][:, :], m.wr[c][:, k, j * P:(j + 1) * P], m.xt[:, k, 0:SEQ],
                                                start=(k == 0), stop=(k == KT - 1))
                    last.then_inc(mm, 1)
                for k in range(KT):
                    last = nc.tensor.matmul(m.ps[2 + c][0:NS, :], m.xt[:, k, SEQ:TOK], m.wr[c][:, k, :],
                                            start=(k == 0), stop=(k == KT - 1))
                last.then_inc(smm, 1)
            pe.wait_ge(l_row, 1)
            nc.tensor.matmul(m.ps[4][:, 0:1], m.ones[0:1, :], lam1, start=True, stop=True).then_inc(l_mm, 1)

        @block.scalar
        def _(s):
            for n in range(HB):
                s.wait_ge(mm, n + 1)
                nc.scalar.activation(m.qt[:, n, :], m.ps[n % 2][:, :], ACT.Copy, scale=DHB ** -0.5).then_inc(ev, 1)
            for c in range(2):
                s.wait_ge(smm, c + 1)
                nc.scalar.activation(qs[:, c * 512:(c + 1) * 512], m.ps[2 + c][0:NS, :], ACT.Copy,
                                     scale=DHB ** -0.5).then_inc(sev, 1)
            s.wait_ge(l_sum, 1)
            nc.scalar.activation(lsum, lsum, ACT.Exp).then_inc(l_exp, 1)

        @block.vector
        def _(v):
            v.wait_ge(l_in, 64)
            nc.vector.tensor_tensor(lprod, lrow[:, 0:2 * DHB], lrow[:, 2 * DHB:4 * DHB], ALU.mult)
            v.drain()
            nc.vector.tensor_reduce(out=lsum, in_=lprod.rearrange("p (a b) -> p a b", b=DHB), axis=AX.X, op=ALU.add).then_inc(l_sum, 1)
            v.wait_ge(l_exp, 1)
            nc.vector.tensor_tensor(lam1, lsum[:, 0:1], lsum[:, 1:2], ALU.subtract)
            v.drain()
            nc.vector.tensor_scalar(lam1, lam1, LAM_INIT, None, ALU.add).then_inc(l_row, 1)
            v.wait_ge(l_mm, 1)
            nc.vector.tensor_copy(m.lam, m.ps[4][:, 0:1])
            v.wait_ge(tab3, 1)
            nc.vector.tensor_reduce(out=odd1, in_=odd8, axis=AX.X, op=ALU.add)
            v.drain()
            nc.vector.tensor_tensor(m.coef, odd1, m.lam[0:2 * HB, :], ALU.mult)
            v.drain()
            nc.vector.tensor_tensor(m.coef, m.coef, odd1, ALU.add)
            v.drain()
            nc.vector.tensor_scalar(m.coef, m.coef, -1.0, 1.0, ALU.mult, ALU.add)


def stage_prompt_attention(nc, ctx, m, a):
    sem = lambda n: ctx.enter_context(m_semaphore(nc, f"pa_{n}"))
    kr_ok, k_tr, kt_ok, sc_mm, sb_ok, nb_ok, p_ok, c_ok, c_tr, c_cp, o_mm, o_ev = (sem(n) for n in
        ("kr_ok", "k_tr", "kt_ok", "sc_mm", "sb_ok", "nb_ok", "p_ok", "c_ok", "c_tr", "c_cp", "o_mm", "o_ev"))
    NQ = SEQ // P
    base = 4608
    khr = view(m.R, base, NQ, P)
    qh = [m.R[:, base + 512 * (1 + u):base + 512 * (2 + u)] for u in range(2)]
    kth = [m.R[:, base + 512 * (3 + u):base + 512 * (4 + u)] for u in range(2)]
    S = [[m.R[:, base + 512 * (5 + 2 * u + j):base + 512 * (6 + 2 * u + j)] for j in range(2)] for u in range(2)]
    ct = [m.R[:, base + 512 * (9 + u):base + 512 * (10 + u)] for u in range(2)]
    mx = [m.small[:, 40 + 2 * u:42 + 2 * u] for u in range(2)]
    ls = [m.small[:, 44 + 2 * u:46 + 2 * u] for u in range(2)]
    units = [(hh, i) for hh in range(2) for i in range(NQ)]

    def pairs(eng, body):
        body(0)
        with eng.Fori(1, HB // 2 - 1) as hp:
            body(hp)
        body(HB // 2 - 1)

    with nc.Block() as block:
        @block.tensor
        def _(pe):
            def k_transpose(h):
                pe.wait_ge(kr_ok, h + 1)
                wait(pe, kt_ok, h)
                for j in range(NQ):
                    last = nc.tensor.transpose(m.ps[0][:, j * P:(j + 1) * P], khr[:, j, :], m.ident[:, :])
                last.then_inc(k_tr, 1)

            def finish(u, hh, i, h):
                pe.wait_ge(c_ok, u + 1)
                wait(pe, c_cp, u)
                for j in range(i + 1):
                    last = nc.tensor.transpose(m.ps[5][:, j * P:(j + 1) * P], S[i % 2][0][:, j * P:(j + 1) * P], m.ident[:, :])
                last.then_inc(c_tr, 1)
                pe.wait_ge(c_cp, u + 1)
                wait(pe, o_ev, u - 1)
                for j in range(i + 1):
                    last = nc.tensor.matmul(m.ps[6 + i % 2][:, 0:DVB], ct[i % 2][:, j * P:(j + 1) * P],
                                            m.vv[:, j, bass.ds(h * DVB, DVB)], start=(j == 0), stop=(j == i))
                last.then_inc(o_mm, 1)

            def body(hp):
                for n, (hh, i) in enumerate(units):
                    u, h = 8 * hp + n, 2 * hp + hh
                    if i == 0:
                        pe.wait_ge(kt_ok, h + 1)
                    wait(pe, sb_ok, 2 * (u - 1))
                    for j in range(2):
                        r = slice(j * DHB, (j + 1) * DHB)
                        last = nc.tensor.matmul(m.ps[1 + 2 * (i % 2) + j][:, 0:(i + 1) * P], qh[hh][r, i * P:(i + 1) * P],
                                                kth[hh][r, 0:(i + 1) * P], start=True, stop=True)
                    last.then_inc(sc_mm, 1)
                    if i == 2 and not (isinstance(h, int) and h == HB - 1):
                        k_transpose(h + 1)
                    if not (isinstance(u, int) and u == 0):
                        ph, pi = (hh, i - 1) if i else (1 - hh, NQ - 1)
                        finish(u - 1, ph, pi, h if i else h - 1)
            k_transpose(0)
            pairs(pe, body)
            finish(HB * NQ - 1, 1, NQ - 1, HB - 1)

        @block.scalar
        def _(s):
            def stage(h, hh):
                wait(s, k_tr, h)
                nc.scalar.copy(khr, m.kk[:, 0:NQ, bass.ds(h * P, P)]).then_inc(kr_ok, 1)
                wait(s, sc_mm, NQ * (h - 1))
                nc.scalar.copy(qh[hh], m.qt[:, bass.ds(h, 1), :].rearrange("p a t -> p (a t)"))

            def k_copy(h, hh):
                s.wait_ge(k_tr, h + 1)
                nc.scalar.copy(kth[hh], m.ps[0][:, :]).then_inc(kt_ok, 1)

            def c_copy(u, i):
                s.wait_ge(c_tr, u + 1)
                wait(s, o_mm, u - 1)
                nc.scalar.copy(ct[i % 2][:, 0:(i + 1) * P], m.ps[5][:, 0:(i + 1) * P]).then_inc(c_cp, 1)

            def body(hp):
                for n, (hh, i) in enumerate(units):
                    u, h = 8 * hp + n, 2 * hp + hh
                    last_head = isinstance(h, int) and h == HB - 1
                    if i == 1 and not last_head:
                        stage(h + 1, 1 - hh)
                    if i == 3 and not last_head:
                        k_copy(h + 1, 1 - hh)
                    s.wait_ge(nb_ok, u + 1)
                    for j in range(2):
                        x = S[i % 2][j][:, 0:(i + 1) * P]
                        last = nc.scalar.activation(x, x, ACT.Exp, bias=mx[i % 2][:, j:j + 1], accum_out=ls[i % 2][:, j:j + 1])
                    last.then_inc(p_ok, 1)
                    if not (isinstance(u, int) and u == 0):
                        c_copy(u - 1, i - 1 if i else NQ - 1)
            stage(0, 0)
            k_copy(0, 0)
            pairs(s, body)
            c_copy(HB * NQ - 1, NQ - 1)

        @block.vector
        def _(v):
            V = nc.vector

            def weigh(u, i):
                v.wait_ge(p_ok, u + 1)
                p1, p2 = (S[i % 2][j][:, 0:(i + 1) * P] for j in range(2))
                V.reciprocal(ls[i % 2], ls[i % 2])
                v.drain()
                V.scalar_tensor_tensor(out=ls[i % 2][:, 1:2], in0=ls[i % 2][:, 1:2], scalar=-1.0, in1=m.lam, op0=ALU.mult, op1=ALU.mult)
                V.tensor_scalar(p1, p1, ls[i % 2][:, 0:1], None, ALU.mult)
                v.drain()
                V.scalar_tensor_tensor(out=p1, in0=p2, scalar=ls[i % 2][:, 1:2], in1=p1, op0=ALU.mult, op1=ALU.add).then_inc(c_ok, 1)

            def keep(u, i, h):
                v.wait_ge(o_mm, u + 1)
                V.tensor_copy(m.v[:, i, bass.ds(h * DVB, DVB)], m.ps[6 + i % 2][:, 0:DVB]).then_inc(o_ev, 1)

            def body(hp):
                for n, (hh, i) in enumerate(units):
                    u, h = 8 * hp + n, 2 * hp + hh
                    w = (i + 1) * P
                    v.wait_ge(sc_mm, u + 1)
                    wait(v, c_tr, u - 1)
                    for j in range(2):
                        V.scalar_tensor_tensor(out=S[i % 2][j][:, 0:w], in0=m.dist[:, SEQ - w:SEQ], scalar=m.slope[:, bass.ds(h, 1)],
                                               in1=m.ps[1 + 2 * (i % 2) + j][:, 0:w], op0=ALU.mult, op1=ALU.add).then_inc(sb_ok, 1)
                    v.drain()
                    for j in range(2):
                        V.tensor_reduce(out=mx[i % 2][:, j:j + 1], in_=S[i % 2][j][:, 0:w], axis=AX.X, op=ALU.max)
                    v.drain()
                    V.tensor_scalar(mx[i % 2], mx[i % 2], -1.0, None, ALU.mult).then_inc(nb_ok, 1)
                    if not (isinstance(u, int) and u == 0):
                        weigh(u - 1, i - 1 if i else NQ - 1)
                    if not (isinstance(u, int) and u <= 1):
                        keep(u - 2, (i - 2) % NQ, h if i >= 2 else h - 1)
            pairs(v, body)
            weigh(HB * NQ - 1, NQ - 1)
            keep(HB * NQ - 2, NQ - 2, HB - 1)
            keep(HB * NQ - 1, NQ - 1, HB - 1)


def stage_sample_attention(nc, ctx, m, a):
    sem = lambda n: ctx.enter_context(m_semaphore(nc, f"sa_{n}"))
    RING = 4
    k_in, v_in = ([sem(f"{n}{u}") for u in range(RING)] for n in ("k_in", "v_in"))
    q_in, kn_in, vn_in, pt_in, o_out, os_in, z_ok, t0, t1, t2 = (sem(n) for n in
        ("q_in", "kn_in", "vn_in", "pt_in", "o_out", "os_in", "z_ok", "t0", "t1", "t2"))
    sc_ok, mx_ok, mx_tr, mr_ok, mb_mm, sh_ok, p_ok, pv_mm, om_ok, or_mm, or_ev = (sem(n) for n in
        ("sc_ok", "mx_ok", "mx_tr", "mr_ok", "mb_mm", "sh_ok", "p_ok", "pv_mm", "om_ok", "or_mm", "or_ev"))
    C = 2 * HB
    NP = PAGES + 1
    kp = [m.W[:, u * D:(u + 1) * D] for u in range(RING)]
    vp = [m.W[:, (RING + u) * D:(RING + u + 1) * D] for u in range(RING)]
    o0 = 13312
    qb, kn, vn = (m.W[:, o0 + j * D:o0 + (j + 1) * D] for j in range(3))
    prod = [m.W[:, o0 + (3 + u) * D:o0 + (4 + u) * D] for u in range(2)]
    bmask = m.W[0:C, o0 + 5 * D:o0 + 6 * D]
    om = m.W[0:C, o0 + 6 * D:o0 + 7 * D]
    orow = m.W[0:1, o0 + 7 * D:o0 + 8 * D]
    o1 = o0 + 8 * D
    S, PR, BT = (view(m.W, o1 + j * NP * C, NP, C) for j in range(3))
    mx = m.W[:, o1 + 3 * NP * C:o1 + 3 * NP * C + C]
    mr = m.W[0:C, o1 + 3 * NP * C + C:o1 + 3 * NP * C + C + 1]
    dg = m.W[0:C, o1 + 3 * NP * C + 2 * C:o1 + 3 * NP * C + 3 * C]
    cf = m.W[0:C, o1 + 3 * NP * C + 3 * C:o1 + 3 * NP * C + 3 * C + 1]
    nd = m.W[:, o1 + 3 * NP * C + 4 * C:o1 + 3 * NP * C + 4 * C + PAGES]
    pt = m.small[0:1, 128:128 + NS * PAGES].bitcast(I32)
    ks = a["cache_k"].rearrange("g p h d -> g p (h d)")
    vs = a["cache_v"].rearrange("g p h d -> g p (h d)")
    PSO, PSL, PSM, PSR = [m.ps[0], m.ps[1]], m.ps[2], m.ps[3], [m.ps[4], m.ps[5]]

    def seqs(eng, body):
        body(0)
        with eng.Fori(1, NS) as b:
            body(b)

    with nc.Block() as block:
        @block.sync
        def _(sp):
            sp.dma_start(pt, a["page_table"].rearrange("b j -> (b j)").unsqueeze(0)).then_inc(pt_in, 16)
            sp.wait_ge(pt_in, 16)

            def body(b):
                wait(sp, sc_ok, NP * b)
                sp.dma_start(qb, m.qsD[bass.ds(b, 1), :].to_broadcast([P, D])).then_inc(q_in, 16)
                if isinstance(b, int):
                    sp.wait_ge(z_ok, 2)
                sp.dma_start(kn[0:1, :], m.newD[0][bass.ds(b, 1), :]).then_inc(kn_in, 16)
                for j in range(PAGES):
                    if not (isinstance(b, int) and j < RING):
                        lag = NP * b + j - RING + 1 if j >= RING else NP * b
                        sp.wait_ge(sc_ok, lag)
                    page = sp.value_load(pt[0:1, bass.ds(b * PAGES + j, 1)], min_val=0, max_val=ks.shape[0] - 1)
                    sp.dma_start(kp[j % RING], ks[bass.ds(page, 1)].rearrange("g p n -> p (g n)")).then_inc(k_in[j % RING], 16)
            seqs(sp, body)
            sp.wait_ge(o_out, 16 * NS)
            sp.dma_start(m.v[0:NS, NTT - 1, :], m.osD).then_inc(os_in, 16)
            sp.wait_ge(os_in, 16)

        @block.gpsimd
        def _(g):
            G = nc.gpsimd
            G.memset(kn, 0.0).then_inc(z_ok, 1)
            G.memset(vn, 0.0).then_inc(z_ok, 1)
            G.memset(bmask, 1.0).then_inc(t0, 1)
            G.iota(nd, pattern=[[P, PAGES]], base=-PAST, channel_multiplier=1, allow_small_or_imprecise_dtypes=True).then_inc(t0, 1)
            G.memset(BT[:, PAGES:NP, :], 0.0).then_inc(t0, 1)
            g.wait_ge(t0, 3)
            b3 = bmask.rearrange("r (h d) -> r h d", d=DVB)
            G.affine_select(out=b3, in_=b3, compare_op=ALU.is_ge, fill=0.0, base=0, pattern=[[-2, HB], [0, DVB]],
                            channel_multiplier=1).then_inc(t1, 1)
            G.affine_select(out=BT[:, PAGES:NP, :], in_=BT[:, PAGES:NP, :], compare_op=ALU.is_ge, fill=NEG, base=0,
                            pattern=[[0, 1], [0, C]], channel_multiplier=-1).then_inc(t1, 1)
            g.wait_ge(t1, 2)
            G.affine_select(out=b3, in_=b3, compare_op=ALU.is_ge, fill=0.0, base=1, pattern=[[2, HB], [0, DVB]],
                            channel_multiplier=-1).then_inc(t2, 1)

        @block.vector
        def _(v):
            V = nc.vector
            v.wait_ge(t2, 1)
            for h in range(HB):
                V.tensor_scalar(BT[:, 0:PAGES, 2 * h:2 * h + 2], nd.unsqueeze(2).to_broadcast([P, PAGES, 2]),
                                2.0 ** (-8.0 * (h + 1) / HB), None, ALU.mult)

            def fold(b, first):
                v.wait_ge(pv_mm, NP * (b + 1))
                V.reciprocal(cf, PSL[0:C, 0:1])
                v.drain()
                V.tensor_tensor(cf, cf, m.coef, ALU.mult)
                v.drain()
                if not first:
                    v.wait_ge(or_mm, b)
                for n in range(2):
                    c = slice(n * 512, (n + 1) * 512)
                    last = V.scalar_tensor_tensor(out=om[:, c], in0=PSO[n][0:C, :], scalar=cf, in1=bmask[:, c], op0=ALU.mult, op1=ALU.mult)
                last.then_inc(om_ok, 1)

            def body(b):
                first = isinstance(b, int) and b == 0
                v.wait_ge(q_in, 16 * b + 16)
                v.wait_ge(kn_in, 16 * b + 16)
                for j in range(NP):
                    if j < PAGES:
                        v.wait_ge(k_in[j % RING], 16 * (PAGES // RING) * b + 16 * (j // RING + 1))
                    V.tensor_tensor(prod[j % 2], kp[j % RING] if j < PAGES else kn, qb, ALU.mult)
                    v.drain()
                    V.tensor_reduce(out=S[:, j, :], in_=prod[j % 2].rearrange("p (c d) -> p c d", d=DHB), axis=AX.X, op=ALU.add).then_inc(sc_ok, 1)
                    if j == 4 and not first:
                        fold(b - 1, isinstance(b, int) and b == 1)
                v.drain()
                V.tensor_tensor(S, S, BT, ALU.add)
                v.drain()
                V.tensor_reduce(out=mx, in_=S.rearrange("p j c -> p c j"), axis=AX.X, op=ALU.max).then_inc(mx_ok, 1)
                v.wait_ge(mx_tr, b + 1)
                V.tensor_reduce(out=mr, in_=PSM[0:C, 0:P], axis=AX.X, op=ALU.max)
                v.drain()
                V.tensor_scalar(dg, m.ident[0:C, 0:C], mr, None, ALU.mult).then_inc(mr_ok, 1)
                v.wait_ge(mb_mm, b + 1)
                V.tensor_tensor(S, S, PSM[:, P:P + C].unsqueeze(1).to_broadcast([P, NP, C]), ALU.subtract).then_inc(sh_ok, 1)
                v.wait_ge(p_ok, b + 1)
            seqs(v, body)
            fold(NS - 1, False)

        @block.scalar
        def _(s):
            s.wait_ge(pt_in, 16)

            def row_out(b):
                s.wait_ge(or_mm, b + 1)
                wait(s, o_out, 16 * b)
                for n in range(2):
                    last = nc.scalar.copy(orow[:, n * 512:(n + 1) * 512], PSR[n][0:1, :])
                last.then_inc(or_ev, 1)
                s.wait_ge(or_ev, b + 1)
                s.dma_start(m.osD[bass.ds(b, 1), :], orow).then_inc(o_out, 16)

            def body(b):
                first = isinstance(b, int) and b == 0
                if first:
                    s.wait_ge(z_ok, 2)
                for j in range(PAGES):
                    if not (first and j < RING):
                        s.wait_ge(pv_mm, NP * b + j - RING + 1 if j >= RING else NP * b)
                    page = s.value_load(pt[0:1, bass.ds(b * PAGES + j, 1)], min_val=0, max_val=ks.shape[0] - 1)
                    s.dma_start(vp[j % RING], vs[bass.ds(page, 1)].rearrange("g p n -> p (g n)")).then_inc(v_in[j % RING], 16)
                    if j == RING - 1:
                        s.dma_start(vn[0:1, :], m.newD[1][bass.ds(b, 1), :]).then_inc(vn_in, 16)
                        s.wait_ge(sh_ok, b + 1)
                        nc.scalar.activation(PR, S, ACT.Exp).then_inc(p_ok, 1)
                        if not first:
                            row_out(b - 1)
            seqs(s, body)
            row_out(NS - 1)

        @block.tensor
        def _(pe):
            def row(b):
                pe.wait_ge(om_ok, b + 1)
                wait(pe, or_ev, b)
                for n in range(2):
                    last = nc.tensor.matmul(PSR[n][:, :], m.ones[0:C, :], om[:, n * 512:(n + 1) * 512], start=True, stop=True)
                last.then_inc(or_mm, 1)

            def body(b):
                first = isinstance(b, int) and b == 0
                pe.wait_ge(mx_ok, b + 1)
                nc.tensor.transpose(PSM[0:C, 0:P], mx, m.ident[:, :]).then_inc(mx_tr, 1)
                pe.wait_ge(mr_ok, b + 1)
                nc.tensor.matmul(PSM[:, P:P + C], m.ones[0:C, :], dg, start=True, stop=True).then_inc(mb_mm, 1)
                if not first:
                    row(b - 1)
                pe.wait_ge(p_ok, b + 1)
                for j in range(NP):
                    if j < PAGES:
                        pe.wait_ge(v_in[j % RING], 16 * (PAGES // RING) * b + 16 * (j // RING + 1))
                    else:
                        pe.wait_ge(vn_in, 16 * b + 16)
                    rows = vp[j % RING] if j < PAGES else vn
                    nc.tensor.matmul(PSL[0:C, 0:1], PR[:, j, :], m.ones[:, 0:1], start=(j == 0), stop=(j == NP - 1))
                    for n in range(2):
                        last = nc.tensor.matmul(PSO[n][0:C, :], PR[:, j, :], rows[:, n * 512:(n + 1) * 512],
                                                start=(j == 0), stop=(j == NP - 1))
                    last.then_inc(pv_mm, 1)
            seqs(pe, body)
            row(NS - 1)


OUTS = [("y_prompt", (1, SEQ, D)), ("y_sample", (NS, 1, D)), ("s_prompt", (1, 1, HA, DKA, DVA)),
        ("s_sample", (1, NS, HA, DKA, DVA)), ("k_prompt", (1, SEQ // PAGE, PAGE, HB, 2 * DHB)),
        ("v_prompt", (1, SEQ // PAGE, PAGE, HB, DVB)), ("k_sample", (NS, 1, HB, 2 * DHB)),
        ("v_sample", (NS, 1, HB, DVB))]


def build(nc, a):
    held.clear()
    with ExitStack() as ctx:
        m = allocate(nc, ctx)
        stage_constants(nc, ctx, m)
        stage_ada(nc, ctx, m, a)
        stage_modulate(nc, ctx, m, "mix0", 0, 3, load_x=(a["x_prompt"], a["x_sample"]))
        stage_ln_rows(nc, ctx, m, "lnm0", a["ln_mix_g"][0], a["ln_mix_b"][0])
        stage_gla_project(nc, ctx, m, a)
        stage_gla_prompt(nc, ctx, m, a)
        stage_gla_sample(nc, ctx, m, a)
        stage_mix_output(nc, ctx, m, "glao", HA, a["gn_a"][0], True, 1.0, a["w_o_a"][0])
        stage_modulate(nc, ctx, m, "ffn0", 3, 3, keep_rows=True)
        stage_route(nc, ctx, m, 0, a)
        stage_experts(nc, ctx, m, 0, a)
        stage_combine(nc, ctx, m, 0)
        end_of_layer(nc)
        stage_modulate(nc, ctx, m, "kvm", 12, 2)
        stage_shared_kv(nc, ctx, m, a)
        stage_modulate(nc, ctx, m, "mix1", 6, 3)
        stage_ln_rows(nc, ctx, m, "lnm1", a["ln_mix_g"][1], a["ln_mix_b"][1])
        stage_queries(nc, ctx, m, a)
        stage_prompt_attention(nc, ctx, m, a)
        stage_sample_attention(nc, ctx, m, a)
        stage_mix_output(nc, ctx, m, "diffo", HB, a["subln_b"][0], False, 1.0 - LAM_INIT, a["w_o_b"][0])
        stage_modulate(nc, ctx, m, "ffn1", 9, 3, keep_rows=True)
        stage_route(nc, ctx, m, 1, a)
        stage_experts(nc, ctx, m, 1, a)
        stage_combine(nc, ctx, m, 1, stores=(a["y_prompt"], a["y_sample"]))


def kernel(**inputs):
    import numpy as _np
    import concourse.bacc as _bacc
    from concourse import mybir as _mybir
    from concourse.bass_utils import run_bass_kernel_spmd as _run

    nc = _bacc.Bacc("TRN2", target_bir_lowering=False, num_devices=1)
    arrays, a = {}, {}
    for name, value in inputs.items():
        x = _np.ascontiguousarray(value)
        arrays[f"in_{name}_dram"] = x
        a[name] = nc.dram_tensor(f"in_{name}_dram", x.shape, _mybir.dt.from_np(x.dtype), kind="ExternalInput").ap()
    for name, shape in OUTS:
        a[name] = nc.dram_tensor(f"out_{name}_dram", shape, F32, kind="ExternalOutput").ap()
    build(nc, a)
    r = _run(nc, [arrays], core_ids=[0])
    return tuple(r.results[0][f"out_{name}_dram"] for name, _ in OUTS)
```

```python
import math
from contextlib import ExitStack, nullcontext

import numpy as np
import concourse.bass as bass
from concourse import mybir

F32 = mybir.dt.float32
I32 = mybir.dt.int32
ALU = mybir.AluOpType
ACT = mybir.ActivationFunctionType
AX = mybir.AxisListType

P = 128
D = 1024
KT = D // P
SEQ, NS = 512, 8
TOK = SEQ + NS
TILES = [(i, P) for i in range(SEQ // P)] + [(SEQ // P, NS)]
NTT = len(TILES)
PAST, PAGE = 2048, 128
PAGES = PAST // PAGE
HA, DKA, DVA, CH = 4, 128, 256, 32
HB, DHB, DVB = 8, 64, 128
NE, NG, EPG, FF = 16, 4, 4, 512
DEPTH = 2
ALPHA = (2.0 * DEPTH) ** 0.25
LN_EPS, RMS_EPS, NEG = 1e-5, 1e-6, -1e30
LAM_INIT = 0.8 - 0.6 * math.exp(-0.3 * 1)
TAU = 16.0
SLOT_TILES = (2 * TOK + NE * (P - 1)) // P
SLOTS = SLOT_TILES * P
MIN_PAIRS = (-(-2 * TOK // P) + 1) // 2
LAST = SLOT_TILES + 1
NVEC = 6 * DEPTH + 2


held = []


def m_semaphore(nc, name):
    s = nc.alloc_semaphore(name=name)
    held.append(s)
    return nullcontext(s)


def end_of_layer(nc):
    nc.all_engine_barrier()
    nc.clear_and_free_semaphores(list(held))
    held.clear()
    nc.all_engine_barrier()


class Mem:
    pass


def rows_of(ap3, i, n):
    return ap3[0:n, i, :]


def allocate(nc, ctx):
    m = Mem()

    def sb(name, shape, dt=F32):
        return ctx.enter_context(nc.sbuf_tensor(name, shape, dt))

    m.x = sb("x_res", [P, NTT, D])
    m.xt = sb("xt", [P, KT, TOK])
    m.mod = sb("mod", [P, 2, 3, D])
    m.lnr = sb("lnr", [P, 2, D])
    m.ident = sb("ident", [P, P])
    m.ones = sb("ones", [P, P])
    m.mv = sb("mv", [P, NTT, 2])
    m.st6 = sb("st6", [P, 2, 6])
    m.rs = sb("rs", [P, 2, NTT])
    m.dest = sb("dest", [P, 2, NTT], I32)
    m.wts = sb("wts", [P, 2, NTT])
    m.idx = sb("idx", [P, SLOT_TILES], I32)
    m.texp = sb("texp", [1, SLOT_TILES + 1], I32)
    m.small = sb("small", [P, 512])
    m.W = sb("arena_w", [P, 24576])
    m.R = sb("arena_r", [P, 10240])
    m.ps = [ctx.enter_context(nc.psum_tensor(f"ps{i}", [P, 512], F32)) for i in range(8)]
    m.psd = lambda n: m.ps[n]
    m.modD = nc.dram_tensor("mod_rows", (NVEC, NS + 1, D), F32).ap()
    m.xmD = nc.dram_tensor("xm_rows", (TOK, D), F32).ap()
    m.yD = nc.dram_tensor("y_rows", (SLOTS, D), F32).ap()
    m.idxD = [nc.dram_tensor(f"slot_token{l}", (SLOTS, 1), I32).ap() for l in range(DEPTH)]
    m.qsD = nc.dram_tensor("q_sample_rows", (NS, D), F32).ap()
    m.newD = [nc.dram_tensor(f"new_{n}_rows", (NS, D), F32).ap() for n in ("k", "v")]
    m.osD = nc.dram_tensor("o_sample_rows", (NS, D), F32).ap()
    return m


def view(t, off, *shape):
    n = int(np.prod(shape))
    v = t[:, off:off + n]
    if len(shape) == 2:
        return v.rearrange("p (a b) -> p a b", b=shape[1])
    if len(shape) == 3:
        return v.rearrange("p (a b c) -> p a b c", b=shape[1], c=shape[2])
    return v


def wait(eng, sem, value):
    if not isinstance(value, int) or value > 0:
        eng.wait_ge(sem, value)


def stage_constants(nc, ctx, m):
    s_z = ctx.enter_context(m_semaphore(nc, "const_filled"))
    with nc.Block() as block:
        @block.gpsimd
        def _(g):
            nc.gpsimd.memset(m.ident[:, :], 0.0).then_inc(s_z, 1)
            nc.gpsimd.memset(m.ones[:, :], 1.0)
            nc.gpsimd.memset(m.mv[:, :, :], 1.0)
            g.wait_ge(s_z, 1)
            nc.gpsimd.affine_select(out=m.ident[:, :], in_=m.ident[:, :], compare_op=ALU.not_equal, fill=1.0,
                                    base=0, pattern=[[-1, P]], channel_multiplier=1)


def stage_ada(nc, ctx, m, a):
    sem = lambda n: ctx.enter_context(m_semaphore(nc, n))
    c_in, ct_ps, ct_ok = sem("ada_c_in"), sem("ada_ct_ps"), sem("ada_ct_ok")
    w_in = [sem(f"ada_w_in{u}") for u in range(2)]
    b_in = [sem(f"ada_b_in{u}") for u in range(2)]
    mm, ev = sem("ada_mm"), sem("ada_ev")
    st = [sem(f"ada_stored{u}") for u in range(2)]
    crow = m.R[0:NS + 1, 0:D]
    ct = view(m.R, D, KT, NS + 1)
    w = [view(m.W, u * KT * D, KT, D) for u in range(2)]
    brow = [m.R[0:NS + 1, (2 + u) * D:(3 + u) * D] for u in range(2)]
    out = [m.R[0:NS + 1, (4 + u) * D:(5 + u) * D] for u in range(2)]
    pw = [a["w_ada"][l].rearrange("(p k) (v n) -> v p k n", k=KT, n=D) for l in range(DEPTH)]
    pw.append(a["w_ada_kv"].rearrange("(p k) (v n) -> v p k n", k=KT, n=D))
    pb = [a["b_ada"][l].rearrange("(v n) -> v n", n=D) for l in range(DEPTH)]
    pb.append(a["b_ada_kv"].rearrange("(v n) -> v n", n=D))
    parts = [(0, 0, 3), (1, 6, 3), (2, 12, 1)]
    with nc.Block() as block:
        @block.sync
        def _(sp):
            sp.dma_start(crow[0:NS, :], a["c_sample"]).then_inc(c_in, 16)
            sp.dma_start(m.R[NS:NS + 1, 0:D], a["c_prompt"]).then_inc(c_in, 16)

            def load(src, i, u, n2):
                sp.dma_start(w[u], pw[src][bass.ds(2 * i + u, 1)].rearrange("a p k n -> p (a k) n")).then_inc(w_in[u], 16)
                sp.dma_start(brow[u], pb[src][bass.ds(2 * i + u, 1)].to_broadcast([NS + 1, D])).then_inc(b_in[u], 16)

            for src, v0, pairs in parts:
                if src == 0:
                    for u in range(2):
                        load(src, 0, u, 0)
                lo = 1 if src == 0 else 0

                def body(i):
                    for u in range(2):
                        sp.wait_ge(mm, 2 * i + (v0 + u - 1))
                        sp.wait_ge(ev, 2 * i + (v0 + u - 1))
                        load(src, i, u, 0)
                if pairs - lo > 1:
                    with sp.Fori(lo, pairs) as i:
                        body(i)
                else:
                    body(lo)
            for u in range(2):
                sp.wait_ge(st[u], 16 * NVEC // 2)

        @block.tensor
        def _(pe):
            pe.wait_ge(c_in, 32)
            for k in range(KT):
                last = nc.tensor.transpose(m.ps[0][:, k * 16:k * 16 + NS + 1],
                                           crow.rearrange("b (p k) -> b k p", k=KT)[:, k, :],
                                           m.ident[0:NS + 1, 0:NS + 1])
            last.then_inc(ct_ps, 1)
            pe.wait_ge(ct_ok, 1)

            def body(i, v0):
                for u in range(2):
                    pe.wait_ge(w_in[u], 16 * i + 8 * v0 + 16)
                    if not (v0 == 0 and isinstance(i, int) and i == 0):
                        pe.wait_ge(ev, 2 * i + (v0 + u - 1))
                    for n in range(2):
                        for k in range(KT):
                            last = nc.tensor.matmul(m.ps[2 * u + n][0:NS + 1, :], ct[:, k, :],
                                                    w[u][:, k, n * 512:(n + 1) * 512],
                                                    start=(k == 0), stop=(k == KT - 1))
                    last.then_inc(mm, 1)
            for src, v0, pairs in parts:
                if src == 0:
                    body(0, 0)
                    with pe.Fori(1, pairs) as i:
                        body(i, v0)
                elif pairs > 1:
                    with pe.Fori(0, pairs) as i:
                        body(i, v0)
                else:
                    body(0, v0)

        @block.vector
        def _(v):
            v.wait_ge(ct_ps, 1)
            nc.vector.tensor_copy(ct, m.ps[0][:, 0:16 * KT].rearrange("p (k c) -> p k c", c=16)[:, :, 0:NS + 1]).then_inc(ct_ok, 1)

            def body(i, v0):
                for u in range(2):
                    v.wait_ge(mm, 2 * i + (v0 + u + 1))
                    v.wait_ge(b_in[u], 16 * i + 8 * v0 + 16)
                    if not (v0 == 0 and isinstance(i, int) and i == 0):
                        v.wait_ge(st[u], 16 * i + 8 * v0)
                    for n in range(2):
                        c = slice(n * 512, (n + 1) * 512)
                        last = nc.vector.tensor_tensor(out[u][:, c], m.ps[2 * u + n][0:NS + 1, :], brow[u][:, c], ALU.add)
                    last.then_inc(ev, 1)
            body(0, 0)
            with v.Fori(1, 3) as i:
                body(i, 0)
            with v.Fori(0, 3) as i:
                body(i, 6)
            body(0, 12)

        @block.scalar
        def _(s):
            def body(i, v0):
                for u in range(2):
                    s.wait_ge(ev, 2 * i + (v0 + u + 1))
                    s.dma_start(m.modD[bass.ds(2 * i + (v0 + u), 1)].rearrange("a b n -> (a b) n"), out[u]).then_inc(st[u], 16)
            with s.Fori(0, NVEC // 2) as i:
                body(i, 0)


def stage_modulate(nc, ctx, m, name, vec, nvec, load_x=None, keep_rows=False):
    sem = lambda n: ctx.enter_context(m_semaphore(nc, f"{name}_{n}"))
    mod_in, x_in, xm_ok, tr, cp = (sem(n) for n in ("mod_in", "x_in", "xm_ok", "transposed", "copied"))
    rows_out = [sem(f"rows_out{u}") for u in range(2)]
    xm = [m.R[:, u * D:(u + 1) * D] for u in range(2)]
    with nc.Block() as block:
        @block.sync
        def _(sp):
            sp.dma_start(m.mod[:, 0, 0:nvec, :], m.modD[vec:vec + nvec, NS, :].partition_broadcast(P)).then_inc(mod_in, 16)
            sp.dma_start(m.mod[0:NS, 1, 0:nvec, :], m.modD[vec:vec + nvec, 0:NS, :].rearrange("v b n -> b v n")).then_inc(mod_in, 16)
            if load_x is not None:
                sp.dma_start(m.x[:, 0:NTT - 1, :], load_x[0].rearrange("b (i p) n -> p (b i) n", p=P)).then_inc(x_in, 16)
                sp.dma_start(m.x[0:NS, NTT - 1, :], load_x[1].rearrange("b s n -> (b s) n")).then_inc(x_in, 16)
            if keep_rows:
                for i, r in TILES:
                    sp.wait_ge(xm_ok, i + 1)
                    sp.dma_start(m.xmD[i * P:i * P + r, :], xm[i % 2][0:r, :]).then_inc(rows_out[i % 2], 16)
                for u in range(2):
                    sp.wait_ge(rows_out[u], 16 * ((NTT + 1 - u) // 2))

        @block.vector
        def _(v):
            v.wait_ge(mod_in, 32)
            nc.vector.tensor_scalar(m.mod[:, 0, 1, :], m.mod[:, 0, 1, :], 1.0, None, ALU.add)
            nc.vector.tensor_scalar(m.mod[0:NS, 1, 1, :], m.mod[0:NS, 1, 1, :], 1.0, None, ALU.add)
            if load_x is not None:
                v.wait_ge(x_in, 32)
            v.drain()
            for i, r in TILES:
                kind = i // (NTT - 1)
                if i >= 2:
                    v.wait_ge(tr, i - 1)
                    if keep_rows:
                        v.wait_ge(rows_out[i % 2], 16 * (i // 2))
                nc.vector.tensor_tensor(xm[i % 2][0:r, :], m.x[0:r, i, :], m.mod[0:r, kind, 1, :], ALU.mult)
                v.drain()
                nc.vector.tensor_tensor(xm[i % 2][0:r, :], xm[i % 2][0:r, :], m.mod[0:r, kind, 0, :], ALU.add).then_inc(xm_ok, 1)

        @block.tensor
        def _(pe):
            for i, r in TILES:
                pe.wait_ge(xm_ok, i + 1)
                if i >= 2:
                    pe.wait_ge(cp, i - 1)
                for k in range(KT):
                    last = nc.tensor.transpose(m.ps[4 * (i % 2) + k // 4][:, (k % 4) * P:(k % 4) * P + r],
                                               xm[i % 2][0:r, :].rearrange("t (p k) -> t k p", k=KT)[:, k, :],
                                               m.ident[0:r, 0:r])
                last.then_inc(tr, 1)

        @block.scalar
        def _(s):
            for i, r in TILES:
                s.wait_ge(tr, i + 1)
                for n in range(2):
                    last = nc.scalar.copy(m.xt[:, 4 * n:4 * n + 4, i * P:i * P + r],
                                          m.ps[4 * (i % 2) + n][:, :].rearrange("p (k t) -> p k t", t=P)[:, :, 0:r])
                last.then_inc(cp, 1)


def stage_gla_project(nc, ctx, m, a):
    sem = lambda n: ctx.enter_context(m_semaphore(nc, f"glap_{n}"))
    w_in = [sem(f"w_in{u}") for u in range(2)]
    g_in, qk_mm, qk_ev, vr_mm, vr_ev, gd_mm, gd_ev, z_mm, z_ev, ab, ex, ln = (sem(n) for n in
        ("g_in", "qk_mm", "qk_ev", "vr_mm", "vr_ev", "gd_mm", "gd_ev", "z_mm", "z_ev", "abs", "exp", "ln"))
    m.wr = [view(m.W, u * 4096, KT, 512) for u in range(2)]
    m.v = view(m.W, 8192, NTT, D)
    m.r = view(m.W, 13312, NTT, D)
    m.q = view(m.W, 18432, HA, TOK)
    m.k = view(m.W, 18432 + HA * TOK, HA, TOK)
    m.g = view(m.R, 0, HA, TOK)
    t1 = view(m.R, HA * TOK, HA, TOK)
    wgd = view(m.R, 2 * HA * TOK, KT, 16)
    wgu = m.R[0:16, 2 * HA * TOK + 128:2 * HA * TOK + 640]
    gd = m.R[0:16, 2 * HA * TOK + 640:2 * HA * TOK + 640 + TOK]
    bg = m.small[:, 0:HA]
    w_src = a["w_in_a"][0].rearrange("(p k) n -> p k n", k=KT)
    with nc.Block() as block:
        @block.sync
        def _(sp):
            for c in range(6):
                if c >= 2:
                    if c - 2 < 2:
                        sp.wait_ge(qk_mm, HA * (c - 1))
                    else:
                        sp.wait_ge(vr_mm, NTT * (c - 3))
                sp.dma_start(m.wr[c % 2], w_src[:, :, c * 512:(c + 1) * 512]).then_inc(w_in[c % 2], 16)
                if c == 1:
                    sp.dma_start(wgd, w_src[:, :, 3072:3088]).then_inc(g_in, 16)
                    sp.dma_start(wgu, a["w_gate_up_a"][0]).then_inc(g_in, 16)
                    with nc.allow_non_contiguous_dma(reason="512 gate offsets, one per partition and head"):
                        sp.dma_start(bg, a["b_gate_a"][0].rearrange("(h p) -> p h", p=P)).then_inc(g_in, 16)

        @block.tensor
        def _(pe):
            for c in range(2):
                pe.wait_ge(w_in[c], 16)
                for h in range(HA):
                    n = c * HA + h
                    if n >= 2:
                        pe.wait_ge(qk_ev, n - 1)
                    for k in range(KT):
                        w = m.wr[c][:, k, h * P:(h + 1) * P]
                        nc.tensor.matmul(m.ps[n % 2][:, :], w, m.xt[:, k, 0:SEQ], start=(k == 0), stop=(k == KT - 1))
                        last = nc.tensor.matmul(m.ps[2 + n % 2][:, 0:NS], w, m.xt[:, k, SEQ:TOK],
                                                start=(k == 0), stop=(k == KT - 1))
                    last.then_inc(qk_mm, 1)
            pe.wait_ge(g_in, 48)
            pe.wait_ge(qk_ev, 2 * HA)
            for k in range(KT):
                nc.tensor.matmul(m.ps[0][0:16, :], wgd[:, k, :], m.xt[:, k, 0:SEQ], start=(k == 0), stop=(k == KT - 1))
                last = nc.tensor.matmul(m.ps[1][0:16, 0:NS], wgd[:, k, :], m.xt[:, k, SEQ:TOK],
                                        start=(k == 0), stop=(k == KT - 1))
            last.then_inc(gd_mm, 1)
            pe.wait_ge(gd_ev, 1)
            for h in range(HA):
                if h >= 1:
                    pe.wait_ge(z_ev, h)
                nc.tensor.matmul(m.ps[2][:, :], wgu[:, h * P:(h + 1) * P], gd[:, 0:SEQ], start=True, stop=True)
                nc.tensor.matmul(m.ps[3][:, 0:NS], wgu[:, h * P:(h + 1) * P], gd[:, SEQ:TOK],
                                 start=True, stop=True).then_inc(z_mm, 1)
            for c in range(4):
                pe.wait_ge(w_in[c % 2], 16 * (c // 2 + 2))
                for i, r in TILES:
                    n = c * NTT + i
                    if n >= 4:
                        pe.wait_ge(vr_ev, n - 3)
                    for k in range(KT):
                        last = nc.tensor.matmul(m.ps[4 + n % 4][0:r, :], m.xt[:, k, i * P:i * P + r],
                                                m.wr[c % 2][:, k, :], start=(k == 0), stop=(k == KT - 1))
                    last.then_inc(vr_mm, 1)

        @block.scalar
        def _(s):
            for n in range(2 * HA):
                s.wait_ge(qk_mm, n + 1)
                dst = (m.q, m.k)[n // HA]
                scale = DKA ** -0.5 if n < HA else 1.0
                nc.scalar.activation(dst[:, n % HA, 0:SEQ], m.ps[n % 2][:, :], ACT.Copy, scale=scale)
                nc.scalar.activation(dst[:, n % HA, SEQ:TOK], m.ps[2 + n % 2][:, 0:NS], ACT.Copy,
                                     scale=scale).then_inc(qk_ev, 1)
            s.wait_ge(z_ev, HA)
            nc.scalar.activation(t1, m.g, ACT.Abs).then_inc(ab, 1)
            s.wait_ge(ab, 1)
            nc.scalar.activation(t1, t1, ACT.Exp, scale=-1.0).then_inc(ex, 1)
            s.wait_ge(ex, 1)
            nc.scalar.activation(t1, t1, ACT.Ln, bias=1.0).then_inc(ln, 1)

        @block.vector
        def _(v):
            v.wait_ge(gd_mm, 1)
            nc.vector.tensor_copy(gd[:, 0:SEQ], m.ps[0][0:16, :])
            nc.vector.tensor_copy(gd[:, SEQ:TOK], m.ps[1][0:16, 0:NS]).then_inc(gd_ev, 1)
            for h in range(HA):
                v.wait_ge(z_mm, h + 1)
                nc.vector.tensor_scalar(m.g[:, h, 0:SEQ], m.ps[2][:, :], bg[:, h:h + 1], None, ALU.add)
                nc.vector.tensor_scalar(m.g[:, h, SEQ:TOK], m.ps[3][:, 0:NS], bg[:, h:h + 1], None, ALU.add).then_inc(z_ev, 1)
            for c in range(4):
                for i, r in TILES:
                    n = c * NTT + i
                    v.wait_ge(vr_mm, n + 1)
                    dst = (m.v, m.r)[c // 2]
                    nc.vector.tensor_copy(dst[0:r, i, (c % 2) * 512:(c % 2 + 1) * 512], m.ps[4 + n % 4][0:r, :]).then_inc(vr_ev, 1)
                if c == 1:
                    v.wait_ge(ln, 1)
                    nc.vector.tensor_scalar(m.g, m.g, 0.0, None, ALU.min)
                    v.drain()
                    nc.vector.tensor_tensor(m.g, m.g, t1, ALU.subtract)
                    v.drain()
                    nc.vector.tensor_scalar(m.g, m.g, 1.0 / TAU, None, ALU.mult)


def stage_gla_prompt(nc, ctx, m, a):
    sem = lambda n: ctx.enter_context(m_semaphore(nc, f"gla_{n}"))
    (start_ok, mask_ok, cum_ok, dif_ok, exp_ok, fac_ok, kl_tr, kl_ok, at_mm, at_ok, v_ok, ds_mm, s_ok, o_mm, o_ev, s_out) = (
        sem(n) for n in ("start_ok", "mask_ok", "cum_ok", "dif_ok", "exp_ok", "fac_ok", "kl_tr", "kl_ok", "at_mm",
                         "at_ok", "v_ok", "ds_mm", "s_ok", "o_mm", "o_ev", "s_out"))
    y_fill = sem("y_fill")
    NCH = P // CH
    off = [HA * TOK]

    def take(*shape):
        v = view(m.R, off[0], *shape)
        off[0] += int(np.prod(shape))
        return v
    cum = take(HA, P)
    mask = take(1, P)[:, 0, :]
    dmid, dlast = take(HA, P), take(HA, P)
    emid, ekey, ecum, elast = take(HA, P), take(HA, P), take(HA, P), take(HA, P)
    kls = take(HA, P)
    ats = take(HA, CH)
    tri = take(1, CH)[:, 0, :]
    S = [view(m.W, u * D, HA, DVA) for u in range(2)]
    vs = view(m.W, 2 * D, HA, DVA)
    eend = view(m.W, 3 * D, HA, NCH)
    qe, qm, km, kl = (view(m.W, 4 * D + j * 512, HA, P) for j in range(4))
    chunks = lambda t: t.rearrange("p h (c t) -> p h c t", t=CH)
    at_ps = m.ps[0][:, 0:P].rearrange("p (h t) -> p h t", t=CH)
    kl_ps = m.ps[1][:, :].rearrange("p (h k) -> p h k", k=P)
    with nc.Block() as block:
        @block.gpsimd
        def _(g):
            nc.gpsimd.memset(mask, 1.0).then_inc(start_ok, 1)
            nc.gpsimd.memset(tri, 1.0).then_inc(start_ok, 1)
            nc.gpsimd.memset(view(m.W, 0, 1, D), 0.0).then_inc(start_ok, 1)
            g.wait_ge(start_ok, 3)
            nc.gpsimd.memset(mask.rearrange("p (c t) -> p c t", t=CH)[:, :, 0:1], 0.0).then_inc(mask_ok, 1)
            for c in range(NCH):
                g.wait_ge(mask_ok, 1 + c)
                nc.gpsimd.affine_select(out=tri[c * CH:(c + 1) * CH, :], in_=tri[c * CH:(c + 1) * CH, :],
                                        compare_op=ALU.is_ge, fill=0.0, base=0, pattern=[[1, CH]],
                                        channel_multiplier=-1).then_inc(mask_ok, 1)

        @block.vector
        def _(v):
            v.wait_ge(mask_ok, 1 + NCH)

            def body(i, first):
                tok = bass.ds(i * P, P)
                if not first:
                    v.wait_ge(exp_ok, i)
                for h in range(HA):
                    last = nc.vector.tensor_tensor_scan(cum[:, h, :], mask, m.g[:, h, tok], 0.0, ALU.mult, ALU.add)
                v.drain()
                c4 = chunks(cum)
                mid = c4[:, :, :, CH // 2 - 1:CH // 2].to_broadcast([P, HA, NCH, CH])
                end = c4[:, :, :, CH - 1:CH].to_broadcast([P, HA, NCH, CH])
                nc.vector.tensor_tensor(chunks(dmid), c4, mid, ALU.subtract)
                nc.vector.tensor_tensor(chunks(dlast), end, c4, ALU.subtract).then_inc(dif_ok, 1)
                v.wait_ge(exp_ok, i + 1)
                if not first:
                    v.wait_ge(o_mm, NCH * i)
                nc.vector.tensor_tensor(kl, m.k[:, :, tok], elast, ALU.mult)
                nc.vector.tensor_tensor(qm, m.q[:, :, tok], emid, ALU.mult)
                nc.vector.tensor_tensor(km, m.k[:, :, tok], ekey, ALU.mult)
                nc.vector.tensor_tensor(qe, m.q[:, :, tok], ecum, ALU.mult).then_inc(fac_ok, 1)
                v.wait_ge(at_mm, i + 1)
                nc.vector.tensor_tensor(ats, at_ps, tri.unsqueeze(1).to_broadcast([P, HA, CH]), ALU.mult).then_inc(at_ok, 1)
                for c in range(NCH):
                    v.wait_ge(ds_mm, NCH * i + c + 1)
                    if c >= 1:
                        v.wait_ge(o_mm, NCH * i + c)
                    for h in range(HA):
                        nc.vector.scalar_tensor_tensor(out=S[(c + 1) % 2][:, h, :], in0=S[c % 2][:, h, :],
                                                       scalar=eend[:, h, c:c + 1],
                                                       in1=m.ps[4 + 2 * (c % 2) + h // 2][:, (h % 2) * DVA:(h % 2 + 1) * DVA],
                                                       op0=ALU.mult, op1=ALU.add).then_inc(s_ok, 1)
                    v.drain()
                v.wait_ge(o_mm, NCH * i + NCH)
                for n in range(2):
                    last = nc.vector.tensor_copy(m.v[:, bass.ds(i, 1), n * 512:(n + 1) * 512].rearrange("p a n -> p (a n)"),
                                                 m.ps[2 + n][:, :])
                last.then_inc(o_ev, 1)
            body(0, True)
            with v.Fori(1, SEQ // P) as i:
                body(i, False)

        @block.scalar
        def _(s):
            def body(i, first):
                if not first:
                    s.wait_ge(o_mm, NCH * i)
                nc.scalar.copy(vs.rearrange("p h n -> p (h n)"), m.v[:, bass.ds(i, 1), :].rearrange("p a n -> p (a n)")).then_inc(v_ok, 1)
                s.wait_ge(dif_ok, i + 1)
                if not first:
                    s.wait_ge(fac_ok, i)
                    s.wait_ge(s_ok, HA * NCH * i)
                nc.scalar.activation(elast, dlast, ACT.Exp)
                nc.scalar.activation(emid, dmid, ACT.Exp)
                nc.scalar.activation(ekey, dmid, ACT.Exp, scale=-1.0)
                nc.scalar.activation(ecum, cum, ACT.Exp)
                nc.scalar.activation(eend, chunks(cum)[:, :, :, CH - 1], ACT.Exp).then_inc(exp_ok, 1)
                s.wait_ge(kl_tr, i + 1)
                nc.scalar.copy(kls, kl_ps).then_inc(kl_ok, 1)
            body(0, True)
            with s.Fori(1, SEQ // P) as i:
                body(i, False)

        @block.tensor
        def _(pe):
            def state(i, c):
                r = slice(c * CH, (c + 1) * CH)
                for h in range(HA):
                    last = nc.tensor.matmul(m.ps[4 + 2 * (c % 2) + h // 2][:, (h % 2) * DVA:(h % 2 + 1) * DVA],
                                            kls[r, h, :], vs[r, h, :], start=True, stop=True, tile_position=(c * CH, 0))
                last.then_inc(ds_mm, 1)

            def body(i, first):
                pe.wait_ge(fac_ok, i + 1)
                for h in range(HA):
                    last = nc.tensor.transpose(kl_ps[:, h, :], kl[:, h, :], m.ident[:, :])
                last.then_inc(kl_tr, 1)
                for h in range(HA):
                    for c in range(NCH):
                        r = slice(c * CH, (c + 1) * CH)
                        last = nc.tensor.matmul(at_ps[r, h, :], km[:, h, r], qm[:, h, r], start=True, stop=True,
                                                tile_position=(0, c * CH))
                last.then_inc(at_mm, 1)
                pe.wait_ge(kl_ok, i + 1)
                pe.wait_ge(v_ok, i + 1)
                pe.wait_ge(at_ok, i + 1)
                if not first:
                    pe.wait_ge(o_ev, i)
                    pe.wait_ge(s_ok, HA * NCH * i)
                state(i, 0)
                for c in range(NCH):
                    r = slice(c * CH, (c + 1) * CH)
                    if c + 1 < NCH:
                        if c >= 1:
                            pe.wait_ge(s_ok, HA * (NCH * i + c))
                        state(i, c + 1)
                    for h in range(HA):
                        o = m.ps[2 + h // 2][r, (h % 2) * DVA:(h % 2 + 1) * DVA]
                        if c >= 1:
                            pe.wait_ge(s_ok, HA * (NCH * i + c - 1) + h + 1)
                        nc.tensor.matmul(o, qe[:, h, r], S[c % 2][:, h, :], start=True, stop=False, tile_position=(0, c * CH))
                        last = nc.tensor.matmul(o, ats[r, h, :], vs[r, h, :], start=False, stop=True,
                                                tile_position=(c * CH, c * CH))
                    last.then_inc(o_mm, 1)
            body(0, True)
            with pe.Fori(1, SEQ // P) as i:
                body(i, False)

        @block.sync
        def _(sp):
            most = 2 * MIN_PAIRS * P
            sp.dma_start(m.yD[most:SLOTS, :].rearrange("(t p) n -> p t n", p=P),
                         m.lnr[:, 0:1, :].to_broadcast([P, (SLOTS - most) // P, D])).then_inc(y_fill, 16)
            sp.wait_ge(y_fill, 16)
            sp.wait_ge(s_ok, HA * NCH * (SEQ // P))
            sp.dma_start(a["s_prompt"].rearrange("l b h k v -> k (l b h) v"), S[0]).then_inc(s_out, 16)
            sp.wait_ge(s_out, 16)


def stage_gla_sample(nc, ctx, m, a):
    sem = lambda n: ctx.enter_context(m_semaphore(nc, f"glas_{n}"))
    st_in, eg_ok, sel_ok, dg_ok, vb_mm, s_ok, o_mm, o_out, qs_ok = (sem(n) for n in
        ("st_in", "eg_ok", "sel_ok", "dg_ok", "vb_mm", "s_ok", "o_mm", "o_out", "qs_ok"))
    st = view(m.W, 0, NS * HA, DVA)
    off = HA * TOK
    eg = view(m.R, off, HA, NS)
    qsel = view(m.R, off + 32, HA, NS * NS)
    sel = m.R[0:NS, off + 32 + HA * NS * NS:off + 32 + HA * NS * NS + NS * P]
    src = a["state_gla"].rearrange("l b h k v -> k (l b h) v")
    dst = a["s_sample"].rearrange("l b h k v -> k (l b h) v")
    with nc.Block() as block:
        @block.sync
        def _(sp):
            sp.dma_start(st, src).then_inc(st_in, 16)
            for b in range(NS):
                sp.wait_ge(s_ok, b + 1)
                sp.dma_start(dst[:, b * HA:(b + 1) * HA, :], st[:, b * HA:(b + 1) * HA, :]).then_inc(o_out, 16)
            sp.wait_ge(o_out, 16 * NS)

        @block.gpsimd
        def _(g):
            nc.gpsimd.memset(sel, 0.0).then_inc(sel_ok, 1)
            g.wait_ge(sel_ok, 1)
            nc.gpsimd.affine_select(out=sel.rearrange("r (b n) -> r b n", n=P), in_=sel.rearrange("r (b n) -> r b n", n=P),
                                    compare_op=ALU.not_equal, fill=1.0, base=0, pattern=[[-1, NS], [0, P]],
                                    channel_multiplier=1).then_inc(dg_ok, 1)

        @block.scalar
        def _(s):
            nc.scalar.activation(eg, m.g[:, :, SEQ:TOK], ACT.Exp).then_inc(eg_ok, 1)

        @block.vector
        def _(v):
            nc.vector.memset(qsel, 0.0)
            v.drain()
            nc.vector.tensor_copy(qsel[:, :, 0:NS * NS:NS + 1], m.q[:, :, SEQ:TOK]).then_inc(qs_ok, 1)
            v.wait_ge(st_in, 16)
            v.wait_ge(eg_ok, 1)
            for b in range(NS):
                for h in range(HA):
                    nc.vector.tensor_scalar(st[:, b * HA + h, :], st[:, b * HA + h, :], eg[:, h, b:b + 1], None, ALU.mult)
                v.wait_ge(vb_mm, b + 1)
                v.drain()
                for h in range(HA):
                    last = nc.vector.scalar_tensor_tensor(
                        out=st[:, b * HA + h, :], in0=m.ps[2 * (b % 2) + h // 2][:, (h % 2) * DVA:(h % 2 + 1) * DVA],
                        scalar=m.k[:, h, SEQ + b:SEQ + b + 1], in1=st[:, b * HA + h, :], op0=ALU.mult, op1=ALU.add)
                last.then_inc(s_ok, 1)
            v.wait_ge(o_mm, 1)
            for h in range(HA):
                nc.vector.tensor_copy(m.v[0:NS, NTT - 1, h * DVA:(h + 1) * DVA], m.ps[4 + h][0:NS, 0:DVA])

        @block.tensor
        def _(pe):
            pe.wait_ge(dg_ok, 1)
            pe.wait_ge(qs_ok, 1)

            def spread(b):
                if b >= 2:
                    pe.wait_ge(s_ok, b - 1)
                for n in range(2):
                    last = nc.tensor.matmul(m.ps[2 * (b % 2) + n][:, :], sel[:, b * P:(b + 1) * P],
                                            m.v[0:NS, NTT - 1, n * 512:(n + 1) * 512], start=True, stop=True)
                last.then_inc(vb_mm, 1)
            spread(0)
            for b in range(NS):
                if b + 1 < NS:
                    spread(b + 1)
                pe.wait_ge(s_ok, b + 1)
                for h in range(HA):
                    last = nc.tensor.matmul(m.ps[4 + h][0:NS, 0:DVA], qsel[:, h, b * NS:(b + 1) * NS], st[:, b * HA + h, :],
                                            start=(b == 0), stop=(b == NS - 1))
            last.then_inc(o_mm, 1)


def stage_mix_output(nc, ctx, m, name, groups, gain, gate_r, factor, w_o):
    sem = lambda n: ctx.enter_context(m_semaphore(nc, f"{name}_{n}"))
    gn_in, w_in, sq_ok, sd_ok, er_ok, row_ok, tr, cp, mm, ev = (sem(n) for n in
        ("gn_in", "w_in", "sq_ok", "sd_ok", "er_ok", "row_ok", "tr", "cp", "mm", "ev"))
    width = D // groups
    gn = m.R[:, 0:width]
    sq = [m.R[:, (1 + u) * D:(2 + u) * D] for u in range(2)]
    er = [m.R[:, (3 + u) * D:(4 + u) * D] for u in range(2)]
    ss = m.R[:, 5 * D:5 * D + NTT * groups].rearrange("p (i g) -> p i g", g=groups)
    rstd = m.R[:, 5 * D + 64:5 * D + 64 + NTT * groups].rearrange("p (i g) -> p i g", g=groups)
    w = view(m.W, 0, KT, D)
    ln = LayerNorm(nc, ctx, m, name)
    with nc.Block() as block:
        @block.sync
        def _(sp):
            sp.dma_start(gn, gain.partition_broadcast(P)).then_inc(gn_in, 16)
            sp.dma_start(w, w_o.rearrange("(p k) n -> p k n", k=KT)).then_inc(w_in, 16)

        @block.scalar
        def _(s):
            for i, r in TILES:
                if gate_r:
                    if i >= 2:
                        s.wait_ge(row_ok, i - 1)
                    nc.scalar.activation(er[i % 2][0:r, :], m.r[0:r, i, :], ACT.Exp, scale=-1.0).then_inc(er_ok, 1)
            s.wait_ge(sq_ok, NTT)
            nc.scalar.activation(rstd, ss, ACT.Sqrt, scale=1.0 / width, bias=m.small[:, 500:501]).then_inc(sd_ok, 1)
            for i, r in TILES:
                s.wait_ge(tr, i + 1)
                for n in range(2):
                    last = nc.scalar.copy(m.xt[:, 4 * n:4 * n + 4, i * P:i * P + r],
                                          m.ps[2 * (i % 2) + n][:, :].rearrange("p (k t) -> p k t", t=P)[:, :, 0:r])
                last.then_inc(cp, 1)
            ln.scalar(s)

        @block.vector
        def _(v):
            nc.vector.memset(ss, 1.0)
            nc.vector.memset(m.small[:, 500:501], RMS_EPS)
            v.wait_ge(gn_in, 16)
            if factor != 1.0:
                nc.vector.tensor_scalar(gn, gn, factor, None, ALU.mult)
            v.drain()
            for i, r in TILES:
                nc.vector.tensor_tensor(sq[i % 2][0:r, :], m.v[0:r, i, :], m.v[0:r, i, :], ALU.mult)
                v.drain()
                nc.vector.tensor_reduce(out=ss[0:r, i, :], in_=sq[i % 2][0:r, :].rearrange("p (g w) -> p g w", g=groups),
                                        axis=AX.X, op=ALU.add).then_inc(sq_ok, 1)
                if gate_r:
                    v.wait_ge(er_ok, i + 1)
                    nc.vector.tensor_scalar(er[i % 2][0:r, :], er[i % 2][0:r, :], 1.0, None, ALU.add)
                    v.drain()
                    nc.vector.reciprocal(er[i % 2][0:r, :], er[i % 2][0:r, :])
                    v.drain()
                    nc.vector.tensor_tensor(m.r[0:r, i, :], m.r[0:r, i, :], er[i % 2][0:r, :], ALU.mult).then_inc(row_ok, 1)
            v.wait_ge(sd_ok, 1)
            nc.vector.reciprocal(rstd, rstd)
            v.drain()
            ready = NTT if gate_r else 0
            for i, r in TILES:
                row = m.v[0:r, i, :].rearrange("p (g w) -> p g w", g=groups)
                nc.vector.tensor_tensor(row, row, rstd[0:r, i, :].unsqueeze(2).to_broadcast([r, groups, width]), ALU.mult)
                v.drain()
                last = nc.vector.tensor_tensor(row, row, gn[0:r, :].unsqueeze(1).to_broadcast([r, groups, width]), ALU.mult)
                if gate_r:
                    v.drain()
                    last = nc.vector.tensor_tensor(m.v[0:r, i, :], m.v[0:r, i, :], m.r[0:r, i, :], ALU.mult)
                last.then_inc(row_ok, 1)
            for i, r in TILES:
                v.wait_ge(mm, i + 1)
                ln.mixed(v, i, r, [m.ps[4 + 2 * (i % 2) + n] for n in range(2)]).then_inc(ev, 1)
                ln.stats(v, i, r)
            ln.normalize(v)

        @block.tensor
        def _(pe):
            ready = NTT if gate_r else 0
            for i, r in TILES:
                pe.wait_ge(row_ok, ready + i + 1)
                if i >= 2:
                    pe.wait_ge(cp, i - 1)
                for k in range(KT):
                    last = nc.tensor.transpose(m.ps[2 * (i % 2) + k // 4][:, (k % 4) * P:(k % 4) * P + r],
                                               m.v[0:r, i, :].rearrange("t (p k) -> t k p", k=KT)[:, k, :],
                                               m.ident[0:r, 0:r])
                last.then_inc(tr, 1)
            pe.wait_ge(w_in, 16)
            for i, r in TILES:
                pe.wait_ge(cp, i + 1)
                if i >= 2:
                    pe.wait_ge(ev, i - 1)
                for n in range(2):
                    for k in range(KT):
                        last = nc.tensor.matmul(m.ps[4 + 2 * (i % 2) + n][0:r, :], m.xt[:, k, i * P:i * P + r],
                                                w[:, k, n * 512:(n + 1) * 512], start=(k == 0), stop=(k == KT - 1))
                last.then_inc(mm, 1)


class LayerNorm:

    def __init__(self, nc, ctx, m, name):
        sem = lambda n: ctx.enter_context(m_semaphore(nc, f"{name}_ln_{n}"))
        self.nc, self.m = nc, m
        self.var_ok, self.sd_ok, self.bias_ok, self.scaled = (sem(n) for n in ("var_ok", "sd_ok", "bias_ok", "scaled"))
        self.done = sem("done")

    def mixed(self, v, i, r, halves):
        nc, m = self.nc, self.m
        for n in range(2):
            c = slice(n * 512, (n + 1) * 512)
            last = nc.vector.tensor_tensor(m.R[0:r, 6 * D + n * 512:6 * D + (n + 1) * 512], halves[n][0:r, :],
                                           m.mod[0:r, i // (NTT - 1), 2, c], ALU.mult)
        return last

    def stats(self, v, i, r):
        nc, m = self.nc, self.m
        v.drain()
        nc.vector.scalar_tensor_tensor(out=m.x[0:r, i, :], in0=m.x[0:r, i, :], scalar=ALPHA,
                                       in1=m.R[0:r, 6 * D:7 * D], op0=ALU.mult, op1=ALU.add)
        v.drain()
        for n in range(2):
            nc.vector.bn_stats(m.st6[0:r, n, :], m.x[0:r, i, n * 512:(n + 1) * 512])
        v.drain()
        nc.vector.bn_aggr(m.mv[0:r, i, :], m.st6[0:r, :, :])

    def normalize(self, v):
        nc, m = self.nc, self.m
        v.drain()
        nc.vector.memset(m.small[:, 501:502], LN_EPS)
        v.drain()
        nc.vector.tensor_copy(m.rs[:, 0, :], m.mv[:, :, 1]).then_inc(self.var_ok, 1)
        v.wait_ge(self.sd_ok, 1)
        nc.vector.reciprocal(m.rs[:, 0, :], m.rs[:, 0, :])
        v.drain()
        nc.vector.scalar_tensor_tensor(out=m.rs[:, 1, :], in0=m.mv[:, :, 0], scalar=-1.0, in1=m.rs[:, 0, :],
                                       op0=ALU.mult, op1=ALU.mult).then_inc(self.bias_ok, 1)
        for i, r in TILES:
            v.wait_ge(self.scaled, i + 1)
            nc.vector.tensor_tensor(m.x[0:r, i, :], m.x[0:r, i, :], m.lnr[0:r, 0, :], ALU.mult)
            v.drain()
            nc.vector.tensor_tensor(m.x[0:r, i, :], m.x[0:r, i, :], m.lnr[0:r, 1, :], ALU.add).then_inc(self.done, 1)

    def scalar(self, s):
        nc, m = self.nc, self.m
        s.wait_ge(self.var_ok, 1)
        nc.scalar.activation(m.rs[:, 0, :], m.rs[:, 0, :], ACT.Sqrt, bias=m.small[:, 501:502]).then_inc(self.sd_ok, 1)
        s.wait_ge(self.bias_ok, 1)
        for i, r in TILES:
            nc.scalar.activation(m.x[0:r, i, :], m.x[0:r, i, :], ACT.Identity, scale=m.rs[0:r, 0, i:i + 1],
                                 bias=m.rs[0:r, 1, i:i + 1]).then_inc(self.scaled, 1)


def stage_route(nc, ctx, m, l, a):
    sem = lambda n: ctx.enter_context(m_semaphore(nc, f"route{l}_{n}"))
    w_in, ln_in, tab, mm, ev, sel_ok, rk_mm, rk2, z_in, z_out, dst_ok, sc_out, ix_in, tri_ok, te_ok = (sem(n) for n in
        ("w_in", "ln_in", "tab", "mm", "ev", "sel_ok", "rk_mm", "rk2", "z_in", "z_out", "dst_ok", "sc_out", "ix_in",
         "tri_ok", "te_ok"))
    ex_ok = sem("ex_ok")
    off = [2 * D]

    def take(*shape):
        v = view(m.R, off[0], *shape)
        off[0] += int(np.prod(shape))
        return v
    wr, br = take(KT, NE), take(1, NE)[:, 0, :]
    L, E, O1, O2, T, RK = (take(NTT, NE) for _ in range(6))
    GS, GM = take(NTT, NG), take(NTT, NG)
    A1, A2, A3 = (take(NTT, 1)[:, :, 0] for _ in range(3))
    G3 = take(NTT, NG)
    valid = take(NTT, 1)[:, :, 0]
    tri = take(1, P)[:, 0, :]
    w16, w4 = take(1, NE)[:, 0, :], take(1, NG)[:, 0, :]
    nt, start, end, zero16 = (take(1, NE)[:, 0, :] for _ in range(4))
    tmp16 = take(1, NE)[:, 0, :]
    cmp_ = take(SLOT_TILES, NE)
    tix, tef = take(1, SLOT_TILES)[:, 0, :], take(1, SLOT_TILES)[:, 0, :]
    toki = take(1, NTT)[:, 0, :].bitcast(I32)
    zi = take(1, SLOT_TILES)[:, 0, :].bitcast(I32)
    t_e = [P, NTT, NE]
    with nc.Block() as block:
        @block.sync
        def _(sp):
            sp.dma_start(wr, a["w_router"].rearrange("(p k) n -> p k n", k=KT)).then_inc(w_in, 16)
            sp.dma_start(br, a["b_router"].partition_broadcast(P)).then_inc(w_in, 16)
            sp.dma_start(m.lnr[:, 0, :], a["ln_ffn_g"][l].partition_broadcast(P)).then_inc(ln_in, 16)
            sp.dma_start(m.lnr[:, 1, :], a["ln_ffn_b"][l].partition_broadcast(P)).then_inc(ln_in, 16)
            sp.wait_ge(z_in, 1)
            sp.dma_start(m.idxD[l].rearrange("(p t) a -> p (t a)", p=P), zi).then_inc(z_out, 16)
            sp.wait_ge(sc_out, 16 * 2 * NTT)
            with nc.allow_non_contiguous_dma(reason="slot tokens, one per partition and tile"):
                sp.dma_start(m.idx[:, :], m.idxD[l].rearrange("(t p) a -> p (t a)", p=P)).then_inc(ix_in, 16)
            sp.wait_ge(ix_in, 16)
            sp.wait_ge(ln_in, 32)

        @block.gpsimd
        def _(g):
            nc.gpsimd.memset(tri, 1.0).then_inc(tri_ok, 1)
            nc.gpsimd.memset(valid, 0.0).then_inc(tri_ok, 1)
            g.wait_ge(tri_ok, 2)
            nc.gpsimd.affine_select(out=tri, in_=tri, compare_op=ALU.is_gt, fill=0.0, base=0, pattern=[[1, P]],
                                    channel_multiplier=-1).then_inc(tab, 1)
            nc.gpsimd.memset(valid[:, 0:NTT - 1], 1.0).then_inc(tab, 1)
            nc.gpsimd.memset(valid[0:NS, NTT - 1:NTT], 1.0).then_inc(tab, 1)
            nc.gpsimd.iota(w16, pattern=[[-1, NE]], base=NE, channel_multiplier=0, allow_small_or_imprecise_dtypes=True).then_inc(tab, 1)
            nc.gpsimd.iota(w4, pattern=[[-1, NG]], base=NG, channel_multiplier=0, allow_small_or_imprecise_dtypes=True).then_inc(tab, 1)
            nc.gpsimd.iota(tix, pattern=[[1, SLOT_TILES]], base=0, channel_multiplier=0,
                           allow_small_or_imprecise_dtypes=True).then_inc(tab, 1)
            nc.gpsimd.iota(toki, pattern=[[P, NTT]], base=0, channel_multiplier=1).then_inc(tab, 1)
            nc.gpsimd.memset(zi, 0).then_inc(z_in, 1)
            g.wait_ge(z_out, 16)
            g.wait_ge(dst_ok, 1)
            g.wait_ge(tab, 7)
            for c in range(2):
                for i, r in TILES:
                    g.indirect_dma_start(out=m.idxD[l], out_offset=bass.IndirectOffsetOnAxis(ap=m.dest[0:r, c, i:i + 1], axis=0),
                                         in_=toki[0:r, i:i + 1], in_offset=None).then_inc(sc_out, 16)

        @block.tensor
        def _(pe):
            pe.wait_ge(w_in, 32)
            for i, r in TILES:
                for k in range(KT):
                    last = nc.tensor.matmul(m.ps[i][0:r, 0:NE], m.xt[:, k, i * P:i * P + r], wr[:, k, :],
                                            start=(k == 0), stop=(k == KT - 1))
            last.then_inc(mm, 1)
            pe.wait_ge(sel_ok, 1)
            pe.wait_ge(tab, 7)
            for i, r in TILES:
                for j in range(i):
                    nc.tensor.matmul(m.ps[i][:, 0:NE], m.ones[:, :], T[:, j, :], start=(j == 0), stop=False)
                nc.tensor.matmul(m.ps[i][:, 0:NE], tri, T[:, i, :], start=(i == 0), stop=True)
            for j in range(NTT):
                last = nc.tensor.matmul(m.ps[5][:, 0:NE], m.ones[:, :], T[:, j, :], start=(j == 0), stop=(j == NTT - 1))
            last.then_inc(rk_mm, 1)

        @block.scalar
        def _(s):
            s.wait_ge(ev, 1)
            nc.scalar.activation(E, L, ACT.Exp).then_inc(ex_ok, 1)

        @block.vector
        def _(v):
            V = nc.vector

            def tt(out, x, y, op):
                last = V.tensor_tensor(out, x, y, op)
                v.drain()
                return last

            def bc(x):
                return x.unsqueeze(2).to_broadcast([P, NTT, x.shape[-1] if False else NE])
            V.memset(L, 0.0)
            v.wait_ge(mm, 1)
            v.wait_ge(w_in, 32)
            v.drain()
            for i, r in TILES:
                V.tensor_tensor(L[0:r, i, :], m.ps[i][0:r, 0:NE], br[0:r, :], ALU.add)
            v.drain()
            V.tensor_reduce(out=A1, in_=L, axis=AX.X, op=ALU.max)
            v.drain()
            V.tensor_tensor(L, L, bc(A1), ALU.subtract).then_inc(ev, 1)
            v.wait_ge(ex_ok, 1)
            V.tensor_reduce(out=A2, in_=E, axis=AX.X, op=ALU.add)
            v.drain()
            V.reciprocal(A2, A2)
            v.drain()
            tt(E, E, bc(A2), ALU.mult)
            e4 = E.rearrange("p i (g e) -> p i g e", e=EPG)
            pairs = [(x, y) for x in range(EPG) for y in range(x + 1, EPG)]
            for n, (x, y) in enumerate(pairs):
                tt(G3 if n else GS, e4[:, :, :, x], e4[:, :, :, y], ALU.add)
                if n:
                    tt(GS, GS, G3, ALU.max)
            v.wait_ge(tab, 7)

            def first_of(onehot, score, best, weights, n):
                V.tensor_reduce(out=best, in_=score, axis=AX.X, op=ALU.max)
                v.drain()
                tt(onehot, score, best.unsqueeze(2).to_broadcast([P, NTT, n]), ALU.is_equal)
                tt(onehot, onehot, weights.unsqueeze(1).to_broadcast([P, NTT, n]), ALU.mult)
                V.tensor_reduce(out=A3, in_=onehot, axis=AX.X, op=ALU.max)
                v.drain()
                tt(onehot, onehot, A3.unsqueeze(2).to_broadcast([P, NTT, n]), ALU.is_equal)
            first_of(GM, GS, A1, w4, NG)
            tt(E.rearrange("p i (g e) -> p i g e", e=EPG), e4, GM.unsqueeze(3).to_broadcast([P, NTT, NG, EPG]), ALU.mult)
            tt(E.rearrange("p i (g e) -> p i g e", e=EPG), e4, GM.unsqueeze(3).to_broadcast([P, NTT, NG, EPG]), ALU.add)
            V.tensor_scalar(E, E, -1.0, None, ALU.add)
            v.drain()
            first_of(O1, E, A1, w16, NE)
            V.scalar_tensor_tensor(out=E, in0=O1, scalar=-4.0, in1=E, op0=ALU.mult, op1=ALU.add)
            v.drain()
            first_of(O2, E, A2, w16, NE)
            tt(A3, A1, A2, ALU.add)
            V.reciprocal(A3, A3)
            v.drain()
            tt(m.wts[:, 0, :], A1, A3, ALU.mult)
            tt(m.wts[:, 1, :], A2, A3, ALU.mult)
            tt(O1, O1, bc(valid), ALU.mult)
            tt(O2, O2, bc(valid), ALU.mult)
            V.tensor_tensor(T, O1, O2, ALU.add).then_inc(sel_ok, 1)
            v.wait_ge(rk_mm, 1)
            V.tensor_scalar(nt, m.ps[5][:, 0:NE], 0.0, None, ALU.is_gt)
            v.drain()
            for c in range(1, NTT):
                V.tensor_scalar(tmp16, m.ps[5][:, 0:NE], float(c * P), None, ALU.is_gt)
                v.drain()
                tt(nt, nt, tmp16, ALU.add)
            V.memset(zero16, 1.0)
            v.drain()
            V.tensor_tensor_scan(end, zero16, nt, 0.0, ALU.mult, ALU.add)
            v.drain()
            tt(start, end, nt, ALU.subtract)
            V.tensor_scalar(start, start, float(P), None, ALU.mult)
            v.drain()
            for i in range(NTT):
                V.tensor_tensor(RK[:, i, :], m.ps[i][:, 0:NE], start, ALU.add)
            v.drain()
            for c, O in enumerate((O1, O2)):
                tt(O, O, RK, ALU.mult)
                V.tensor_reduce(out=A1, in_=O, axis=AX.X, op=ALU.add)
                v.drain()
                V.tensor_copy(m.dest[:, c, :], A1).then_inc(rk2, 1)
                v.drain()
            v.nop().then_inc(dst_ok, 1)
            tt(cmp_, end.unsqueeze(1).to_broadcast([P, SLOT_TILES, NE]), tix.unsqueeze(2).to_broadcast([P, SLOT_TILES, NE]), ALU.is_le)
            V.tensor_reduce(out=tef, in_=cmp_, axis=AX.X, op=ALU.add)
            v.drain()
            V.tensor_scalar(tef, tef, float(NE - 1), None, ALU.min)
            v.drain()
            V.tensor_copy(m.texp[0:1, 0:SLOT_TILES], tef[0:1, :])
            v.drain()
            half = SLOT_TILES // 2
            V.tensor_scalar(tef[0:1, 0:half], tix[0:1, 0:SLOT_TILES:2], end[0:1, NE - 1:NE], None, ALU.is_lt)
            v.drain()
            V.tensor_reduce(out=tmp16[0:1, 0:1], in_=tef[0:1, 0:half], axis=AX.X, op=ALU.add)
            v.drain()
            V.tensor_scalar(m.texp[0:1, SLOT_TILES:SLOT_TILES + 1], tmp16[0:1, 0:1], float(-MIN_PAIRS), None, ALU.add).then_inc(te_ok, 1)


def stage_experts(nc, ctx, m, l, a):
    sem = lambda n: ctx.enter_context(m_semaphore(nc, f"moe{l}_{n}"))
    x_in, wg_in, wu_in, wd_in, y_out = ([sem(f"{n}{u}") for u in range(2)] for n in ("x_in", "wg_in", "wu_in", "wd_in", "y_out"))
    x_tr, x_cp, g_mm, u_mm, e_ok, h_ok, h_tr, h_cp, d_mm, y_v, y_s = (sem(n) for n in
        ("x_tr", "x_cp", "g_mm", "u_mm", "e_ok", "h_ok", "h_tr", "h_cp", "d_mm", "y_v", "y_s"))
    NT = SLOT_TILES
    FT = FF // P
    wg = [view(m.W, u * 4096, KT, FF) for u in range(2)]
    wu = [view(m.W, 8192 + u * 4096, KT, FF) for u in range(2)]
    wd = [view(m.W, 16384 + u * 4096, FT, D) for u in range(2)]
    xg = [m.R[:, u * D:(u + 1) * D] for u in range(2)]
    xgt = [view(m.R, 2 * D + u * D, KT, P) for u in range(2)]
    ys = [m.R[:, (4 + u) * D:(5 + u) * D] for u in range(2)]
    es = [m.R[:, 6 * D + u * FF:6 * D + (u + 1) * FF] for u in range(2)]
    hs = [m.R[:, 7 * D + u * FF:7 * D + (u + 1) * FF] for u in range(2)]
    ht = [view(m.R, 8 * D + u * FF, FT, P) for u in range(2)]
    ixc = [m.small[:, 504 + u:505 + u].bitcast(I32) for u in range(2)]
    src = [a[n][l] for n in ("w_exp_gate", "w_exp_up", "w_exp_down")]
    pst = [m.ps[0], m.ps[1]]
    psg, psu, psh, psy = m.ps[2], m.ps[3], m.ps[4], [m.ps[5], m.ps[6]]

    def tiles(eng, step):
        pairs = eng.value_load(m.texp[0:1, NT:NT + 1], min_val=0, max_val=NT // 2 - MIN_PAIRS) + MIN_PAIRS
        for t in range(4):
            step(t // 2, t % 2, t)
        with eng.Fori(2, pairs - 1) as i:
            for u in range(2):
                step(i, u, None)
        step(pairs - 1, 0, None)
        step(pairs - 1, 1, LAST)
        return pairs

    with nc.Block() as block:
        @block.sync
        def _(sp):
            def step(i, u, t):
                e = sp.value_load(m.texp[0:1, bass.ds(2 * i + u, 1)], min_val=0, max_val=NE - 1)
                for w, s, done, free, k in ((wg, src[0], wg_in, g_mm, KT), (wu, src[1], wu_in, u_mm, KT), (wd, src[2], wd_in, d_mm, FT)):
                    if t is None or t >= 2:
                        sp.wait_ge(free, 2 * i + u - 1)
                    sp.dma_start(w[u].rearrange("p k n -> p (k n)"),
                                 s[bass.ds(e, 1)].rearrange("a (p k) n -> p (a k n)", k=k)).then_inc(done[u], 16)
            tiles(sp, step)

        @block.gpsimd
        def _(g):
            def step(i, u, t):
                if t is None or t >= 2:
                    g.wait_ge(x_tr, 2 * i + u - 1)
                nc.gpsimd.tensor_copy(ixc[u], m.idx[:, bass.ds(2 * i + u, 1)])
                g.drain()
                g.indirect_dma_start(out=xg[u], out_offset=None, in_=m.xmD,
                                     in_offset=bass.IndirectOffsetOnAxis(ap=ixc[u], axis=0)).then_inc(x_in[u], 16)
            pairs = tiles(g, step)
            for u in range(2):
                g.wait_ge(y_out[u], 16 * pairs)

        @block.tensor
        def _(pe):
            def x_transpose(i, u, first):
                pe.wait_ge(x_in[u], 16 * i + 16)
                if not first:
                    pe.wait_ge(x_cp, 2 * i + u)
                for k in range(KT):
                    last = nc.tensor.transpose(pst[k // 4][:, (k % 4) * P:(k % 4 + 1) * P],
                                               xg[u].rearrange("t (p k) -> t k p", k=KT)[:, k, :], m.ident[:, :])
                last.then_inc(x_tr, 1)

            def h_transpose(u, n):
                pe.wait_ge(h_ok, n + 1)
                wait(pe, h_cp, n)
                for k in range(FT):
                    last = nc.tensor.transpose(psh[:, k * P:(k + 1) * P],
                                               hs[u].rearrange("t (p k) -> t k p", k=FT)[:, k, :], m.ident[:, :])
                last.then_inc(h_tr, 1)

            def down(u, n, wd_value):
                pe.wait_ge(h_cp, n + 1)
                pe.wait_ge(wd_in[u], wd_value)
                wait(pe, y_v, n)
                wait(pe, y_s, n)
                for c in range(2):
                    for k in range(FT):
                        last = nc.tensor.matmul(psy[c][:, :], ht[u][:, k, :], wd[u][:, k, c * 512:(c + 1) * 512],
                                                start=(k == 0), stop=(k == FT - 1))
                last.then_inc(d_mm, 1)

            def step(i, u, t):
                n = 2 * i + u
                pe.wait_ge(x_cp, n + 1)
                pe.wait_ge(wg_in[u], 16 * i + 16)
                wait(pe, e_ok, n)
                for k in range(KT):
                    last = nc.tensor.matmul(psg[:, :], xgt[u][:, k, :], wg[u][:, k, :], start=(k == 0), stop=(k == KT - 1))
                last.then_inc(g_mm, 1)
                if t != 0:
                    h_transpose(1 - u, n - 1)
                if t != LAST:
                    x_transpose(i + u, 1 - u, False)
                pe.wait_ge(wu_in[u], 16 * i + 16)
                wait(pe, h_ok, n)
                for k in range(KT):
                    last = nc.tensor.matmul(psu[:, :], xgt[u][:, k, :], wu[u][:, k, :], start=(k == 0), stop=(k == KT - 1))
                last.then_inc(u_mm, 1)
                if t != 0:
                    down(1 - u, n - 1, 16 * i + 16 * u)
            x_transpose(0, 0, True)
            pairs = tiles(pe, step)
            h_transpose(1, 2 * pairs - 1)
            down(1, 2 * pairs - 1, 16 * pairs)

        @block.scalar
        def _(s):
            def x_copy(u, n):
                s.wait_ge(x_tr, n + 1)
                wait(s, u_mm, n - 1)
                for c in range(2):
                    last = nc.scalar.copy(xgt[u][:, 4 * c:4 * c + 4, :], pst[c][:, :].rearrange("p (k t) -> p k t", t=P))
                last.then_inc(x_cp, 1)

            def h_copy(u, n):
                s.wait_ge(h_tr, n + 1)
                wait(s, d_mm, n - 1)
                nc.scalar.copy(ht[u], psh[:, :].rearrange("p (k t) -> p k t", t=P)).then_inc(h_cp, 1)

            def y_store(u, n, done):
                s.wait_ge(d_mm, n + 1)
                wait(s, y_out[u], done)
                nc.scalar.copy(ys[u][:, 512:1024], psy[1][:, :]).then_inc(y_s, 1)
                s.wait_ge(y_s, n + 1)
                s.wait_ge(y_v, n + 1)
                s.dma_start(m.yD[bass.ds(n * P, P), :], ys[u]).then_inc(y_out[u], 16)

            def step(i, u, t):
                n = 2 * i + u
                s.wait_ge(g_mm, n + 1)
                if t is None or t >= 2:
                    s.wait_ge(h_ok, n - 1)
                nc.scalar.activation(es[u], psg[:, :], ACT.Silu).then_inc(e_ok, 1)
                if t != 0:
                    h_copy(1 - u, n - 1)
                if t != LAST:
                    x_copy(1 - u, n + 1)
                if t != 0:
                    y_store(1 - u, n - 1, 16 * (i + u - 1))
            x_copy(0, 0)
            pairs = tiles(s, step)
            h_copy(1, 2 * pairs - 1)
            y_store(1, 2 * pairs - 1, 16 * (pairs - 1))

        @block.vector
        def _(v):
            V = nc.vector

            def y_copy(u, n, done):
                v.wait_ge(d_mm, n + 1)
                wait(v, y_out[u], done)
                V.tensor_copy(ys[u][:, 0:512], psy[0][:, :]).then_inc(y_v, 1)

            def step(i, u, t):
                n = 2 * i + u
                v.wait_ge(e_ok, n + 1)
                v.wait_ge(u_mm, n + 1)
                if t is None or t >= 2:
                    v.wait_ge(h_tr, n - 1)
                V.tensor_tensor(hs[u], es[u], psu[:, :], ALU.mult).then_inc(h_ok, 1)
                if t != 0:
                    y_copy(1 - u, n - 1, 16 * (i + u - 1))
            pairs = tiles(v, step)
            y_copy(1, 2 * pairs - 1, 16 * (pairs - 1))


def stage_combine(nc, ctx, m, l, stores=None):
    sem = lambda n: ctx.enter_context(m_semaphore(nc, f"comb{l}_{n}"))
    y_in = [sem(f"y_in{u}") for u in range(2)]
    w_ok, f_ok, out = sem("w_ok"), sem("f_ok"), sem("stored")
    y = [[m.R[:, (2 * u + c) * D:(2 * u + c + 1) * D] for c in range(2)] for u in range(2)]
    ln = LayerNorm(nc, ctx, m, f"comb{l}")
    with nc.Block() as block:
        @block.gpsimd
        def _(g):
            for i, r in TILES:
                if i >= 2:
                    g.wait_ge(f_ok, i - 1)
                for c in range(2):
                    g.indirect_dma_start(out=y[i % 2][c][0:r, :], out_offset=None, in_=m.yD,
                                         in_offset=bass.IndirectOffsetOnAxis(ap=m.dest[0:r, c, i:i + 1], axis=0)
                                         ).then_inc(y_in[i % 2], 16)

        @block.vector
        def _(v):
            for i, r in TILES:
                v.wait_ge(y_in[i % 2], 32 * (i // 2 + 1))
                y1, y2 = y[i % 2]
                nc.vector.tensor_scalar(y1[0:r, :], y1[0:r, :], m.wts[0:r, 0, i:i + 1], None, ALU.mult)
                v.drain()
                nc.vector.scalar_tensor_tensor(out=y1[0:r, :], in0=y2[0:r, :], scalar=m.wts[0:r, 1, i:i + 1],
                                               in1=y1[0:r, :], op0=ALU.mult, op1=ALU.add)
                v.drain()
                ln.mixed(v, i, r, [y1[:, 0:512], y1[:, 512:1024]]).then_inc(f_ok, 1)
                ln.stats(v, i, r)
            ln.normalize(v)

        @block.scalar
        def _(s):
            ln.scalar(s)

        @block.sync
        def _(sp):
            if stores is not None:
                for i, r in TILES:
                    sp.wait_ge(ln.done, i + 1)
                    dst = (stores[0].rearrange("b t n -> (b t) n")[i * P:(i + 1) * P, :] if i < NTT - 1
                           else stores[1].rearrange("b s n -> (b s) n"))
                    sp.dma_start(dst, m.x[0:r, i, :]).then_inc(out, 16)
                sp.wait_ge(out, 16 * NTT)


def stage_ln_rows(nc, ctx, m, name, g, b):
    s_in = ctx.enter_context(m_semaphore(nc, f"{name}_in"))
    with nc.Block() as block:
        @block.sync
        def _(sp):
            sp.dma_start(m.lnr[:, 0, :], g.partition_broadcast(P)).then_inc(s_in, 16)
            sp.dma_start(m.lnr[:, 1, :], b.partition_broadcast(P)).then_inc(s_in, 16)
            sp.wait_ge(s_in, 32)


def stage_shared_kv(nc, ctx, m, a):
    sem = lambda n: ctx.enter_context(m_semaphore(nc, f"kv_{n}"))
    w_in = [sem(f"w_in{u}") for u in range(2)]
    mm, ev, out = sem("mm"), sem("ev"), sem("stored")
    m.kk = view(m.W, 13312, NTT, D)
    m.vv = view(m.W, 18432, NTT, D)
    w_src = a["w_kv"].rearrange("(p k) n -> p k n", k=KT)
    with nc.Block() as block:
        @block.sync
        def _(sp):
            for c in range(4):
                if c >= 2:
                    sp.wait_ge(mm, NTT * (c - 1))
                sp.dma_start(m.wr[c % 2], w_src[:, :, c * 512:(c + 1) * 512]).then_inc(w_in[c % 2], 16)
            for j, (t, name) in enumerate(((m.kk, "k"), (m.vv, "v"))):
                sp.wait_ge(ev, 2 * NTT * (j + 1))
                sp.dma_start(a[f"{name}_prompt"].rearrange("b g p h d -> p (b g) (h d)"), t[:, 0:NTT - 1, :]).then_inc(out, 16)
                sp.dma_start(a[f"{name}_sample"].rearrange("b s h d -> (b s) (h d)"), t[0:NS, NTT - 1, :]).then_inc(out, 16)
                sp.dma_start(m.newD[j], t[0:NS, NTT - 1, :]).then_inc(out, 16)
            sp.wait_ge(out, 96)

        @block.tensor
        def _(pe):
            for c in range(4):
                pe.wait_ge(w_in[c % 2], 16 * (c // 2 + 1))
                for i, r in TILES:
                    n = c * NTT + i
                    wait(pe, ev, n - 3)
                    for k in range(KT):
                        last = nc.tensor.matmul(m.ps[4 + n % 4][0:r, :], m.xt[:, k, i * P:i * P + r],
                                                m.wr[c % 2][:, k, :], start=(k == 0), stop=(k == KT - 1))
                    last.then_inc(mm, 1)

        @block.vector
        def _(v):
            for c in range(4):
                for i, r in TILES:
                    n = c * NTT + i
                    v.wait_ge(mm, n + 1)
                    nc.vector.tensor_copy((m.kk, m.vv)[c // 2][0:r, i, (c % 2) * 512:(c % 2 + 1) * 512],
                                          m.ps[4 + n % 4][0:r, :]).then_inc(ev, 1)


def stage_queries(nc, ctx, m, a):
    sem = lambda n: ctx.enter_context(m_semaphore(nc, f"q_{n}"))
    w_in = [sem(f"w_in{u}") for u in range(2)]
    mm, ev, smm, sev, qs_out, l_in, l_sum, l_exp, l_row, l_mm, tab0, tab1, tab2, tab3 = (sem(n) for n in
        ("mm", "ev", "smm", "sev", "qs_out", "l_in", "l_sum", "l_exp", "l_row", "l_mm", "tab0", "tab1", "tab2", "tab3"))
    m.qt = view(m.R, 0, HB, SEQ)
    m.dist = m.R[:, 4096:4608]
    m.slope = m.small[:, 16:16 + HB]
    m.lam = m.small[:, 32:33]
    m.coef = m.small[:, 33:34]
    qs = m.R[0:NS, 5120:6144]
    lrow = m.R[0:1, 6144:6400]
    lprod = m.R[0:1, 6400:6528]
    lsum = m.R[0:1, 6528:6530]
    lam1 = m.R[0:1, 6530:6531]
    odd8 = m.R[:, 6600:6664]
    odd1 = m.R[:, 6664:6665]
    w_src = a["w_q_b"][0].rearrange("(p k) n -> p k n", k=KT)
    with nc.Block() as block:
        @block.sync
        def _(sp):
            for n, name in enumerate(("lam_q1", "lam_q2", "lam_k1", "lam_k2")):
                sp.dma_start(lrow[:, n * DHB:(n + 1) * DHB], a[name]).then_inc(l_in, 16)
            for c in range(2):
                sp.dma_start(m.wr[c], w_src[:, :, c * 512:(c + 1) * 512]).then_inc(w_in[c], 16)
            sp.wait_ge(sev, 2)
            sp.dma_start(m.qsD, qs).then_inc(qs_out, 16)
            sp.wait_ge(qs_out, 16)

        @block.gpsimd
        def _(g):
            nc.gpsimd.iota(m.dist, pattern=[[1, SEQ]], base=P - SEQ, channel_multiplier=-1,
                           allow_small_or_imprecise_dtypes=True).then_inc(tab0, 1)
            g.wait_ge(tab0, 1)
            nc.gpsimd.affine_select(out=m.dist, in_=m.dist, compare_op=ALU.is_ge, fill=NEG, base=SEQ - P,
                                    pattern=[[-1, SEQ]], channel_multiplier=1).then_inc(tab1, 1)
            for h in range(HB):
                nc.gpsimd.memset(m.slope[:, h:h + 1], 2.0 ** (-8.0 * (h + 1) / HB)).then_inc(tab1, 1)
            nc.gpsimd.memset(odd8, 0.0).then_inc(tab2, 1)
            g.wait_ge(tab2, 1)
            nc.gpsimd.affine_select(out=odd8, in_=odd8, compare_op=ALU.not_equal, fill=1.0, base=-1,
                                    pattern=[[-2, P // 2]], channel_multiplier=1).then_inc(tab3, 1)

        @block.tensor
        def _(pe):
            for c in range(2):
                pe.wait_ge(w_in[c], 16)
                for j in range(4):
                    n = 4 * c + j
                    wait(pe, ev, n - 1)
                    for k in range(KT):
                        last = nc.tensor.matmul(m.ps[n % 2][:, :], m.wr[c][:, k, j * P:(j + 1) * P], m.xt[:, k, 0:SEQ],
                                                start=(k == 0), stop=(k == KT - 1))
                    last.then_inc(mm, 1)
                for k in range(KT):
                    last = nc.tensor.matmul(m.ps[2 + c][0:NS, :], m.xt[:, k, SEQ:TOK], m.wr[c][:, k, :],
                                            start=(k == 0), stop=(k == KT - 1))
                last.then_inc(smm, 1)
            pe.wait_ge(l_row, 1)
            nc.tensor.matmul(m.ps[4][:, 0:1], m.ones[0:1, :], lam1, start=True, stop=True).then_inc(l_mm, 1)

        @block.scalar
        def _(s):
            for n in range(HB):
                s.wait_ge(mm, n + 1)
                nc.scalar.activation(m.qt[:, n, :], m.ps[n % 2][:, :], ACT.Copy, scale=DHB ** -0.5).then_inc(ev, 1)
            for c in range(2):
                s.wait_ge(smm, c + 1)
                nc.scalar.activation(qs[:, c * 512:(c + 1) * 512], m.ps[2 + c][0:NS, :], ACT.Copy,
                                     scale=DHB ** -0.5).then_inc(sev, 1)
            s.wait_ge(l_sum, 1)
            nc.scalar.activation(lsum, lsum, ACT.Exp).then_inc(l_exp, 1)

        @block.vector
        def _(v):
            v.wait_ge(l_in, 64)
            nc.vector.tensor_tensor(lprod, lrow[:, 0:2 * DHB], lrow[:, 2 * DHB:4 * DHB], ALU.mult)
            v.drain()
            nc.vector.tensor_reduce(out=lsum, in_=lprod.rearrange("p (a b) -> p a b", b=DHB), axis=AX.X, op=ALU.add).then_inc(l_sum, 1)
            v.wait_ge(l_exp, 1)
            nc.vector.tensor_tensor(lam1, lsum[:, 0:1], lsum[:, 1:2], ALU.subtract)
            v.drain()
            nc.vector.tensor_scalar(lam1, lam1, LAM_INIT, None, ALU.add).then_inc(l_row, 1)
            v.wait_ge(l_mm, 1)
            nc.vector.tensor_copy(m.lam, m.ps[4][:, 0:1])
            v.wait_ge(tab3, 1)
            nc.vector.tensor_reduce(out=odd1, in_=odd8, axis=AX.X, op=ALU.add)
            v.drain()
            nc.vector.tensor_tensor(m.coef, odd1, m.lam, ALU.mult)
            v.drain()
            nc.vector.tensor_tensor(m.coef, m.coef, odd1, ALU.add)
            v.drain()
            nc.vector.tensor_scalar(m.coef, m.coef, -1.0, 1.0, ALU.mult, ALU.add)


def stage_attention(nc, ctx, m, a):
    sem = lambda n: ctx.enter_context(m_semaphore(nc, f"at_{n}"))
    kr_ok, k_tr, kt_ok, sc_mm, sb_ok, nb_ok, p_ok, c_ok, c_tr, c_cp, o_mm, o_ev = (sem(n) for n in
        ("kr_ok", "k_tr", "kt_ok", "sc_mm", "sb_ok", "nb_ok", "p_ok", "c_ok", "c_tr", "c_cp", "o_mm", "o_ev"))
    RING, GRP = 8, 4
    VG = PAGES // 2
    k_in = [sem(f"k_in{u}") for u in range(RING)]
    v_in = [sem(f"v_in{u}") for u in range(2)]
    q_in, kn_in, vn_in, pt_in, o_out, os_in, z_ok, t0, t1, t2 = (sem(n) for n in
        ("q_in", "kn_in", "vn_in", "pt_in", "o_out", "os_in", "z_ok", "t0", "t1", "t2"))
    dp_ok, pp_ok = sem("dp_ok"), sem("pp_ok")
    ks_ok, mx_ok, mx_tr, mr_ok, mb_mm, sh_ok, e_ok, l_ok, l_mm, l_ev, pv_mm, om_ok, or_mm, or_ev = (sem(n) for n in
        ("ks_ok", "mx_ok", "mx_tr", "mr_ok", "mb_mm", "sh_ok", "e_ok", "l_ok", "l_mm", "l_ev", "pv_mm", "om_ok",
         "or_mm", "or_ev"))
    NQ = SEQ // P
    C, CP = 2 * HB, 32
    NP = PAGES + 1
    base = 4608
    khr = view(m.R, base, NQ, P)
    qh = m.R[:, base + 512:base + 1024]
    kth = m.R[:, base + 1024:base + 1536]
    SP = [[m.R[:, base + 512 * (5 + 2 * u + j):base + 512 * (6 + 2 * u + j)] for j in range(2)] for u in range(2)]
    ct = [m.R[:, base + 512 * (9 + u):base + 512 * (10 + u)] for u in range(2)]
    mx = [m.small[:, 40 + 2 * u:42 + 2 * u] for u in range(2)]
    ls = [m.small[:, 44 + 2 * u:46 + 2 * u] for u in range(2)]
    r1 = [m.small[:, 48 + i:49 + i] for i in range(NQ)]
    lm = m.small[:, 52:53]
    kp = [m.W[:, u * D:(u + 1) * D] for u in range(4)] + [m.lnr[:, 0, :], m.lnr[:, 1, :],
                                                        m.kk[:, NTT - 1, :], m.vv[:, NTT - 1, :]]
    vp = [m.W[:, (4 + u) * D:(5 + u) * D] for u in range(4)]
    xtf = m.xt[:, :, :].rearrange("p k t -> p (k t)")
    qb, kn = xtf[:, 0:D], xtf[:, D:2 * D]
    prod = [xtf[:, 2 * D:3 * D], xtf[:, 3 * D:4 * D], m.v[:, NTT - 1, :]]
    vn, bmask, om = m.mod[:, 0, 0, :], m.mod[:, 0, 1, :], m.mod[:, 1, 0, :]
    orow = m.mod[0:1, 1, 1, :]
    o1 = 23552
    S, BT = (view(m.W, o1 + j * NP * C, NP, C) for j in range(2))
    m1 = m.W[:, o1 + 2 * NP * C:o1 + 2 * NP * C + C]
    mr = m.W[0:C, o1 + 560:o1 + 561]
    cf = m.W[:, o1 + 561:o1 + 562]
    dg = m.W[0:C, o1 + 562:o1 + 562 + C]
    nd = m.W[:, o1 + 580:o1 + 580 + PAGES]
    lw = m.W[:, o1 + 600:o1 + 600 + GRP * CP].rearrange("p (g c) -> p g c", c=CP)
    lsum = m.W[:, o1 + 730:o1 + 730 + C]
    PR = view(m.R, base + 1536, NP, CP)
    pt = m.small[0:1, 128:128 + NS * PAGES].bitcast(I32)
    ks = a["cache_k"].rearrange("g p h d -> g p (h d)")
    vs = a["cache_v"].rearrange("g p h d -> g p (h d)")
    KT_B, SC_B, CT_B, O_B, PSO, MISC = m.ps[0], [m.ps[1], m.ps[2]], m.ps[3], m.ps[4], [m.ps[5], m.ps[6]], m.ps[7]

    def seqs(eng, body):
        body(0)
        body(1)
        with eng.Fori(2, NS - 1) as b:
            body(b)
        body(NS - 1)

    with nc.Block() as block:
        @block.sync
        def _(sp):
            sp.dma_start(pt, a["page_table"].rearrange("b j -> (b j)").unsqueeze(0)).then_inc(pt_in, 16)
            sp.wait_ge(pt_in, 16)

            def body(b):
                wait(sp, ks_ok, NP * b)
                sp.dma_start(qb, m.qsD[bass.ds(b, 1), :].to_broadcast([P, D])).then_inc(q_in, 16)
                if isinstance(b, int) and b == 0:
                    sp.wait_ge(z_ok, 4)
                sp.dma_start(kn[0:1, :], m.newD[0][bass.ds(b, 1), :]).then_inc(kn_in, 16)
                for j in range(PAGES):
                    if j >= RING:
                        wait(sp, ks_ok, NP * b + j - RING + 1)
                    page = sp.value_load(pt[0:1, bass.ds(b * PAGES + j, 1)], min_val=0, max_val=ks.shape[0] - 1)
                    sp.dma_start(kp[j % RING], ks[bass.ds(page, 1)].rearrange("g p n -> p (g n)")).then_inc(k_in[j % RING], 16)
            seqs(sp, body)
            sp.wait_ge(o_out, 16 * NS)
            sp.dma_start(m.v[0:NS, NTT - 1, :], m.osD).then_inc(os_in, 16)
            sp.wait_ge(os_in, 16)

        @block.gpsimd
        def _(g):
            G = nc.gpsimd
            G.memset(kn, 0.0).then_inc(z_ok, 1)
            G.memset(vn, 0.0).then_inc(z_ok, 1)
            G.memset(PR, 0.0).then_inc(z_ok, 1)
            G.memset(lw, 1.0).then_inc(z_ok, 1)
            G.memset(bmask, 1.0).then_inc(t0, 1)
            G.iota(nd, pattern=[[P, PAGES]], base=-PAST, channel_multiplier=1, allow_small_or_imprecise_dtypes=True).then_inc(t0, 1)
            G.memset(BT[:, PAGES:NP, :], 0.0).then_inc(t0, 1)
            g.wait_ge(t0, 3)
            G.affine_select(out=BT[:, PAGES:NP, :], in_=BT[:, PAGES:NP, :], compare_op=ALU.is_ge, fill=NEG, base=0,
                            pattern=[[0, 1], [0, C]], channel_multiplier=-1).then_inc(t1, 1)
            for n in range(GRP):
                b3 = bmask[n * CP:(n + 1) * CP, :].rearrange("r (h d) -> r h d", d=DVB)
                G.affine_select(out=b3, in_=b3, compare_op=ALU.is_ge, fill=0.0, base=0, pattern=[[-2, HB], [0, DVB]],
                                channel_multiplier=1).then_inc(t1, 1)
                g.wait_ge(t1, 2 * n + 2)
                G.affine_select(out=b3, in_=b3, compare_op=ALU.is_ge, fill=0.0, base=1, pattern=[[2, HB], [0, DVB]],
                                channel_multiplier=-1).then_inc(t1, 1)
                g.wait_ge(t1, 2 * n + 3)

            def body(b):
                g.wait_ge(q_in, 16 * b + 16)
                for j in range(1, PAGES, 2):
                    g.wait_ge(k_in[j % RING], 16 * (PAGES // RING) * b + 16 * (j // RING + 1))
                    wait(g, ks_ok, NP * b + j - 1)
                    G.tensor_tensor(prod[2], kp[j % RING], qb, ALU.mult).then_inc(pp_ok, 1)
            seqs(g, body)

        @block.tensor
        def _(pe):
            def k_transpose(h):
                pe.wait_ge(kr_ok, h + 1)
                wait(pe, kt_ok, h)
                for j in range(NQ):
                    last = nc.tensor.transpose(KT_B[:, j * P:(j + 1) * P], khr[:, j, :], m.ident[:, :])
                last.then_inc(k_tr, 1)

            def finish(u, i, h):
                pe.wait_ge(c_ok, u + 1)
                wait(pe, c_cp, u)
                for j in range(i + 1):
                    last = nc.tensor.transpose(CT_B[:, j * P:(j + 1) * P], SP[i % 2][0][:, j * P:(j + 1) * P], m.ident[:, :])
                last.then_inc(c_tr, 1)
                pe.wait_ge(c_cp, u + 1)
                wait(pe, o_ev, u)
                for j in range(i + 1):
                    last = nc.tensor.matmul(O_B[:, (i % 2) * DVB:(i % 2 + 1) * DVB], ct[i % 2][:, j * P:(j + 1) * P],
                                            m.vv[:, j, bass.ds(h * DVB, DVB)], start=(j == 0), stop=(j == i))
                last.then_inc(o_mm, 1)

            def values(b, p):
                half = p % 2
                if p == 0:
                    pe.wait_ge(e_ok, b + 1)
                    wait(pe, om_ok, b)
                pe.wait_ge(v_in[half], 32 * (VG // 2 * b + p // 2 + 1))
                for n in range(2):
                    c = slice(n * 512, (n + 1) * 512)
                    for j in (2 * p, 2 * p + 1):
                        g = j % GRP
                        last = nc.tensor.matmul(PSO[n][g * CP:(g + 1) * CP, :], PR[:, j, :], vp[j % 4][:, c],
                                                start=(j < GRP), stop=(j >= PAGES - GRP and g > 0), tile_position=(0, g * CP))
                if p == VG - 1:
                    pe.wait_ge(vn_in, 16 * b + 16)
                    for n in range(2):
                        last = nc.tensor.matmul(PSO[n][0:CP, :], PR[:, PAGES, :], vn[:, n * 512:(n + 1) * 512],
                                                start=False, stop=True, tile_position=(0, 0))
                last.then_inc(pv_mm, 1)

            def row(b, u):
                pe.wait_ge(om_ok, b + 1)
                pe.wait_ge(sb_ok, 2 * u)
                for n in range(2):
                    last = nc.tensor.matmul(SC_B[n][:, :], m.ones[:, :], om[:, n * 512:(n + 1) * 512], start=True, stop=True)
                last.then_inc(or_mm, 1)

            def softmax(b):
                pe.wait_ge(mx_ok, b + 1)
                nc.tensor.transpose(MISC[0:C, 0:P], m1, m.ident[:, :]).then_inc(mx_tr, 1)
                pe.wait_ge(mr_ok, b + 1)
                nc.tensor.matmul(MISC[:, P:P + C], m.ones[0:C, :], dg, start=True, stop=True).then_inc(mb_mm, 1)
                pe.wait_ge(l_ok, b + 1)
                nc.tensor.matmul(MISC[:, 160:161], lw.rearrange("p g c -> p (g c)"), m.ones[:, 0:1], start=True, stop=True).then_inc(l_mm, 1)

            def body(b):
                st = isinstance(b, int)
                for i in range(NQ):
                    u = NQ * b + i
                    if i == 0:
                        pe.wait_ge(kt_ok, b + 1)
                    wait(pe, sb_ok, 2 * u)
                    if i == 2 and not (st and b < 2):
                        pe.wait_ge(or_ev, b - 1)
                    for j in range(2):
                        r = slice(j * DHB, (j + 1) * DHB)
                        last = nc.tensor.matmul(SC_B[j][:, 0:(i + 1) * P], qh[r, i * P:(i + 1) * P],
                                                kth[r, 0:(i + 1) * P], start=True, stop=True)
                    last.then_inc(sc_mm, 1)
                    if i == 2 and not (st and b == HB - 1):
                        k_transpose(b + 1)
                    if not (st and b == 0):
                        values(b - 1, 2 * i)
                    if i:
                        finish(u - 1, i - 1, b)
                    if not (st and b == 0):
                        values(b - 1, 2 * i + 1)
                    if i == 1 and not (st and b < 2):
                        row(b - 2, u + 1)
                softmax(b)
                finish(NQ * b + NQ - 1, NQ - 1, b)
            k_transpose(0)
            seqs(pe, body)
            row(NS - 2, HB * NQ)
            for p in range(VG):
                values(NS - 1, p)
            pe.wait_ge(or_ev, NS - 1)
            row(NS - 1, HB * NQ)

        @block.scalar
        def _(s):
            def stage(h):
                wait(s, k_tr, h)
                nc.scalar.copy(khr, m.kk[:, 0:NQ, bass.ds(h * P, P)]).then_inc(kr_ok, 1)

            def q_copy(h):
                wait(s, sc_mm, NQ * h)
                nc.scalar.copy(qh, m.qt[:, bass.ds(h, 1), :].rearrange("p a t -> p (a t)"))

            def k_copy(h):
                s.wait_ge(k_tr, h + 1)
                nc.scalar.copy(kth, KT_B[:, :]).then_inc(kt_ok, 1)

            def c_copy(u, i):
                s.wait_ge(c_tr, u + 1)
                wait(s, o_mm, u - 1)
                nc.scalar.copy(ct[i % 2][:, 0:(i + 1) * P], CT_B[:, 0:(i + 1) * P]).then_inc(c_cp, 1)

            def load_values(b, p):
                if not (isinstance(b, int) and VG * b + p < 2):
                    s.wait_ge(pv_mm, VG * b + p - 1)
                for g in range(2):
                    page = s.value_load(pt[0:1, bass.ds(b * PAGES + 2 * p + g, 1)], min_val=0, max_val=ks.shape[0] - 1)
                    s.dma_start(vp[2 * (p % 2) + g], vs[bass.ds(page, 1)].rearrange("g p n -> p (g n)")).then_inc(v_in[p % 2], 16)

            def load_new(b):
                wait(s, pv_mm, VG * b)
                s.dma_start(vn[0:1, :], m.newD[1][bass.ds(b, 1), :]).then_inc(vn_in, 16)

            def row_out(b):
                s.wait_ge(or_mm, b + 1)
                wait(s, o_out, 16 * b)
                for n in range(2):
                    last = nc.scalar.copy(orow[:, n * 512:(n + 1) * 512], SC_B[n][0:1, :])
                last.then_inc(or_ev, 1)
                s.wait_ge(or_ev, b + 1)
                s.dma_start(m.osD[bass.ds(b, 1), :], orow).then_inc(o_out, 16)

            def body(b):
                st = isinstance(b, int)
                for i in range(NQ):
                    u = NQ * b + i
                    if not (st and b == 0):
                        load_values(b - 1, 2 * i + 1)
                    if i:
                        c_copy(u - 1, i - 1)
                    s.wait_ge(nb_ok, u + 1)
                    for j in range(2):
                        x = SP[i % 2][j][:, 0:(i + 1) * P]
                        last = nc.scalar.activation(x, x, ACT.Exp, bias=mx[i % 2][:, j:j + 1], accum_out=ls[i % 2][:, j:j + 1])
                    last.then_inc(p_ok, 1)
                    if i == 1 and not (st and b == HB - 1):
                        stage(b + 1)
                    if i == NQ - 1:
                        load_values(b, 0)
                        if not (st and b == HB - 1):
                            q_copy(b + 1)
                            k_copy(b + 1)
                    elif not (st and b == 0):
                        load_values(b - 1, 2 * i + 2)
                        if i == 1:
                            load_new(b - 1)
                    if i == 1 and not (st and b < 2):
                        row_out(b - 2)
                s.wait_ge(sh_ok, b + 1)
                wait(s, pv_mm, VG * b)
                nc.scalar.activation(PR[:, :, 0:C], S, ACT.Exp).then_inc(e_ok, 1)
                c_copy(NQ * b + NQ - 1, NQ - 1)
            s.wait_ge(pt_in, 16)
            s.wait_ge(z_ok, 4)
            stage(0)
            q_copy(0)
            k_copy(0)
            seqs(s, body)
            load_values(NS - 1, 1)
            load_new(NS - 1)
            row_out(NS - 2)
            for p in range(2, VG):
                load_values(NS - 1, p)
            row_out(NS - 1)

        @block.vector
        def _(v):
            V = nc.vector
            v.wait_ge(t1, 2 * GRP + 1)
            for h in range(HB):
                V.tensor_scalar(BT[:, 0:PAGES, 2 * h:2 * h + 2], nd.unsqueeze(2).to_broadcast([P, PAGES, 2]),
                                2.0 ** (-8.0 * (h + 1) / HB), None, ALU.mult)

            def weigh(u, i):
                v.wait_ge(p_ok, u + 1)
                p1, p2 = (SP[i % 2][j][:, 0:(i + 1) * P] for j in range(2))
                V.reciprocal(r1[i], ls[i % 2][:, 1:2])
                V.tensor_scalar(lm, ls[i % 2][:, 0:1], m.lam, -1.0, ALU.mult, ALU.mult)
                v.drain()
                V.tensor_tensor(lm, lm, r1[i], ALU.mult)
                v.drain()
                V.reciprocal(r1[i], ls[i % 2][:, 0:1])
                V.scalar_tensor_tensor(out=p1, in0=p2, scalar=lm, in1=p1, op0=ALU.mult, op1=ALU.add).then_inc(c_ok, 1)

            def keep(u, i, h):
                v.wait_ge(o_mm, u + 1)
                V.tensor_scalar(m.v[:, i, bass.ds(h * DVB, DVB)], O_B[:, (i % 2) * DVB:(i % 2 + 1) * DVB], r1[i], None,
                                ALU.mult).then_inc(o_ev, 1)

            def unit(b, i):
                st = isinstance(b, int)
                u, w = NQ * b + i, (i + 1) * P
                v.wait_ge(sc_mm, u + 1)
                wait(v, c_tr, u - 1)
                for j in range(2):
                    V.scalar_tensor_tensor(out=SP[i % 2][j][:, 0:w], in0=m.dist[:, SEQ - w:SEQ], scalar=m.slope[:, bass.ds(b, 1)],
                                           in1=SC_B[j][:, 0:w], op0=ALU.mult, op1=ALU.add).then_inc(sb_ok, 1)
                v.drain()
                for j in range(2):
                    V.tensor_reduce(out=mx[i % 2][:, j:j + 1], in_=SP[i % 2][j][:, 0:w], axis=AX.X, op=ALU.max)
                v.drain()
                V.tensor_scalar(mx[i % 2], mx[i % 2], -1.0, None, ALU.mult).then_inc(nb_ok, 1)

            def multiply(b, j):
                if j < PAGES:
                    v.wait_ge(k_in[j % RING], 16 * (PAGES // RING) * b + 16 * (j // RING + 1))
                if j >= 4:
                    v.wait_ge(ks_ok, NP * b + j - 3)
                V.tensor_tensor(prod[j // 2 % 2], kp[j % RING] if j < PAGES else kn, qb, ALU.mult).then_inc(dp_ok, 1)

            def sum_page(b, j):
                if j % 2:
                    v.wait_ge(pp_ok, PAGES // 2 * b + (j + 1) // 2)
                else:
                    v.wait_ge(dp_ok, (PAGES // 2 + 1) * b + j // 2 + 1)
                V.tensor_reduce(out=S[:, j, :], in_=prod[2 if j % 2 else j // 2 % 2].rearrange("p (c d) -> p c d", d=DHB),
                                axis=AX.X, op=ALU.add).then_inc(ks_ok, 1)

            def fold(b):
                v.wait_ge(pv_mm, VG * (b + 1))
                wait(v, or_mm, b)
                for n in range(2):
                    c = slice(n * 512, (n + 1) * 512)
                    last = V.scalar_tensor_tensor(out=om[:, c], in0=PSO[n][:, :], scalar=cf, in1=bmask[:, c], op0=ALU.mult, op1=ALU.mult)
                last.then_inc(om_ok, 1)

            def body(b):
                st = isinstance(b, int)
                v.wait_ge(q_in, 16 * b + 16)
                v.wait_ge(kn_in, 16 * b + 16)
                multiply(b, 0)
                for i in range(NQ):
                    for j in range(GRP * i, GRP * i + GRP, 2):
                        multiply(b, j + 2)
                        sum_page(b, j)
                        sum_page(b, j + 1)
                        if j == GRP * i and i > 0:
                            weigh(NQ * b + i - 1, i - 1)
                            if i > 1:
                                keep(NQ * b + i - 2, i - 2, b)
                            elif not (st and b == 0):
                                keep(NQ * b - 1, NQ - 1, b - 1)
                    unit(b, i)
                sum_page(b, PAGES)
                v.drain()
                V.tensor_tensor(S, S, BT, ALU.add)
                v.drain()
                V.tensor_reduce(out=m1, in_=S.rearrange("p j c -> p c j"), axis=AX.X, op=ALU.max).then_inc(mx_ok, 1)
                weigh(NQ * b + NQ - 1, NQ - 1)
                v.wait_ge(mx_tr, b + 1)
                V.tensor_reduce(out=mr, in_=MISC[0:C, 0:P], axis=AX.X, op=ALU.max)
                v.drain()
                V.tensor_scalar(dg, m.ident[0:C, 0:C], mr, None, ALU.mult).then_inc(mr_ok, 1)
                keep(NQ * b + NQ - 2, NQ - 2, b)
                v.wait_ge(mb_mm, b + 1)
                V.tensor_tensor(S, S, MISC[:, P:P + C].unsqueeze(1).to_broadcast([P, NP, C]), ALU.subtract).then_inc(sh_ok, 1)
                if not (st and b == 0):
                    fold(b - 1)
                v.wait_ge(e_ok, b + 1)
                V.tensor_reduce(out=lsum, in_=PR[:, :, 0:C].rearrange("p j c -> p c j"), axis=AX.X, op=ALU.add)
                v.drain()
                V.tensor_copy(lw[:, :, 0:C], lsum.unsqueeze(1).to_broadcast([P, GRP, C])).then_inc(l_ok, 1)
                v.wait_ge(l_mm, b + 1)
                V.reciprocal(cf, MISC[:, 160:161])
                v.drain()
                V.tensor_tensor(cf, cf, m.coef, ALU.mult)
                v.drain()
            seqs(v, body)
            keep(HB * NQ - 1, NQ - 1, HB - 1)
            fold(NS - 1)


OUTS = [("y_prompt", (1, SEQ, D)), ("y_sample", (NS, 1, D)), ("s_prompt", (1, 1, HA, DKA, DVA)),
        ("s_sample", (1, NS, HA, DKA, DVA)), ("k_prompt", (1, SEQ // PAGE, PAGE, HB, 2 * DHB)),
        ("v_prompt", (1, SEQ // PAGE, PAGE, HB, DVB)), ("k_sample", (NS, 1, HB, 2 * DHB)),
        ("v_sample", (NS, 1, HB, DVB))]


def build(nc, a):
    held.clear()
    with ExitStack() as ctx:
        m = allocate(nc, ctx)
        stage_constants(nc, ctx, m)
        stage_ada(nc, ctx, m, a)
        stage_modulate(nc, ctx, m, "mix0", 0, 3, load_x=(a["x_prompt"], a["x_sample"]))
        stage_ln_rows(nc, ctx, m, "lnm0", a["ln_mix_g"][0], a["ln_mix_b"][0])
        stage_gla_project(nc, ctx, m, a)
        stage_gla_prompt(nc, ctx, m, a)
        stage_gla_sample(nc, ctx, m, a)
        stage_mix_output(nc, ctx, m, "glao", HA, a["gn_a"][0], True, 1.0, a["w_o_a"][0])
        stage_modulate(nc, ctx, m, "ffn0", 3, 3, keep_rows=True)
        stage_route(nc, ctx, m, 0, a)
        stage_experts(nc, ctx, m, 0, a)
        stage_combine(nc, ctx, m, 0)
        end_of_layer(nc)
        stage_modulate(nc, ctx, m, "kvm", 12, 2)
        stage_shared_kv(nc, ctx, m, a)
        stage_modulate(nc, ctx, m, "mix1", 6, 3)
        stage_queries(nc, ctx, m, a)
        stage_attention(nc, ctx, m, a)
        stage_ln_rows(nc, ctx, m, "lnm1", a["ln_mix_g"][1], a["ln_mix_b"][1])
        stage_mix_output(nc, ctx, m, "diffo", HB, a["subln_b"][0], False, 1.0 - LAM_INIT, a["w_o_b"][0])
        stage_modulate(nc, ctx, m, "ffn1", 9, 3, keep_rows=True)
        stage_route(nc, ctx, m, 1, a)
        stage_experts(nc, ctx, m, 1, a)
        stage_combine(nc, ctx, m, 1, stores=(a["y_prompt"], a["y_sample"]))


def kernel(**inputs):
    import numpy as _np
    import concourse.bacc as _bacc
    from concourse import mybir as _mybir
    from concourse.bass_utils import run_bass_kernel_spmd as _run

    nc = _bacc.Bacc("TRN2", target_bir_lowering=False, num_devices=1)
    arrays, a = {}, {}
    for name, value in inputs.items():
        x = _np.ascontiguousarray(value)
        arrays[f"in_{name}_dram"] = x
        a[name] = nc.dram_tensor(f"in_{name}_dram", x.shape, _mybir.dt.from_np(x.dtype), kind="ExternalInput").ap()
    for name, shape in OUTS:
        a[name] = nc.dram_tensor(f"out_{name}_dram", shape, F32, kind="ExternalOutput").ap()
    build(nc, a)
    r = _run(nc, [arrays], core_ids=[0])
    return tuple(r.results[0][f"out_{name}_dram"] for name, _ in OUTS)
```

```python
import math
from contextlib import ExitStack, nullcontext

import numpy as np
import concourse.bass as bass
from concourse import mybir

F32 = mybir.dt.float32
I32 = mybir.dt.int32
ALU = mybir.AluOpType
ACT = mybir.ActivationFunctionType
AX = mybir.AxisListType

P = 128
D = 1024
KT = D // P
SEQ, NS = 512, 8
TOK = SEQ + NS
TILES = [(i, P) for i in range(SEQ // P)] + [(SEQ // P, NS)]
NTT = len(TILES)
PAST, PAGE = 2048, 128
PAGES = PAST // PAGE
HA, DKA, DVA, CH = 4, 128, 256, 32
HB, DHB, DVB = 8, 64, 128
NE, NG, EPG, FF = 16, 4, 4, 512
DEPTH = 2
ALPHA = (2.0 * DEPTH) ** 0.25
LN_EPS, RMS_EPS, NEG = 1e-5, 1e-6, -1e30
LAM_INIT = 0.8 - 0.6 * math.exp(-0.3 * 1)
TAU = 16.0
SLOT_TILES = (2 * TOK + NE * (P - 1)) // P
SLOTS = SLOT_TILES * P
MIN_PAIRS = (-(-2 * TOK // P) + 1) // 2
LAST = SLOT_TILES + 1
NVEC = 6 * DEPTH + 2


held = []


def m_semaphore(nc, name):
    s = nc.alloc_semaphore(name=name)
    held.append(s)
    return nullcontext(s)


def free_semaphores(nc):
    nc.all_engine_barrier()
    nc.clear_and_free_semaphores(list(held))
    held.clear()
    nc.all_engine_barrier()


class Mem:
    pass


def rows_of(ap3, i, n):
    return ap3[0:n, i, :]


def allocate(nc, ctx):
    m = Mem()

    def sb(name, shape, dt=F32):
        return ctx.enter_context(nc.sbuf_tensor(name, shape, dt))

    m.x = sb("x_res", [P, NTT, D])
    m.xt = sb("xt", [P, KT, SEQ + 32])
    m.mod = sb("mod", [P, 2, 3, D])
    m.lnr = sb("lnr", [P, 2, D])
    m.ident = sb("ident", [P, P])
    m.ones = sb("ones", [P, P])
    m.fold = sb("fold", [P, 32])
    m.mv = sb("mv", [P, NTT, 2])
    m.st6 = sb("st6", [P, 2, 6])
    m.rs = sb("rs", [P, 2, NTT])
    m.dest = sb("dest", [P, 2, NTT], I32)
    m.wts = sb("wts", [P, 2, NTT])
    m.idx = sb("idx", [P, SLOT_TILES], I32)
    m.texp = sb("texp", [1, SLOT_TILES + 1], I32)
    m.full = sb("full", [1, SLOT_TILES], I32)
    m.small = sb("small", [P, 512])
    m.W = sb("arena_w", [P, 24576])
    m.R = sb("arena_r", [P, 9984])
    m.ps = [ctx.enter_context(nc.psum_tensor(f"ps{i}", [P, 512], F32)) for i in range(8)]
    m.psd = lambda n: m.ps[n]
    m.modD = nc.dram_tensor("mod_rows", (NVEC, NS + 1, D), F32).ap()
    m.xmD = nc.dram_tensor("xm_rows", (TOK, D), F32).ap()
    m.yD = nc.dram_tensor("y_rows", (SLOTS, D), F32).ap()
    m.idxD = [nc.dram_tensor(f"slot_token{l}", (SLOTS, 1), I32).ap() for l in range(DEPTH)]
    m.qsD = nc.dram_tensor("q_sample_rows", (NS, D), F32).ap()
    m.newD = [nc.dram_tensor(f"new_{n}_rows", (NS, D), F32).ap() for n in ("k", "v")]
    m.osD = nc.dram_tensor("o_sample_rows", (NS, D), F32).ap()
    return m


def view(t, off, *shape):
    n = int(np.prod(shape))
    v = t[:, off:off + n]
    if len(shape) == 2:
        return v.rearrange("p (a b) -> p a b", b=shape[1])
    if len(shape) == 3:
        return v.rearrange("p (a b c) -> p a b c", b=shape[1], c=shape[2])
    return v


def wait(eng, sem, value):
    if not isinstance(value, int) or value > 0:
        eng.wait_ge(sem, value)


def first_chunks(nc, ctx, m, name, src):
    m.wr = [view(m.W, u * 4096, KT, 512) for u in range(2)]
    return [(m.wr[c], src.rearrange("(p k) n -> p k n", k=KT)[:, :, c * 512:(c + 1) * 512],
             ctx.enter_context(m_semaphore(nc, f"{name}_w_in{c}"))) for c in range(2)]


def stage_constants(nc, ctx, m):
    s_z = ctx.enter_context(m_semaphore(nc, "const_filled"))
    s_id = ctx.enter_context(m_semaphore(nc, "ident_ok"))
    with nc.Block() as block:
        @block.gpsimd
        def _(g):
            nc.gpsimd.memset(m.ident[:, :], 0.0).then_inc(s_z, 1)
            nc.gpsimd.memset(m.ones[:, :], 1.0)
            nc.gpsimd.memset(m.mv[:, :, :], 1.0)
            nc.gpsimd.memset(m.xt[:, :, TOK:SEQ + 32], 0.0)
            g.wait_ge(s_z, 1)
            nc.gpsimd.affine_select(out=m.ident[:, :], in_=m.ident[:, :], compare_op=ALU.not_equal, fill=1.0,
                                    base=0, pattern=[[-1, P]], channel_multiplier=1).then_inc(s_id, 1)

        @block.vector
        def _(v):
            v.wait_ge(s_id, 1)
            nc.vector.tensor_reduce(out=m.fold[:, :], in_=m.ident[:, :].rearrange("p (g r) -> p r g", r=32), axis=AX.X, op=ALU.add)


def sample_parts(nc, m, bank, lhs, w):
    for k in range(KT):
        g = k % 4
        last = nc.tensor.matmul(bank[32 * g:32 * g + 32, :], lhs[:, k, :], w[:, k, :], start=(k < 4), stop=(k >= 4),
                                tile_position=(0, 32 * g))
    return last


def sample_sum(nc, m, bank, shares):
    return nc.tensor.matmul(bank[0:32, :], m.fold[:, :], shares, start=True, stop=True)


def stage_ada(nc, ctx, m, a):
    sem = lambda n: ctx.enter_context(m_semaphore(nc, n))
    c_in, ct_ps, ct_ok = sem("ada_c_in"), sem("ada_ct_ps"), sem("ada_ct_ok")
    w_in = [sem(f"ada_w_in{u}") for u in range(2)]
    b_in = [sem(f"ada_b_in{u}") for u in range(2)]
    mm, ev, copied, summed = (sem(f"ada_{n}") for n in ("mm", "ev", "copied", "summed"))
    st = [sem(f"ada_stored{u}") for u in range(2)]
    crow = m.R[0:NS + 1, 0:D]
    ct = view(m.R, D, KT, 32)
    shares = m.R[:, 6 * D:7 * D]
    w = [view(m.W, u * KT * D, KT, D) for u in range(2)]
    brow = [m.R[0:NS + 1, (2 + u) * D:(3 + u) * D] for u in range(2)]
    out = [m.R[0:NS + 1, (4 + u) * D:(5 + u) * D] for u in range(2)]
    pw = [a["w_ada"][l].rearrange("(p k) (v n) -> v p k n", k=KT, n=D) for l in range(DEPTH)]
    pw.append(a["w_ada_kv"].rearrange("(p k) (v n) -> v p k n", k=KT, n=D))
    pb = [a["b_ada"][l].rearrange("(v n) -> v n", n=D) for l in range(DEPTH)]
    pb.append(a["b_ada_kv"].rearrange("(v n) -> v n", n=D))
    parts = [(0, 0, 3), (1, 6, 3), (2, 12, 1)]
    with nc.Block() as block:
        @block.sync
        def _(sp):
            sp.dma_start(crow[0:NS, :], a["c_sample"]).then_inc(c_in, 16)
            sp.dma_start(m.R[NS:NS + 1, 0:D], a["c_prompt"]).then_inc(c_in, 16)

            def load(src, i, u, n2):
                sp.dma_start(w[u], pw[src][bass.ds(2 * i + u, 1)].rearrange("a p k n -> p (a k) n")).then_inc(w_in[u], 16)
                sp.dma_start(brow[u], pb[src][bass.ds(2 * i + u, 1)].to_broadcast([NS + 1, D])).then_inc(b_in[u], 16)

            for src, v0, pairs in parts:
                if src == 0:
                    for u in range(2):
                        load(src, 0, u, 0)
                lo = 1 if src == 0 else 0

                def body(i):
                    for u in range(2):
                        sp.wait_ge(mm, 2 * i + (v0 + u - 1))
                        sp.wait_ge(ev, 2 * i + (v0 + u - 1))
                        load(src, i, u, 0)
                if pairs - lo > 1:
                    with sp.Fori(lo, pairs) as i:
                        body(i)
                else:
                    body(lo)
            for u in range(2):
                sp.wait_ge(st[u], 16 * NVEC // 2)

        @block.tensor
        def _(pe):
            pe.wait_ge(c_in, 32)
            for k in range(KT):
                last = nc.tensor.transpose(m.ps[0][:, k * 16:k * 16 + NS + 1],
                                           crow.rearrange("b (p k) -> b k p", k=KT)[:, k, :],
                                           m.ident[0:NS + 1, 0:NS + 1])
            last.then_inc(ct_ps, 1)
            pe.wait_ge(ct_ok, 1)

            def body(i, v0):
                for u in range(2):
                    pe.wait_ge(w_in[u], 16 * i + 8 * v0 + 16)
                    for n in range(2):
                        last = sample_parts(nc, m, m.ps[n], ct, w[u][:, :, n * 512:(n + 1) * 512])
                    last.then_inc(mm, 1)
                    pe.wait_ge(copied, 2 * i + (v0 + u + 1))
                    if not (v0 == 0 and u == 0 and isinstance(i, int) and i == 0):
                        pe.wait_ge(ev, 2 * i + (v0 + u))
                    for n in range(2):
                        last = sample_sum(nc, m, m.ps[2 + n], shares[:, n * 512:(n + 1) * 512])
                    last.then_inc(summed, 1)
            for src, v0, pairs in parts:
                if src == 0:
                    body(0, 0)
                    with pe.Fori(1, pairs) as i:
                        body(i, v0)
                elif pairs > 1:
                    with pe.Fori(0, pairs) as i:
                        body(i, v0)
                else:
                    body(0, v0)

        @block.vector
        def _(v):
            nc.vector.memset(ct, 0.0)
            v.drain()
            v.wait_ge(ct_ps, 1)
            nc.vector.tensor_copy(ct[:, :, 0:NS + 1], m.ps[0][:, 0:16 * KT].rearrange("p (k c) -> p k c", c=16)[:, :, 0:NS + 1]).then_inc(ct_ok, 1)

            def body(i, v0):
                for u in range(2):
                    v.wait_ge(summed, 2 * i + (v0 + u + 1))
                    v.wait_ge(b_in[u], 16 * i + 8 * v0 + 16)
                    if not (v0 == 0 and isinstance(i, int) and i == 0):
                        v.wait_ge(st[u], 16 * i + 8 * v0)
                    for n in range(2):
                        c = slice(n * 512, (n + 1) * 512)
                        last = nc.vector.tensor_tensor(out[u][:, c], m.ps[2 + n][0:NS + 1, :], brow[u][:, c], ALU.add)
                    last.then_inc(ev, 1)
            body(0, 0)
            with v.Fori(1, 3) as i:
                body(i, 0)
            with v.Fori(0, 3) as i:
                body(i, 6)
            body(0, 12)

        @block.scalar
        def _(s):
            def copy(v):
                s.wait_ge(mm, v + 1)
                if not isinstance(v, int):
                    s.wait_ge(summed, v)
                for n in range(2):
                    last = nc.scalar.copy(shares[:, n * 512:(n + 1) * 512], m.ps[n][:, :])
                last.then_inc(copied, 1)

            def store(v, u):
                s.wait_ge(ev, v + 1)
                s.dma_start(m.modD[bass.ds(v, 1)].rearrange("a b n -> (a b) n"), out[u]).then_inc(st[u], 16)
            copy(0)
            with s.Fori(0, NVEC // 2 - 1) as i:
                for u in range(2):
                    copy(2 * i + u + 1)
                    store(2 * i + u, u)
            s.wait_ge(summed, NVEC - 1)
            copy(NVEC - 1)
            for v in (NVEC - 2, NVEC - 1):
                store(v, v % 2)


def stage_modulate(nc, ctx, m, name, vec, nvec, load_x=None, keep_rows=False, ahead=()):
    sem = lambda n: ctx.enter_context(m_semaphore(nc, f"{name}_{n}"))
    mod_in, x_in, xm_ok, tr, cp = (sem(n) for n in ("mod_in", "x_in", "xm_ok", "transposed", "copied"))
    rows_out = [sem(f"rows_out{u}") for u in range(2)]
    xm = [m.R[:, u * D:(u + 1) * D] for u in range(2)]
    with nc.Block() as block:
        @block.sync
        def _(sp):
            sp.dma_start(m.mod[:, 0, 0:nvec, :], m.modD[vec:vec + nvec, NS, :].partition_broadcast(P)).then_inc(mod_in, 16)
            sp.dma_start(m.mod[0:NS, 1, 0:nvec, :], m.modD[vec:vec + nvec, 0:NS, :].rearrange("v b n -> b v n")).then_inc(mod_in, 16)
            if load_x is not None:
                sp.dma_start(m.x[:, 0:NTT - 1, :], load_x[0].rearrange("b (i p) n -> p (b i) n", p=P)).then_inc(x_in, 16)
                sp.dma_start(m.x[0:NS, NTT - 1, :], load_x[1].rearrange("b s n -> (b s) n")).then_inc(x_in, 16)
            for buf, src, loaded in ahead:
                sp.dma_start(buf, src).then_inc(loaded, 16)
            if keep_rows:
                for i, r in TILES:
                    sp.wait_ge(xm_ok, i + 1)
                    sp.dma_start(m.xmD[i * P:i * P + r, :], xm[i % 2][0:r, :]).then_inc(rows_out[i % 2], 16)
                for u in range(2):
                    sp.wait_ge(rows_out[u], 16 * ((NTT + 1 - u) // 2))

        @block.vector
        def _(v):
            v.wait_ge(mod_in, 32)
            nc.vector.tensor_scalar(m.mod[:, 0, 1, :], m.mod[:, 0, 1, :], 1.0, None, ALU.add)
            nc.vector.tensor_scalar(m.mod[0:NS, 1, 1, :], m.mod[0:NS, 1, 1, :], 1.0, None, ALU.add)
            if load_x is not None:
                v.wait_ge(x_in, 32)
            v.drain()
            for i, r in TILES:
                kind = i // (NTT - 1)
                if i >= 2:
                    v.wait_ge(tr, i - 1)
                    if keep_rows:
                        v.wait_ge(rows_out[i % 2], 16 * (i // 2))
                nc.vector.tensor_tensor(xm[i % 2][0:r, :], m.x[0:r, i, :], m.mod[0:r, kind, 1, :], ALU.mult)
                v.drain()
                nc.vector.tensor_tensor(xm[i % 2][0:r, :], xm[i % 2][0:r, :], m.mod[0:r, kind, 0, :], ALU.add).then_inc(xm_ok, 1)

        @block.tensor
        def _(pe):
            for i, r in TILES:
                pe.wait_ge(xm_ok, i + 1)
                if i >= 2:
                    pe.wait_ge(cp, i - 1)
                for k in range(KT):
                    last = nc.tensor.transpose(m.ps[4 * (i % 2) + k // 4][:, (k % 4) * P:(k % 4) * P + r],
                                               xm[i % 2][0:r, :].rearrange("t (p k) -> t k p", k=KT)[:, k, :],
                                               m.ident[0:r, 0:r])
                last.then_inc(tr, 1)

        @block.scalar
        def _(s):
            for i, r in TILES:
                s.wait_ge(tr, i + 1)
                for n in range(2):
                    last = nc.scalar.copy(m.xt[:, 4 * n:4 * n + 4, i * P:i * P + r],
                                          m.ps[4 * (i % 2) + n][:, :].rearrange("p (k t) -> p k t", t=P)[:, :, 0:r])
                last.then_inc(cp, 1)


def stage_gla_project(nc, ctx, m, a, ahead):
    sem = lambda n: ctx.enter_context(m_semaphore(nc, f"glap_{n}"))
    w_in = [loaded for _, _, loaded in ahead]
    g_in, qk_mm, qk_ev, vr_mm, v_ev, r_ev, gd_mm, gd_ev, z_mm, z_ev, ab, ex, ln = (sem(n) for n in
        ("g_in", "qk_mm", "qk_ev", "vr_mm", "v_ev", "r_ev", "gd_mm", "gd_ev", "z_mm", "z_ev", "abs", "exp", "ln"))
    sh_mm, sh_cp, sm_mm, sm_ev = (sem(n) for n in ("sh_mm", "sh_cp", "sm_mm", "sm_ev"))
    shares = m.R[:, 6144:6656]
    m.v = view(m.W, 8192, NTT, D)
    m.r = view(m.W, 13312, NTT, D)
    m.q = view(m.W, 18432, HA, TOK)
    m.k = view(m.W, 18432 + HA * TOK, HA, TOK)
    m.g = view(m.R, 0, HA, TOK)
    t1 = view(m.R, HA * TOK, HA, TOK)
    wgd = view(m.R, 2 * HA * TOK, KT, 16)
    wgu = m.R[0:16, 2 * HA * TOK + 128:2 * HA * TOK + 640]
    gd = m.R[0:16, 2 * HA * TOK + 640:2 * HA * TOK + 640 + TOK]
    bg = m.small[:, 0:HA]
    w_src = a["w_in_a"][0].rearrange("(p k) n -> p k n", k=KT)
    with nc.Block() as block:
        @block.sync
        def _(sp):
            for c in range(6):
                if c >= 2:
                    if c - 2 < 2:
                        sp.wait_ge(qk_mm, HA * (c - 1))
                    else:
                        sp.wait_ge(vr_mm, (NTT - 1) * (c - 3))
                    sp.dma_start(m.wr[c % 2], w_src[:, :, c * 512:(c + 1) * 512]).then_inc(w_in[c % 2], 16)
                if c == 1:
                    sp.dma_start(wgd, w_src[:, :, 3072:3088]).then_inc(g_in, 16)
                    sp.dma_start(wgu, a["w_gate_up_a"][0]).then_inc(g_in, 16)
                    with nc.allow_non_contiguous_dma(reason="512 gate offsets, one per partition and head"):
                        sp.dma_start(bg, a["b_gate_a"][0].rearrange("(h p) -> p h", p=P)).then_inc(g_in, 16)

        @block.tensor
        def _(pe):
            for c in range(2):
                pe.wait_ge(w_in[c], 16)
                for h in range(HA):
                    n = c * HA + h
                    if n >= 2:
                        pe.wait_ge(qk_ev, n - 1)
                    for k in range(KT):
                        w = m.wr[c][:, k, h * P:(h + 1) * P]
                        nc.tensor.matmul(m.ps[n % 2][:, :], w, m.xt[:, k, 0:SEQ], start=(k == 0), stop=(k == KT - 1))
                        last = nc.tensor.matmul(m.ps[2 + n % 2][:, 0:NS], w, m.xt[:, k, SEQ:TOK],
                                                start=(k == 0), stop=(k == KT - 1))
                    last.then_inc(qk_mm, 1)
            pe.wait_ge(g_in, 48)
            pe.wait_ge(qk_ev, 2 * HA)
            for k in range(KT):
                nc.tensor.matmul(m.ps[0][0:16, :], wgd[:, k, :], m.xt[:, k, 0:SEQ], start=(k == 0), stop=(k == KT - 1))
                last = nc.tensor.matmul(m.ps[1][0:16, 0:NS], wgd[:, k, :], m.xt[:, k, SEQ:TOK],
                                        start=(k == 0), stop=(k == KT - 1))
            last.then_inc(gd_mm, 1)
            pe.wait_ge(gd_ev, 1)
            for h in range(HA):
                if h >= 1:
                    pe.wait_ge(z_ev, h)
                nc.tensor.matmul(m.ps[2][:, :], wgu[:, h * P:(h + 1) * P], gd[:, 0:SEQ], start=True, stop=True)
                nc.tensor.matmul(m.ps[3][:, 0:NS], wgu[:, h * P:(h + 1) * P], gd[:, SEQ:TOK],
                                 start=True, stop=True).then_inc(z_mm, 1)
            for c in range(4):
                pe.wait_ge(w_in[c % 2], 16 * (c // 2 + 2))
                wait(pe, sh_cp, c)
                sample_parts(nc, m, m.ps[0], m.xt[:, :, SEQ:SEQ + 32], m.wr[c % 2]).then_inc(sh_mm, 1)
                for i in range(NTT - 1):
                    n = c * (NTT - 1) + i
                    wait(pe, *((v_ev, n - 3) if n - 4 < 2 * (NTT - 1) else (r_ev, n - 3 - 2 * (NTT - 1))))
                    for k in range(KT):
                        last = nc.tensor.matmul(m.ps[4 + n % 4][:, :], m.xt[:, k, i * P:(i + 1) * P],
                                                m.wr[c % 2][:, k, :], start=(k == 0), stop=(k == KT - 1))
                    last.then_inc(vr_mm, 1)
                pe.wait_ge(sh_cp, c + 1)
                wait(pe, sm_ev, c)
                sample_sum(nc, m, m.ps[1], shares).then_inc(sm_mm, 1)

        @block.scalar
        def _(s):
            for n in range(2 * HA):
                s.wait_ge(qk_mm, n + 1)
                dst = (m.q, m.k)[n // HA]
                scale = DKA ** -0.5 if n < HA else 1.0
                nc.scalar.activation(dst[:, n % HA, 0:SEQ], m.ps[n % 2][:, :], ACT.Copy, scale=scale)
                nc.scalar.activation(dst[:, n % HA, SEQ:TOK], m.ps[2 + n % 2][:, 0:NS], ACT.Copy,
                                     scale=scale).then_inc(qk_ev, 1)
            s.wait_ge(z_ev, HA)
            nc.scalar.activation(t1, m.g, ACT.Abs).then_inc(ab, 1)
            s.wait_ge(ab, 1)
            nc.scalar.activation(t1, t1, ACT.Exp, scale=-1.0).then_inc(ex, 1)
            s.wait_ge(ex, 1)
            nc.scalar.activation(t1, t1, ACT.Ln, bias=1.0).then_inc(ln, 1)
            for c in range(4):
                s.wait_ge(sh_mm, c + 1)
                wait(s, sm_mm, c)
                nc.scalar.copy(shares, m.ps[0][:, :]).then_inc(sh_cp, 1)
                for i in range(NTT - 1):
                    if c >= 2:
                        n = c * (NTT - 1) + i
                        s.wait_ge(vr_mm, n + 1)
                        nc.scalar.activation(m.r[:, i, (c - 2) * 512:(c - 1) * 512], m.ps[4 + n % 4][:, :], ACT.Silu).then_inc(r_ev, 1)
                s.wait_ge(sm_mm, c + 1)
                nc.scalar.activation((m.v, m.r)[c // 2][0:NS, NTT - 1, (c % 2) * 512:(c % 2 + 1) * 512], m.ps[1][0:NS, :],
                                     (ACT.Copy, ACT.Silu)[c // 2]).then_inc(sm_ev, 1)

        @block.vector
        def _(v):
            v.wait_ge(gd_mm, 1)
            nc.vector.tensor_copy(gd[:, 0:SEQ], m.ps[0][0:16, :])
            nc.vector.tensor_copy(gd[:, SEQ:TOK], m.ps[1][0:16, 0:NS]).then_inc(gd_ev, 1)
            for h in range(HA):
                v.wait_ge(z_mm, h + 1)
                nc.vector.tensor_scalar(m.g[:, h, 0:SEQ], m.ps[2][:, :], bg[:, h:h + 1], None, ALU.add)
                nc.vector.tensor_scalar(m.g[:, h, SEQ:TOK], m.ps[3][:, 0:NS], bg[:, h:h + 1], None, ALU.add).then_inc(z_ev, 1)
            for c in range(2):
                for i in range(NTT - 1):
                    n = c * (NTT - 1) + i
                    v.wait_ge(vr_mm, n + 1)
                    nc.vector.tensor_copy(m.v[:, i, c * 512:(c + 1) * 512], m.ps[4 + n % 4][:, :]).then_inc(v_ev, 1)
                if c == 1:
                    v.wait_ge(ln, 1)
                    nc.vector.tensor_scalar(m.g, m.g, 0.0, None, ALU.min)
                    v.drain()
                    nc.vector.tensor_tensor(m.g, m.g, t1, ALU.subtract)
                    v.drain()
                    nc.vector.tensor_scalar(m.g, m.g, 1.0 / TAU, None, ALU.mult)


def stage_gla_prompt(nc, ctx, m, a):
    sem = lambda n: ctx.enter_context(m_semaphore(nc, f"gla_{n}"))
    (start_ok, mask_ok, cum_ok, dif_ok, exp_ok, fac_ok, kl_tr, kl_ok, at_mm, at_ok, v_ok, ds_mm, s_ok, o_mm, o_ev, s_out) = (
        sem(n) for n in ("start_ok", "mask_ok", "cum_ok", "dif_ok", "exp_ok", "fac_ok", "kl_tr", "kl_ok", "at_mm",
                         "at_ok", "v_ok", "ds_mm", "s_ok", "o_mm", "o_ev", "s_out"))
    y_fill = sem("y_fill")
    NCH = P // CH
    off = [HA * TOK]

    def take(*shape):
        v = view(m.R, off[0], *shape)
        off[0] += int(np.prod(shape))
        return v
    cum = take(HA, P)
    mask = take(1, P)[:, 0, :]
    dmid, dlast = take(HA, P), take(HA, P)
    emid, ekey, ecum, elast = take(HA, P), take(HA, P), take(HA, P), take(HA, P)
    kls = take(HA, P)
    ats = take(HA, CH)
    tri = take(1, CH)[:, 0, :]
    S = [view(m.W, u * D, HA, DVA) for u in range(2)]
    vs = view(m.W, 2 * D, HA, DVA)
    eend = view(m.W, 3 * D, HA, NCH)
    qe, qm, km, kl = (view(m.W, 4 * D + j * 512, HA, P) for j in range(4))
    chunks = lambda t: t.rearrange("p h (c t) -> p h c t", t=CH)
    at_ps = m.ps[0][:, 0:P].rearrange("p (h t) -> p h t", t=CH)
    kl_ps = m.ps[1][:, :].rearrange("p (h k) -> p h k", k=P)
    with nc.Block() as block:
        @block.gpsimd
        def _(g):
            nc.gpsimd.memset(mask, 1.0).then_inc(start_ok, 1)
            nc.gpsimd.memset(tri, 1.0).then_inc(start_ok, 1)
            nc.gpsimd.memset(view(m.W, 0, 1, D), 0.0).then_inc(start_ok, 1)
            g.wait_ge(start_ok, 3)
            nc.gpsimd.memset(mask.rearrange("p (c t) -> p c t", t=CH)[:, :, 0:1], 0.0).then_inc(mask_ok, 1)
            for c in range(NCH):
                g.wait_ge(mask_ok, 1 + c)
                nc.gpsimd.affine_select(out=tri[c * CH:(c + 1) * CH, :], in_=tri[c * CH:(c + 1) * CH, :],
                                        compare_op=ALU.is_ge, fill=0.0, base=0, pattern=[[1, CH]],
                                        channel_multiplier=-1).then_inc(mask_ok, 1)

        @block.vector
        def _(v):
            v.wait_ge(mask_ok, 1 + NCH)

            def body(i, first):
                tok = bass.ds(i * P, P)
                if not first:
                    v.wait_ge(exp_ok, i)
                for h in range(HA):
                    last = nc.vector.tensor_tensor_scan(cum[:, h, :], mask, m.g[:, h, tok], 0.0, ALU.mult, ALU.add)
                v.drain()
                c4 = chunks(cum)
                mid = c4[:, :, :, CH // 2 - 1:CH // 2].to_broadcast([P, HA, NCH, CH])
                end = c4[:, :, :, CH - 1:CH].to_broadcast([P, HA, NCH, CH])
                nc.vector.tensor_tensor(chunks(dmid), c4, mid, ALU.subtract)
                nc.vector.tensor_tensor(chunks(dlast), end, c4, ALU.subtract).then_inc(dif_ok, 1)
                v.wait_ge(exp_ok, i + 1)
                if not first:
                    v.wait_ge(o_mm, NCH * i)
                nc.vector.tensor_tensor(kl, m.k[:, :, tok], elast, ALU.mult)
                nc.vector.tensor_tensor(qm, m.q[:, :, tok], emid, ALU.mult)
                nc.vector.tensor_tensor(km, m.k[:, :, tok], ekey, ALU.mult)
                nc.vector.tensor_tensor(qe, m.q[:, :, tok], ecum, ALU.mult).then_inc(fac_ok, 1)
                v.wait_ge(at_mm, i + 1)
                nc.vector.tensor_tensor(ats, at_ps, tri.unsqueeze(1).to_broadcast([P, HA, CH]), ALU.mult).then_inc(at_ok, 1)
                for c in range(NCH):
                    v.wait_ge(ds_mm, NCH * i + c + 1)
                    if c >= 1:
                        v.wait_ge(o_mm, NCH * i + c)
                    for h in range(HA):
                        nc.vector.scalar_tensor_tensor(out=S[(c + 1) % 2][:, h, :], in0=S[c % 2][:, h, :],
                                                       scalar=eend[:, h, c:c + 1],
                                                       in1=m.ps[4 + 2 * (c % 2) + h // 2][:, (h % 2) * DVA:(h % 2 + 1) * DVA],
                                                       op0=ALU.mult, op1=ALU.add).then_inc(s_ok, 1)
                    v.drain()
                v.wait_ge(o_mm, NCH * i + NCH)
                for n in range(2):
                    last = nc.vector.tensor_copy(m.v[:, bass.ds(i, 1), n * 512:(n + 1) * 512].rearrange("p a n -> p (a n)"),
                                                 m.ps[2 + n][:, :])
                last.then_inc(o_ev, 1)
            body(0, True)
            with v.Fori(1, SEQ // P) as i:
                body(i, False)

        @block.scalar
        def _(s):
            def body(i, first):
                if not first:
                    s.wait_ge(o_mm, NCH * i)
                nc.scalar.copy(vs.rearrange("p h n -> p (h n)"), m.v[:, bass.ds(i, 1), :].rearrange("p a n -> p (a n)")).then_inc(v_ok, 1)
                s.wait_ge(dif_ok, i + 1)
                if not first:
                    s.wait_ge(fac_ok, i)
                    s.wait_ge(s_ok, HA * NCH * i)
                nc.scalar.activation(elast, dlast, ACT.Exp)
                nc.scalar.activation(emid, dmid, ACT.Exp)
                nc.scalar.activation(ekey, dmid, ACT.Exp, scale=-1.0)
                nc.scalar.activation(ecum, cum, ACT.Exp)
                nc.scalar.activation(eend, chunks(cum)[:, :, :, CH - 1], ACT.Exp).then_inc(exp_ok, 1)
                s.wait_ge(kl_tr, i + 1)
                nc.scalar.copy(kls, kl_ps).then_inc(kl_ok, 1)
            body(0, True)
            with s.Fori(1, SEQ // P) as i:
                body(i, False)

        @block.tensor
        def _(pe):
            def state(i, c):
                r = slice(c * CH, (c + 1) * CH)
                for h in range(HA):
                    last = nc.tensor.matmul(m.ps[4 + 2 * (c % 2) + h // 2][:, (h % 2) * DVA:(h % 2 + 1) * DVA],
                                            kls[r, h, :], vs[r, h, :], start=True, stop=True, tile_position=(c * CH, 0))
                last.then_inc(ds_mm, 1)

            def body(i, first):
                pe.wait_ge(fac_ok, i + 1)
                for h in range(HA):
                    last = nc.tensor.transpose(kl_ps[:, h, :], kl[:, h, :], m.ident[:, :])
                last.then_inc(kl_tr, 1)
                for h in range(HA):
                    for c in range(NCH):
                        r = slice(c * CH, (c + 1) * CH)
                        last = nc.tensor.matmul(at_ps[r, h, :], km[:, h, r], qm[:, h, r], start=True, stop=True,
                                                tile_position=(0, c * CH))
                last.then_inc(at_mm, 1)
                pe.wait_ge(kl_ok, i + 1)
                pe.wait_ge(v_ok, i + 1)
                pe.wait_ge(at_ok, i + 1)
                if not first:
                    pe.wait_ge(o_ev, i)
                    pe.wait_ge(s_ok, HA * NCH * i)
                state(i, 0)
                for c in range(NCH):
                    r = slice(c * CH, (c + 1) * CH)
                    if c + 1 < NCH:
                        if c >= 1:
                            pe.wait_ge(s_ok, HA * (NCH * i + c))
                        state(i, c + 1)
                    for h in range(HA):
                        o = m.ps[2 + h // 2][r, (h % 2) * DVA:(h % 2 + 1) * DVA]
                        if c >= 1:
                            pe.wait_ge(s_ok, HA * (NCH * i + c - 1) + h + 1)
                        nc.tensor.matmul(o, qe[:, h, r], S[c % 2][:, h, :], start=True, stop=False, tile_position=(0, c * CH))
                        last = nc.tensor.matmul(o, ats[r, h, :], vs[r, h, :], start=False, stop=True,
                                                tile_position=(c * CH, c * CH))
                    last.then_inc(o_mm, 1)
            body(0, True)
            with pe.Fori(1, SEQ // P) as i:
                body(i, False)

        @block.sync
        def _(sp):
            most = 2 * MIN_PAIRS * P
            sp.dma_start(m.yD[most:SLOTS, :].rearrange("(t p) n -> p t n", p=P),
                         m.lnr[:, 0:1, :].to_broadcast([P, (SLOTS - most) // P, D])).then_inc(y_fill, 16)
            sp.wait_ge(y_fill, 16)
            sp.wait_ge(s_ok, HA * NCH * (SEQ // P))
            sp.dma_start(a["s_prompt"].rearrange("l b h k v -> k (l b h) v"), S[0]).then_inc(s_out, 16)
            sp.wait_ge(s_out, 16)


def stage_gla_sample(nc, ctx, m, a):
    sem = lambda n: ctx.enter_context(m_semaphore(nc, f"glas_{n}"))
    st_in, eg_ok, sel_ok, dg_ok, vb_mm, s_ok, o_mm, o_out, qs_ok = (sem(n) for n in
        ("st_in", "eg_ok", "sel_ok", "dg_ok", "vb_mm", "s_ok", "o_mm", "o_out", "qs_ok"))
    st = view(m.W, 0, NS * HA, DVA)
    off = HA * TOK
    eg = view(m.R, off, HA, NS)
    qsel = view(m.R, off + 32, HA, NS * NS)
    sel = m.R[0:NS, off + 32 + HA * NS * NS:off + 32 + HA * NS * NS + NS * P]
    src = a["state_gla"].rearrange("l b h k v -> k (l b h) v")
    dst = a["s_sample"].rearrange("l b h k v -> k (l b h) v")
    with nc.Block() as block:
        @block.sync
        def _(sp):
            sp.dma_start(st, src).then_inc(st_in, 16)
            for b in range(NS):
                sp.wait_ge(s_ok, b + 1)
                sp.dma_start(dst[:, b * HA:(b + 1) * HA, :], st[:, b * HA:(b + 1) * HA, :]).then_inc(o_out, 16)
            sp.wait_ge(o_out, 16 * NS)

        @block.gpsimd
        def _(g):
            nc.gpsimd.memset(sel, 0.0).then_inc(sel_ok, 1)
            g.wait_ge(sel_ok, 1)
            nc.gpsimd.affine_select(out=sel.rearrange("r (b n) -> r b n", n=P), in_=sel.rearrange("r (b n) -> r b n", n=P),
                                    compare_op=ALU.not_equal, fill=1.0, base=0, pattern=[[-1, NS], [0, P]],
                                    channel_multiplier=1).then_inc(dg_ok, 1)

        @block.scalar
        def _(s):
            nc.scalar.activation(eg, m.g[:, :, SEQ:TOK], ACT.Exp).then_inc(eg_ok, 1)

        @block.vector
        def _(v):
            nc.vector.memset(qsel, 0.0)
            v.drain()
            nc.vector.tensor_copy(qsel[:, :, 0:NS * NS:NS + 1], m.q[:, :, SEQ:TOK]).then_inc(qs_ok, 1)
            v.wait_ge(st_in, 16)
            v.wait_ge(eg_ok, 1)
            for b in range(NS):
                for h in range(HA):
                    nc.vector.tensor_scalar(st[:, b * HA + h, :], st[:, b * HA + h, :], eg[:, h, b:b + 1], None, ALU.mult)
                v.wait_ge(vb_mm, b + 1)
                v.drain()
                for h in range(HA):
                    last = nc.vector.scalar_tensor_tensor(
                        out=st[:, b * HA + h, :], in0=m.ps[2 * (b % 2) + h // 2][:, (h % 2) * DVA:(h % 2 + 1) * DVA],
                        scalar=m.k[:, h, SEQ + b:SEQ + b + 1], in1=st[:, b * HA + h, :], op0=ALU.mult, op1=ALU.add)
                last.then_inc(s_ok, 1)
            v.wait_ge(o_mm, 1)
            for h in range(HA):
                nc.vector.tensor_copy(m.v[0:NS, NTT - 1, h * DVA:(h + 1) * DVA], m.ps[4 + h][0:NS, 0:DVA])

        @block.tensor
        def _(pe):
            pe.wait_ge(dg_ok, 1)
            pe.wait_ge(qs_ok, 1)

            def spread(b):
                if b >= 2:
                    pe.wait_ge(s_ok, b - 1)
                for n in range(2):
                    last = nc.tensor.matmul(m.ps[2 * (b % 2) + n][:, :], sel[:, b * P:(b + 1) * P],
                                            m.v[0:NS, NTT - 1, n * 512:(n + 1) * 512], start=True, stop=True)
                last.then_inc(vb_mm, 1)
            spread(0)
            for b in range(NS):
                if b + 1 < NS:
                    spread(b + 1)
                pe.wait_ge(s_ok, b + 1)
                for h in range(HA):
                    last = nc.tensor.matmul(m.ps[4 + h][0:NS, 0:DVA], qsel[:, h, b * NS:(b + 1) * NS], st[:, b * HA + h, :],
                                            start=(b == 0), stop=(b == NS - 1))
            last.then_inc(o_mm, 1)


def stage_mix_output(nc, ctx, m, name, groups, gain, gate_r, factor, w_o):
    sem = lambda n: ctx.enter_context(m_semaphore(nc, f"{name}_{n}"))
    gn_in, w_in, eps_ok, sq_ok, sd_ok, row_ok, tr, cp, mm, ev, sh_mm, sh_cp = (sem(n) for n in
        ("gn_in", "w_in", "eps_ok", "sq_ok", "sd_ok", "row_ok", "tr", "cp", "mm", "ev", "sh_mm", "sh_cp"))
    width = D // groups
    gn = m.R[:, 0:width]
    sq = [m.R[:, (1 + u) * D:(2 + u) * D] for u in range(2)]
    shares = [m.R[:, 3 * D + 512 * n:3 * D + 512 * (n + 1)] for n in range(2)]
    ss = m.R[:, 5 * D:5 * D + NTT * groups].rearrange("p (i g) -> p i g", g=groups)
    w = view(m.W, 0, KT, D)
    order = [TILES[-1]] + TILES[:-1]
    ln = LayerNorm(nc, ctx, m, name)
    with nc.Block() as block:
        @block.sync
        def _(sp):
            sp.dma_start(gn, gain.partition_broadcast(P)).then_inc(gn_in, 16)
            sp.dma_start(w, w_o.rearrange("(p k) n -> p k n", k=KT)).then_inc(w_in, 16)

        @block.scalar
        def _(s):
            def transposed(s, n):
                i, r = order[n]
                s.wait_ge(tr, n + 1)
                for c in range(2):
                    last = nc.scalar.copy(m.xt[:, 4 * c:4 * c + 4, i * P:i * P + r],
                                          m.ps[2 * (n % 2) + c][:, :].rearrange("p (k t) -> p k t", t=P)[:, :, 0:r])
                last.then_inc(cp, 1)

            s.wait_ge(eps_ok, 1)
            for n, (i, r) in enumerate(order):
                s.wait_ge(sq_ok, n + 1)
                nc.scalar.activation(ss[0:r, i, :], ss[0:r, i, :], ACT.Sqrt, scale=1.0 / width, bias=m.small[0:r, 500:501]).then_inc(sd_ok, 1)
                if n == NTT - 1:
                    ln.scalar(s, *order[0])
                if n:
                    transposed(s, n - 1)
                if n == 2:
                    s.wait_ge(sh_mm, 1)
                    for c in range(2):
                        last = nc.scalar.copy(shares[c], m.ps[4 + c][:, :])
                    last.then_inc(sh_cp, 1)
            ln.scalar(s, *order[1])
            transposed(s, NTT - 1)
            for i, r in order[2:]:
                ln.scalar(s, i, r)

        @block.vector
        def _(v):
            nc.vector.memset(m.small[:, 500:501], RMS_EPS)
            nc.vector.memset(m.small[:, 501:502], LN_EPS).then_inc(eps_ok, 1)
            v.wait_ge(gn_in, 16)
            if factor != 1.0:
                nc.vector.tensor_scalar(gn, gn, factor, None, ALU.mult)
            v.drain()

            def squares(n):
                i, r = order[n]
                nc.vector.tensor_tensor(sq[n % 2][0:r, :], m.v[0:r, i, :], m.v[0:r, i, :], ALU.mult)
                v.drain()
                nc.vector.tensor_reduce(out=ss[0:r, i, :], in_=sq[n % 2][0:r, :].rearrange("p (g w) -> p g w", g=groups),
                                        axis=AX.X, op=ALU.add).then_inc(sq_ok, 1)
            squares(0)
            for n, (i, r) in enumerate(order):
                if n + 1 < NTT:
                    squares(n + 1)
                v.wait_ge(sd_ok, n + 1)
                nc.vector.reciprocal(ss[0:r, i, :], ss[0:r, i, :])
                row = m.v[0:r, i, :].rearrange("p (g w) -> p g w", g=groups)
                nc.vector.tensor_tensor(row, row, gn[0:r, :].unsqueeze(1).to_broadcast([r, groups, width]), ALU.mult)
                v.drain()
                last = nc.vector.tensor_tensor(row, row, ss[0:r, i, :].unsqueeze(2).to_broadcast([r, groups, width]), ALU.mult)
                if gate_r:
                    v.drain()
                    last = nc.vector.tensor_tensor(m.v[0:r, i, :], m.v[0:r, i, :], m.r[0:r, i, :], ALU.mult)
                last.then_inc(row_ok, 1)
            for n, (i, r) in enumerate(order):
                v.wait_ge(mm, n + 1)
                banks = (6, 7) if n == 0 else (4, 5) if n % 2 else (6, 7)
                ln.mixed(v, i, r, [m.ps[b] for b in banks]).then_inc(ev, 1)
                ln.stats(v, i, r)
                if n:
                    ln.shift(v, *order[n - 1])
            ln.shift(v, *order[-1])

        @block.tensor
        def _(pe):
            def transpose(n):
                i, r = order[n]
                pe.wait_ge(row_ok, n + 1)
                wait(pe, cp, n - 1)
                for k in range(KT):
                    last = nc.tensor.transpose(m.ps[2 * (n % 2) + k // 4][:, (k % 4) * P:(k % 4) * P + r],
                                               m.v[0:r, i, :].rearrange("t (p k) -> t k p", k=KT)[:, k, :],
                                               m.ident[0:r, 0:r])
                last.then_inc(tr, 1)

            def project(n):
                i, r = order[n]
                pe.wait_ge(cp, n + 1)
                wait(pe, ev, n - 1)
                for c in range(2):
                    for k in range(KT):
                        last = nc.tensor.matmul(m.ps[(4 if n % 2 else 6) + c][0:r, :], m.xt[:, k, i * P:i * P + r],
                                                w[:, k, c * 512:(c + 1) * 512], start=(k == 0), stop=(k == KT - 1))
                last.then_inc(mm, 1)
            transpose(0)
            transpose(1)
            pe.wait_ge(w_in, 16)
            pe.wait_ge(cp, 1)
            for n in range(2):
                last = sample_parts(nc, m, m.ps[4 + n], m.xt[:, :, SEQ:SEQ + 32], w[:, :, n * 512:(n + 1) * 512])
            last.then_inc(sh_mm, 1)
            transpose(2)
            pe.wait_ge(sh_cp, 1)
            for n in range(2):
                last = sample_sum(nc, m, m.ps[6 + n], shares[n])
            last.then_inc(mm, 1)
            for n in range(1, NTT):
                project(n)
                if n + 2 < NTT:
                    transpose(n + 2)


class LayerNorm:

    def __init__(self, nc, ctx, m, name):
        sem = lambda n: ctx.enter_context(m_semaphore(nc, f"{name}_ln_{n}"))
        self.nc, self.m = nc, m
        self.var_ok, self.sd_ok, self.bias_ok, self.scaled = (sem(n) for n in ("var_ok", "sd_ok", "bias_ok", "scaled"))
        self.done = sem("done")
        self.tiles = self.sds = self.scales = 0

    def mixed(self, v, i, r, halves):
        nc, m = self.nc, self.m
        for n in range(2):
            c = slice(n * 512, (n + 1) * 512)
            last = nc.vector.tensor_tensor(m.R[0:r, 6 * D + n * 512:6 * D + (n + 1) * 512], halves[n][0:r, :],
                                           m.mod[0:r, i // (NTT - 1), 2, c], ALU.mult)
        return last

    def stats(self, v, i, r):
        nc, m = self.nc, self.m
        v.drain()
        nc.vector.scalar_tensor_tensor(out=m.x[0:r, i, :], in0=m.x[0:r, i, :], scalar=ALPHA,
                                       in1=m.R[0:r, 6 * D:7 * D], op0=ALU.mult, op1=ALU.add)
        v.drain()
        for n in range(2):
            nc.vector.bn_stats(m.st6[0:r, n, :], m.x[0:r, i, n * 512:(n + 1) * 512])
        v.drain()
        nc.vector.bn_aggr(m.mv[0:r, i, :], m.st6[0:r, :, :]).then_inc(self.var_ok, 1)
        self.tiles += 1
        v.wait_ge(self.sd_ok, self.tiles)
        nc.vector.reciprocal(m.rs[0:r, 0, i:i + 1], m.rs[0:r, 0, i:i + 1])
        v.drain()
        nc.vector.scalar_tensor_tensor(out=m.rs[0:r, 1, i:i + 1], in0=m.mv[0:r, i, 0:1], scalar=-1.0,
                                       in1=m.rs[0:r, 0, i:i + 1], op0=ALU.mult, op1=ALU.mult).then_inc(self.bias_ok, 1)

    def shift(self, v, i, r):
        nc, m = self.nc, self.m
        self.scales += 1
        v.wait_ge(self.scaled, self.scales)
        nc.vector.tensor_tensor(m.x[0:r, i, :], m.x[0:r, i, :], m.lnr[0:r, 0, :], ALU.mult)
        v.drain()
        nc.vector.tensor_tensor(m.x[0:r, i, :], m.x[0:r, i, :], m.lnr[0:r, 1, :], ALU.add).then_inc(self.done, 1)

    def scalar(self, s, i, r):
        nc, m = self.nc, self.m
        self.sds += 1
        s.wait_ge(self.var_ok, self.sds)
        nc.scalar.activation(m.rs[0:r, 0, i:i + 1], m.mv[0:r, i, 1:2], ACT.Sqrt, bias=m.small[0:r, 501:502]).then_inc(self.sd_ok, 1)
        s.wait_ge(self.bias_ok, self.sds)
        nc.scalar.activation(m.x[0:r, i, :], m.x[0:r, i, :], ACT.Identity, scale=m.rs[0:r, 0, i:i + 1],
                             bias=m.rs[0:r, 1, i:i + 1]).then_inc(self.scaled, 1)


def expert_weights(nc, ctx, m, l, a):
    return [(n, [view(m.W, (2 * j + u) * 4096, k, 4096 // k) for u in range(2)], a[f"w_exp_{n}"][l],
             [ctx.enter_context(m_semaphore(nc, f"moe{l}_{n}_in{u}")) for u in range(2)], k)
            for j, (n, k) in enumerate((("gate", KT), ("up", KT), ("down", FF // P)))]


def load_expert(sp, m, weights, tile, u, free=None):
    e = sp.value_load(m.texp[0:1, tile], min_val=0, max_val=NE - 1)
    for name, buf, source, loaded, k in weights:
        if free is not None:
            sp.wait_ge(*free[name])
        sp.dma_start(buf[u].rearrange("p k n -> p (k n)"),
                     source[bass.ds(e, 1)].rearrange("a (p k) n -> p (a k n)", k=k)).then_inc(loaded[u], 16)


def stage_route(nc, ctx, m, l, a, weights):
    sem = lambda n: ctx.enter_context(m_semaphore(nc, f"route{l}_{n}"))
    w_in, ln_in, tab, mm, ev, sel_ok, rk_mm, rk2, z_in, z_out, dst_ok, sc_out, ix_in, tri_ok, te_ok = (sem(n) for n in
        ("w_in", "ln_in", "tab", "mm", "ev", "sel_ok", "rk_mm", "rk2", "z_in", "z_out", "dst_ok", "sc_out", "ix_in",
         "tri_ok", "te_ok"))
    ex_ok = sem("ex_ok")
    off = [2 * D]

    def take(*shape):
        v = view(m.R, off[0], *shape)
        off[0] += int(np.prod(shape))
        return v
    wr, br = take(KT, NE), take(1, NE)[:, 0, :]
    L, E, O1, O2, T, RK = (take(NTT, NE) for _ in range(6))
    GS, GM = take(NTT, NG), take(NTT, NG)
    A1, A2, A3 = (take(NTT, 1)[:, :, 0] for _ in range(3))
    G3 = take(NTT, NG)
    valid = take(NTT, 1)[:, :, 0]
    tri = take(1, P)[:, 0, :]
    w16, w4 = take(1, NE)[:, 0, :], take(1, NG)[:, 0, :]
    nt, start, end, zero16 = (take(1, NE)[:, 0, :] for _ in range(4))
    tmp16 = take(1, NE)[:, 0, :]
    lim = take(1, NE)[:, 0, :]
    cmp_ = take(SLOT_TILES, NE)
    cmp2 = take(SLOT_TILES, NE)
    tix, tef = take(1, SLOT_TILES)[:, 0, :], take(1, SLOT_TILES)[:, 0, :]
    toki = take(1, NTT)[:, 0, :].bitcast(I32)
    zi = take(1, SLOT_TILES)[:, 0, :].bitcast(I32)
    t_e = [P, NTT, NE]
    with nc.Block() as block:
        @block.sync
        def _(sp):
            sp.dma_start(wr, a["w_router"].rearrange("(p k) n -> p k n", k=KT)).then_inc(w_in, 16)
            sp.dma_start(br, a["b_router"].partition_broadcast(P)).then_inc(w_in, 16)
            sp.dma_start(m.lnr[:, 0, :], a["ln_ffn_g"][l].partition_broadcast(P)).then_inc(ln_in, 16)
            sp.dma_start(m.lnr[:, 1, :], a["ln_ffn_b"][l].partition_broadcast(P)).then_inc(ln_in, 16)
            sp.wait_ge(z_in, 1)
            sp.dma_start(m.idxD[l].rearrange("(p t) a -> p (t a)", p=P), zi).then_inc(z_out, 16)
            sp.wait_ge(te_ok, 1)
            load_expert(sp, m, weights[0:2], slice(0, 1), 0)
            sp.wait_ge(ln_in, 32)

        @block.gpsimd
        def _(g):
            nc.gpsimd.memset(tri, 1.0).then_inc(tri_ok, 1)
            nc.gpsimd.memset(valid, 0.0).then_inc(tri_ok, 1)
            g.wait_ge(tri_ok, 2)
            nc.gpsimd.affine_select(out=tri, in_=tri, compare_op=ALU.is_gt, fill=0.0, base=0, pattern=[[1, P]],
                                    channel_multiplier=-1).then_inc(tab, 1)
            nc.gpsimd.memset(valid[:, 0:NTT - 1], 1.0).then_inc(tab, 1)
            nc.gpsimd.memset(valid[0:NS, NTT - 1:NTT], 1.0).then_inc(tab, 1)
            nc.gpsimd.iota(w16, pattern=[[-1, NE]], base=NE, channel_multiplier=0, allow_small_or_imprecise_dtypes=True).then_inc(tab, 1)
            nc.gpsimd.iota(w4, pattern=[[-1, NG]], base=NG, channel_multiplier=0, allow_small_or_imprecise_dtypes=True).then_inc(tab, 1)
            nc.gpsimd.iota(tix, pattern=[[1, SLOT_TILES]], base=0, channel_multiplier=0,
                           allow_small_or_imprecise_dtypes=True).then_inc(tab, 1)
            nc.gpsimd.iota(toki, pattern=[[P, NTT]], base=0, channel_multiplier=1).then_inc(tab, 1)
            nc.gpsimd.memset(zi, 0).then_inc(z_in, 1)
            g.wait_ge(z_out, 16)
            g.wait_ge(dst_ok, 1)
            g.wait_ge(tab, 7)
            for c in range(2):
                for i, r in TILES:
                    g.indirect_dma_start(out=m.idxD[l], out_offset=bass.IndirectOffsetOnAxis(ap=m.dest[0:r, c, i:i + 1], axis=0),
                                         in_=toki[0:r, i:i + 1], in_offset=None).then_inc(sc_out, 16)

        @block.tensor
        def _(pe):
            pe.wait_ge(w_in, 32)
            for i, r in TILES:
                for k in range(KT):
                    last = nc.tensor.matmul(m.ps[i][0:r, 0:NE], m.xt[:, k, i * P:i * P + r], wr[:, k, :],
                                            start=(k == 0), stop=(k == KT - 1))
            last.then_inc(mm, 1)
            pe.wait_ge(sel_ok, 1)
            pe.wait_ge(tab, 7)
            for i, r in TILES:
                for j in range(i):
                    nc.tensor.matmul(m.ps[i][:, 0:NE], m.ones[:, :], T[:, j, :], start=(j == 0), stop=False)
                nc.tensor.matmul(m.ps[i][:, 0:NE], tri, T[:, i, :], start=(i == 0), stop=True)
            for j in range(NTT):
                last = nc.tensor.matmul(m.ps[5][:, 0:NE], m.ones[:, :], T[:, j, :], start=(j == 0), stop=(j == NTT - 1))
            last.then_inc(rk_mm, 1)

        @block.scalar
        def _(s):
            s.wait_ge(ev, 1)
            nc.scalar.activation(E, L, ACT.Exp).then_inc(ex_ok, 1)
            s.wait_ge(sc_out, 16 * 2 * NTT)
            with nc.allow_non_contiguous_dma(reason="slot tokens, one per partition and tile"):
                s.dma_start(m.idx[:, :], m.idxD[l].rearrange("(t p) a -> p (t a)", p=P)).then_inc(ix_in, 16)
            s.wait_ge(ix_in, 16)

        @block.vector
        def _(v):
            V = nc.vector

            def tt(out, x, y, op):
                last = V.tensor_tensor(out, x, y, op)
                v.drain()
                return last

            def bc(x):
                return x.unsqueeze(2).to_broadcast([P, NTT, x.shape[-1] if False else NE])
            V.memset(L, 0.0)
            v.wait_ge(mm, 1)
            v.wait_ge(w_in, 32)
            v.drain()
            for i, r in TILES:
                V.tensor_tensor(L[0:r, i, :], m.ps[i][0:r, 0:NE], br[0:r, :], ALU.add)
            v.drain()
            V.tensor_reduce(out=A1, in_=L, axis=AX.X, op=ALU.max)
            v.drain()
            V.tensor_tensor(L, L, bc(A1), ALU.subtract).then_inc(ev, 1)
            v.wait_ge(ex_ok, 1)
            V.tensor_reduce(out=A2, in_=E, axis=AX.X, op=ALU.add)
            v.drain()
            V.reciprocal(A2, A2)
            v.drain()
            tt(E, E, bc(A2), ALU.mult)
            e4 = E.rearrange("p i (g e) -> p i g e", e=EPG)
            pairs = [(x, y) for x in range(EPG) for y in range(x + 1, EPG)]
            for n, (x, y) in enumerate(pairs):
                tt(G3 if n else GS, e4[:, :, :, x], e4[:, :, :, y], ALU.add)
                if n:
                    tt(GS, GS, G3, ALU.max)
            v.wait_ge(tab, 7)

            def first_of(onehot, score, best, weights, n):
                V.tensor_reduce(out=best, in_=score, axis=AX.X, op=ALU.max)
                v.drain()
                tt(onehot, score, best.unsqueeze(2).to_broadcast([P, NTT, n]), ALU.is_equal)
                tt(onehot, onehot, weights.unsqueeze(1).to_broadcast([P, NTT, n]), ALU.mult)
                V.tensor_reduce(out=A3, in_=onehot, axis=AX.X, op=ALU.max)
                v.drain()
                tt(onehot, onehot, A3.unsqueeze(2).to_broadcast([P, NTT, n]), ALU.is_equal)
            first_of(GM, GS, A1, w4, NG)
            tt(E.rearrange("p i (g e) -> p i g e", e=EPG), e4, GM.unsqueeze(3).to_broadcast([P, NTT, NG, EPG]), ALU.mult)
            tt(E.rearrange("p i (g e) -> p i g e", e=EPG), e4, GM.unsqueeze(3).to_broadcast([P, NTT, NG, EPG]), ALU.add)
            V.tensor_scalar(E, E, -1.0, None, ALU.add)
            v.drain()
            first_of(O1, E, A1, w16, NE)
            V.scalar_tensor_tensor(out=E, in0=O1, scalar=-4.0, in1=E, op0=ALU.mult, op1=ALU.add)
            v.drain()
            first_of(O2, E, A2, w16, NE)
            tt(A3, A1, A2, ALU.add)
            V.reciprocal(A3, A3)
            v.drain()
            tt(m.wts[:, 0, :], A1, A3, ALU.mult)
            tt(m.wts[:, 1, :], A2, A3, ALU.mult)
            tt(O1, O1, bc(valid), ALU.mult)
            tt(O2, O2, bc(valid), ALU.mult)
            V.tensor_tensor(T, O1, O2, ALU.add).then_inc(sel_ok, 1)
            v.wait_ge(rk_mm, 1)
            V.tensor_scalar(nt, m.ps[5][:, 0:NE], 0.0, None, ALU.is_gt)
            v.drain()
            for c in range(1, NTT):
                V.tensor_scalar(tmp16, m.ps[5][:, 0:NE], float(c * P), None, ALU.is_gt)
                v.drain()
                tt(nt, nt, tmp16, ALU.add)
            V.memset(zero16, 1.0)
            v.drain()
            V.tensor_tensor_scan(end, zero16, nt, 0.0, ALU.mult, ALU.add)
            v.drain()
            tt(start, end, nt, ALU.subtract)
            V.tensor_scalar(start, start, float(P), None, ALU.mult)
            v.drain()
            for i in range(NTT):
                V.tensor_tensor(RK[:, i, :], m.ps[i][:, 0:NE], start, ALU.add)
            v.drain()
            for c, O in enumerate((O1, O2)):
                tt(O, O, RK, ALU.mult)
                V.tensor_reduce(out=A1, in_=O, axis=AX.X, op=ALU.add)
                v.drain()
                V.tensor_copy(m.dest[:, c, :], A1).then_inc(rk2, 1)
                v.drain()
            v.nop().then_inc(dst_ok, 1)
            tt(cmp_, end.unsqueeze(1).to_broadcast([P, SLOT_TILES, NE]), tix.unsqueeze(2).to_broadcast([P, SLOT_TILES, NE]), ALU.is_le)
            V.tensor_reduce(out=tef, in_=cmp_, axis=AX.X, op=ALU.add)
            v.drain()
            V.tensor_scalar(tef, tef, float(NE - 1), None, ALU.min)
            v.drain()
            V.tensor_copy(m.texp[0:1, 0:SLOT_TILES], tef[0:1, :])
            V.tensor_tensor(lim, start, m.ps[5][:, 0:NE], ALU.add)
            v.drain()
            V.tensor_scalar(start, start, 1.0 / P, None, ALU.mult)
            V.tensor_scalar(lim, lim, 1.0 / P, -0.5, ALU.mult, ALU.add)
            v.drain()
            tt(cmp_, start.unsqueeze(1).to_broadcast([P, SLOT_TILES, NE]), tix.unsqueeze(2).to_broadcast([P, SLOT_TILES, NE]), ALU.is_le)
            tt(cmp2, lim.unsqueeze(1).to_broadcast([P, SLOT_TILES, NE]), tix.unsqueeze(2).to_broadcast([P, SLOT_TILES, NE]), ALU.is_gt)
            tt(cmp_, cmp_, cmp2, ALU.mult)
            V.tensor_reduce(out=tef, in_=cmp_, axis=AX.X, op=ALU.add)
            v.drain()
            V.tensor_copy(m.full[0:1, :], tef[0:1, :])
            v.drain()
            half = SLOT_TILES // 2
            V.tensor_scalar(tef[0:1, 0:half], tix[0:1, 0:SLOT_TILES:2], end[0:1, NE - 1:NE], None, ALU.is_lt)
            v.drain()
            V.tensor_reduce(out=tmp16[0:1, 0:1], in_=tef[0:1, 0:half], axis=AX.X, op=ALU.add)
            v.drain()
            V.tensor_scalar(m.texp[0:1, SLOT_TILES:SLOT_TILES + 1], tmp16[0:1, 0:1], float(-MIN_PAIRS), None, ALU.add).then_inc(te_ok, 1)


def stage_experts(nc, ctx, m, l, weights):
    sem = lambda n: ctx.enter_context(m_semaphore(nc, f"moe{l}_{n}"))
    x_in, y_out = ([sem(f"{n}{u}") for u in range(2)] for n in ("x_in", "y_out"))
    x_tr, x_cp, gu_mm, zeroed, e_ok, h_ok, h_tr, h_cp, d_mm, y_v, y_s = (sem(n) for n in
        ("x_tr", "x_cp", "gu_mm", "zeroed", "e_ok", "h_ok", "h_tr", "h_cp", "d_mm", "y_v", "y_s"))
    NT = SLOT_TILES
    FT = FF // P
    wg, wu, wd = (buf for _, buf, _, _, _ in weights)
    wg_in, wu_in, wd_in = (loaded for _, _, _, loaded, _ in weights)
    xg = [m.R[:, u * D:(u + 1) * D] for u in range(2)]
    xgt = [view(m.R, 2 * D + u * D, KT, P) for u in range(2)]
    ys = [m.R[:, (4 + u) * D:(5 + u) * D] for u in range(2)]
    es = [m.R[:, 6 * D + u * FF:6 * D + (u + 1) * FF] for u in range(2)]
    hs = [m.R[:, 7 * D + u * FF:7 * D + (u + 1) * FF] for u in range(2)]
    ht = [view(m.R, 8 * D + u * FF, FT, P) for u in range(2)]
    ixc = [m.small[:, 504 + u:505 + u].bitcast(I32) for u in range(2)]
    pst = [m.ps[0], m.ps[1]]
    psg, psu, psh, psy = m.ps[2], m.ps[3], m.ps[4], [m.ps[5], m.ps[6]]

    def tiles(eng, step):
        pairs = eng.value_load(m.texp[0:1, NT:NT + 1], min_val=0, max_val=NT // 2 - MIN_PAIRS) + MIN_PAIRS
        for t in range(4):
            step(t // 2, t % 2, t)
        with eng.Fori(2, pairs - 1) as i:
            for u in range(2):
                step(i, u, None)
        step(pairs - 1, 0, None)
        step(pairs - 1, 1, LAST)
        return pairs

    with nc.Block() as block:
        @block.sync
        def _(sp):
            def step(i, u, t):
                if t == 0:
                    load_expert(sp, m, weights[2:3], slice(0, 1), 0)
                elif t == 1:
                    load_expert(sp, m, weights, slice(1, 2), 1)
                else:
                    load_expert(sp, m, weights, bass.ds(2 * i + u, 1), u,
                                {"gate": (gu_mm, 4 * i + (2 * u - 2)), "up": (gu_mm, 4 * i + (2 * u - 2)),
                                 "down": (d_mm, 4 * i + (2 * u - 2))})
            tiles(sp, step)

        @block.gpsimd
        def _(g):
            def step(i, u, t):
                if t is None or t >= 2:
                    g.wait_ge(x_tr, 2 * i + u - 1)
                nc.gpsimd.tensor_copy(ixc[u], m.idx[:, bass.ds(2 * i + u, 1)])
                g.drain()
                g.indirect_dma_start(out=xg[u], out_offset=None, in_=m.xmD,
                                     in_offset=bass.IndirectOffsetOnAxis(ap=ixc[u], axis=0)).then_inc(x_in[u], 16)
            pairs = tiles(g, step)
            for u in range(2):
                g.wait_ge(y_out[u], 16 * pairs)

        @block.tensor
        def _(pe):
            def x_transpose(i, u, first):
                pe.wait_ge(x_in[u], 16 * i + 16)
                if not first:
                    pe.wait_ge(x_cp, 2 * i + u)
                for k in range(KT):
                    last = nc.tensor.transpose(pst[k // 4][:, (k % 4) * P:(k % 4 + 1) * P],
                                               xg[u].rearrange("t (p k) -> t k p", k=KT)[:, k, :], m.ident[:, :])
                last.then_inc(x_tr, 1)

            def h_transpose(u, n):
                pe.wait_ge(h_ok, n + 1)
                wait(pe, h_cp, n)
                for k in range(FT):
                    last = nc.tensor.transpose(psh[:, k * P:(k + 1) * P],
                                               hs[u].rearrange("t (p k) -> t k p", k=FT)[:, k, :], m.ident[:, :])
                last.then_inc(h_tr, 1)

            def both_halves(done, full, product):
                product(0).then_inc(done, 1)
                with pe.If_ne(full.val, 0):
                    product(1).then_inc(done, 1)
                with pe.Else():
                    pe.nop().then_inc(done, 1)

            def is_full(tile):
                return pe.value_load(m.full[0:1, tile], min_val=0, max_val=1)

            def down(u, n, wd_value, full):
                pe.wait_ge(h_cp, n + 1)
                pe.wait_ge(wd_in[u], wd_value)
                wait(pe, y_v, n)
                wait(pe, y_s, n)

                def product(a):
                    for k in range(FT):
                        for c in range(2):
                            at = 64 * (a if c == 0 else 1 - a)
                            last = nc.tensor.matmul(psy[c][at:at + 64, :], ht[u][:, k, 64 * (1 - a):64 * (2 - a)],
                                                    wd[u][:, k, c * 512:(c + 1) * 512],
                                                    start=(k == 0), stop=(k == FT - 1), tile_position=(0, at))
                    return last
                both_halves(d_mm, full, product)

            def step(i, u, t):
                n = 2 * i + u
                full = is_full(bass.ds(n, 1))
                pe.wait_ge(x_cp, n + 1)
                pe.wait_ge(wg_in[u], 16 * i + 16)
                pe.wait_ge(wu_in[u], 16 * i + 16)
                wait(pe, e_ok, n)
                wait(pe, h_ok, n)

                def product(a):
                    for k in range(KT):
                        for ps, w, at in ((psg, wg, 64 * a), (psu, wu, 64 * (1 - a))):
                            last = nc.tensor.matmul(ps[at:at + 64, :], xgt[u][:, k, 64 * a:64 * (a + 1)], w[u][:, k, :],
                                                    start=(k == 0), stop=(k == KT - 1), tile_position=(0, at))
                    return last
                both_halves(gu_mm, full, product)
                if t != 0:
                    full = is_full(bass.ds(n - 1, 1))
                    h_transpose(1 - u, n - 1)
                if t != LAST:
                    x_transpose(i + u, 1 - u, False)
                if t != 0:
                    down(1 - u, n - 1, 16 * i + 16 * u, full)
            pe.wait_ge(zeroed, 1)
            x_transpose(0, 0, True)
            pairs = tiles(pe, step)
            full = is_full(bass.ds(2 * pairs - 1, 1))
            h_transpose(1, 2 * pairs - 1)
            down(1, 2 * pairs - 1, 16 * pairs, full)

        @block.scalar
        def _(s):
            def x_copy(u, n):
                s.wait_ge(x_tr, n + 1)
                wait(s, gu_mm, 2 * n - 2)
                for c in range(2):
                    last = nc.scalar.copy(xgt[u][:, 4 * c:4 * c + 4, :], pst[c][:, :].rearrange("p (k t) -> p k t", t=P))
                last.then_inc(x_cp, 1)

            def h_copy(u, n):
                s.wait_ge(h_tr, n + 1)
                wait(s, d_mm, 2 * n - 2)
                nc.scalar.copy(ht[u], psh[:, :].rearrange("p (k t) -> p k t", t=P)).then_inc(h_cp, 1)

            def y_store(u, n, done):
                s.wait_ge(d_mm, 2 * n + 2)
                wait(s, y_out[u], done)
                nc.scalar.copy(ys[u][0:64, 512:1024], psy[1][64:128, :])
                nc.scalar.copy(ys[u][64:128, 512:1024], psy[1][0:64, :]).then_inc(y_s, 1)
                s.wait_ge(y_s, n + 1)
                s.wait_ge(y_v, n + 1)
                s.dma_start(m.yD[bass.ds(n * P, P), :], ys[u]).then_inc(y_out[u], 16)

            def step(i, u, t):
                n = 2 * i + u
                s.wait_ge(gu_mm, 2 * n + 2)
                if t is None or t >= 2:
                    s.wait_ge(h_ok, n - 1)
                nc.scalar.activation(es[u][64:128, :], psg[0:64, :], ACT.Silu)
                nc.scalar.activation(es[u][0:64, :], psg[64:128, :], ACT.Silu).then_inc(e_ok, 1)
                if t != 0:
                    h_copy(1 - u, n - 1)
                if t != LAST:
                    x_copy(1 - u, n + 1)
                if t != 0:
                    y_store(1 - u, n - 1, 16 * (i + u - 1))
            x_copy(0, 0)
            pairs = tiles(s, step)
            h_copy(1, 2 * pairs - 1)
            y_store(1, 2 * pairs - 1, 16 * (pairs - 1))

        @block.vector
        def _(v):
            V = nc.vector
            for bank in (psg, psu, *psy):
                last = V.memset(bank[:, :], 0.0)
            last.then_inc(zeroed, 1)

            def y_copy(u, n, done):
                v.wait_ge(d_mm, 2 * n + 2)
                wait(v, y_out[u], done)
                V.tensor_copy(ys[u][:, 0:512], psy[0][:, :]).then_inc(y_v, 1)

            def step(i, u, t):
                n = 2 * i + u
                v.wait_ge(e_ok, n + 1)
                if t is None or t >= 2:
                    v.wait_ge(h_tr, n - 1)
                V.tensor_tensor(hs[u], es[u], psu[:, :], ALU.mult).then_inc(h_ok, 1)
                if t != 0:
                    y_copy(1 - u, n - 1, 16 * (i + u - 1))
            pairs = tiles(v, step)
            y_copy(1, 2 * pairs - 1, 16 * (pairs - 1))


def stage_combine(nc, ctx, m, l, stores=None):
    sem = lambda n: ctx.enter_context(m_semaphore(nc, f"comb{l}_{n}"))
    y_in = [sem(f"y_in{u}") for u in range(2)]
    w_ok, f_ok, out = sem("w_ok"), sem("f_ok"), sem("stored")
    y = [[m.R[:, (2 * u + c) * D:(2 * u + c + 1) * D] for c in range(2)] for u in range(2)]
    ln = LayerNorm(nc, ctx, m, f"comb{l}")
    with nc.Block() as block:
        @block.gpsimd
        def _(g):
            for i, r in TILES:
                if i >= 2:
                    g.wait_ge(f_ok, i - 1)
                for c in range(2):
                    g.indirect_dma_start(out=y[i % 2][c][0:r, :], out_offset=None, in_=m.yD,
                                         in_offset=bass.IndirectOffsetOnAxis(ap=m.dest[0:r, c, i:i + 1], axis=0)
                                         ).then_inc(y_in[i % 2], 16)

        @block.vector
        def _(v):
            nc.vector.memset(m.small[:, 501:502], LN_EPS).then_inc(w_ok, 1)
            for i, r in TILES:
                v.wait_ge(y_in[i % 2], 32 * (i // 2 + 1))
                y1, y2 = y[i % 2]
                nc.vector.tensor_scalar(y1[0:r, :], y1[0:r, :], m.wts[0:r, 0, i:i + 1], None, ALU.mult)
                v.drain()
                nc.vector.scalar_tensor_tensor(out=y1[0:r, :], in0=y2[0:r, :], scalar=m.wts[0:r, 1, i:i + 1],
                                               in1=y1[0:r, :], op0=ALU.mult, op1=ALU.add)
                v.drain()
                ln.mixed(v, i, r, [y1[:, 0:512], y1[:, 512:1024]]).then_inc(f_ok, 1)
                ln.stats(v, i, r)
                if i:
                    ln.shift(v, *TILES[i - 1])
            ln.shift(v, *TILES[-1])

        @block.scalar
        def _(s):
            s.wait_ge(w_ok, 1)
            for i, r in TILES:
                ln.scalar(s, i, r)

        @block.sync
        def _(sp):
            if stores is not None:
                for i, r in TILES:
                    sp.wait_ge(ln.done, i + 1)
                    dst = (stores[0].rearrange("b t n -> (b t) n")[i * P:(i + 1) * P, :] if i < NTT - 1
                           else stores[1].rearrange("b s n -> (b s) n"))
                    sp.dma_start(dst, m.x[0:r, i, :]).then_inc(out, 16)
                sp.wait_ge(out, 16 * NTT)


def stage_ln_rows(nc, ctx, m, name, g, b):
    s_in = ctx.enter_context(m_semaphore(nc, f"{name}_in"))
    with nc.Block() as block:
        @block.sync
        def _(sp):
            sp.dma_start(m.lnr[:, 0, :], g.partition_broadcast(P)).then_inc(s_in, 16)
            sp.dma_start(m.lnr[:, 1, :], b.partition_broadcast(P)).then_inc(s_in, 16)
            sp.wait_ge(s_in, 32)


def stage_shared_kv(nc, ctx, m, a, ahead):
    sem = lambda n: ctx.enter_context(m_semaphore(nc, f"kv_{n}"))
    w_in = [loaded for _, _, loaded in ahead]
    mm, ev, out = sem("mm"), sem("ev"), sem("stored")
    sh_mm, sh_cp, sm_mm, sm_ev = (sem(n) for n in ("sh_mm", "sh_cp", "sm_mm", "sm_ev"))
    shares = m.R[:, 6144:6656]
    m.kk = view(m.W, 13312, NTT, D)
    m.vv = view(m.W, 18432, NTT, D)
    w_src = a["w_kv"].rearrange("(p k) n -> p k n", k=KT)
    with nc.Block() as block:
        @block.sync
        def _(sp):
            for c in range(2, 4):
                sp.wait_ge(mm, (NTT - 1) * (c - 1))
                sp.dma_start(m.wr[c % 2], w_src[:, :, c * 512:(c + 1) * 512]).then_inc(w_in[c % 2], 16)
            for j, (t, name) in enumerate(((m.kk, "k"), (m.vv, "v"))):
                sp.wait_ge(ev, 2 * (NTT - 1) * (j + 1))
                sp.wait_ge(sm_ev, 2 * (j + 1))
                sp.dma_start(a[f"{name}_prompt"].rearrange("b g p h d -> p (b g) (h d)"), t[:, 0:NTT - 1, :]).then_inc(out, 16)
                sp.dma_start(a[f"{name}_sample"].rearrange("b s h d -> (b s) (h d)"), t[0:NS, NTT - 1, :]).then_inc(out, 16)
                sp.dma_start(m.newD[j], t[0:NS, NTT - 1, :]).then_inc(out, 16)
            sp.wait_ge(out, 96)

        @block.tensor
        def _(pe):
            for c in range(4):
                pe.wait_ge(w_in[c % 2], 16 * (c // 2 + 1))
                wait(pe, sh_cp, c)
                sample_parts(nc, m, m.ps[0], m.xt[:, :, SEQ:SEQ + 32], m.wr[c % 2]).then_inc(sh_mm, 1)
                for i in range(NTT - 1):
                    n = c * (NTT - 1) + i
                    wait(pe, ev, n - 3)
                    for k in range(KT):
                        last = nc.tensor.matmul(m.ps[4 + n % 4][:, :], m.xt[:, k, i * P:(i + 1) * P],
                                                m.wr[c % 2][:, k, :], start=(k == 0), stop=(k == KT - 1))
                    last.then_inc(mm, 1)
                pe.wait_ge(sh_cp, c + 1)
                wait(pe, sm_ev, c)
                sample_sum(nc, m, m.ps[1], shares).then_inc(sm_mm, 1)

        @block.scalar
        def _(s):
            for c in range(4):
                s.wait_ge(sh_mm, c + 1)
                wait(s, sm_mm, c)
                nc.scalar.copy(shares, m.ps[0][:, :]).then_inc(sh_cp, 1)
                s.wait_ge(sm_mm, c + 1)
                nc.scalar.copy((m.kk, m.vv)[c // 2][0:NS, NTT - 1, (c % 2) * 512:(c % 2 + 1) * 512],
                               m.ps[1][0:NS, :]).then_inc(sm_ev, 1)

        @block.vector
        def _(v):
            for c in range(4):
                for i in range(NTT - 1):
                    n = c * (NTT - 1) + i
                    v.wait_ge(mm, n + 1)
                    nc.vector.tensor_copy((m.kk, m.vv)[c // 2][:, i, (c % 2) * 512:(c % 2 + 1) * 512],
                                          m.ps[4 + n % 4][:, :]).then_inc(ev, 1)


def stage_queries(nc, ctx, m, a, ahead):
    sem = lambda n: ctx.enter_context(m_semaphore(nc, f"q_{n}"))
    w_in = [loaded for _, _, loaded in ahead]
    mm, ev, smm, sev, qs_out, l_in, l_sum, l_exp, l_row, l_mm, tab0, tab1, tab2, tab3 = (sem(n) for n in
        ("mm", "ev", "smm", "sev", "qs_out", "l_in", "l_sum", "l_exp", "l_row", "l_mm", "tab0", "tab1", "tab2", "tab3"))
    m.qt = view(m.R, 0, HB, SEQ)
    m.dist = m.R[:, 4096:4608]
    m.slope = m.small[:, 16:16 + HB]
    m.lam = m.small[:, 32:33]
    m.coef = m.small[:, 33:34]
    sh_mm, sh_cp = sem("sh_mm"), sem("sh_cp")
    shares = m.R[:, 7168:7680]
    qs = m.R[0:NS, 5120:6144]
    lrow = m.R[0:1, 6144:6400]
    lprod = m.R[0:1, 6400:6528]
    lsum = m.R[0:1, 6528:6530]
    lam1 = m.R[0:1, 6530:6531]
    odd8 = m.R[:, 6600:6664]
    odd1 = m.R[:, 6664:6665]
    with nc.Block() as block:
        @block.sync
        def _(sp):
            for n, name in enumerate(("lam_q1", "lam_q2", "lam_k1", "lam_k2")):
                sp.dma_start(lrow[:, n * DHB:(n + 1) * DHB], a[name]).then_inc(l_in, 16)
            sp.wait_ge(sev, 2)
            sp.dma_start(m.qsD, qs).then_inc(qs_out, 16)
            sp.wait_ge(qs_out, 16)

        @block.gpsimd
        def _(g):
            nc.gpsimd.iota(m.dist, pattern=[[1, SEQ]], base=P - SEQ, channel_multiplier=-1,
                           allow_small_or_imprecise_dtypes=True).then_inc(tab0, 1)
            g.wait_ge(tab0, 1)
            nc.gpsimd.affine_select(out=m.dist, in_=m.dist, compare_op=ALU.is_ge, fill=NEG, base=SEQ - P,
                                    pattern=[[-1, SEQ]], channel_multiplier=1).then_inc(tab1, 1)
            for h in range(HB):
                nc.gpsimd.memset(m.slope[:, h:h + 1], 2.0 ** (-8.0 * (h + 1) / HB)).then_inc(tab1, 1)
            nc.gpsimd.memset(odd8, 0.0).then_inc(tab2, 1)
            g.wait_ge(tab2, 1)
            nc.gpsimd.affine_select(out=odd8, in_=odd8, compare_op=ALU.not_equal, fill=1.0, base=-1,
                                    pattern=[[-2, P // 2]], channel_multiplier=1).then_inc(tab3, 1)

        @block.tensor
        def _(pe):
            for c in range(2):
                pe.wait_ge(w_in[c], 16)
                for j in range(4):
                    n = 4 * c + j
                    wait(pe, ev, n - 1)
                    for k in range(KT):
                        last = nc.tensor.matmul(m.ps[n % 2][:, :], m.wr[c][:, k, j * P:(j + 1) * P], m.xt[:, k, 0:SEQ],
                                                start=(k == 0), stop=(k == KT - 1))
                    last.then_inc(mm, 1)
                wait(pe, sh_cp, c)
                sample_parts(nc, m, m.ps[5], m.xt[:, :, SEQ:SEQ + 32], m.wr[c]).then_inc(sh_mm, 1)
                pe.wait_ge(sh_cp, c + 1)
                sample_sum(nc, m, m.ps[2 + c], shares).then_inc(smm, 1)
            pe.wait_ge(l_row, 1)
            nc.tensor.matmul(m.ps[4][:, 0:1], m.ones[0:1, :], lam1, start=True, stop=True).then_inc(l_mm, 1)

        @block.scalar
        def _(s):
            for n in range(HB):
                s.wait_ge(mm, n + 1)
                nc.scalar.activation(m.qt[:, n, :], m.ps[n % 2][:, :], ACT.Copy, scale=DHB ** -0.5).then_inc(ev, 1)
            for c in range(2):
                s.wait_ge(smm, c + 1)
                nc.scalar.activation(qs[:, c * 512:(c + 1) * 512], m.ps[2 + c][0:NS, :], ACT.Copy,
                                     scale=DHB ** -0.5).then_inc(sev, 1)
            s.wait_ge(l_sum, 1)
            nc.scalar.activation(lsum, lsum, ACT.Exp).then_inc(l_exp, 1)

        @block.vector
        def _(v):
            for c in range(2):
                v.wait_ge(sh_mm, c + 1)
                wait(v, smm, c)
                nc.vector.tensor_copy(shares, m.ps[5][:, :]).then_inc(sh_cp, 1)
            v.wait_ge(l_in, 64)
            nc.vector.tensor_tensor(lprod, lrow[:, 0:2 * DHB], lrow[:, 2 * DHB:4 * DHB], ALU.mult)
            v.drain()
            nc.vector.tensor_reduce(out=lsum, in_=lprod.rearrange("p (a b) -> p a b", b=DHB), axis=AX.X, op=ALU.add).then_inc(l_sum, 1)
            v.wait_ge(l_exp, 1)
            nc.vector.tensor_tensor(lam1, lsum[:, 0:1], lsum[:, 1:2], ALU.subtract)
            v.drain()
            nc.vector.tensor_scalar(lam1, lam1, LAM_INIT, None, ALU.add).then_inc(l_row, 1)
            v.wait_ge(l_mm, 1)
            nc.vector.tensor_copy(m.lam, m.ps[4][:, 0:1])
            v.wait_ge(tab3, 1)
            nc.vector.tensor_reduce(out=odd1, in_=odd8, axis=AX.X, op=ALU.add)
            v.drain()
            nc.vector.tensor_tensor(m.coef, odd1, m.lam, ALU.mult)
            v.drain()
            nc.vector.tensor_tensor(m.coef, m.coef, odd1, ALU.add)
            v.drain()
            nc.vector.tensor_scalar(m.coef, m.coef, -1.0, 1.0, ALU.mult, ALU.add)


def stage_attention(nc, ctx, m, a):
    sem = lambda n: ctx.enter_context(m_semaphore(nc, f"at_{n}"))
    kr_ok, k_tr, kt_ok, sc_mm, sb_ok, nb_ok, p_ok, c_ok, c_tr, c_cp, o_mm, o_ev = (sem(n) for n in
        ("kr_ok", "k_tr", "kt_ok", "sc_mm", "sb_ok", "nb_ok", "p_ok", "c_ok", "c_tr", "c_cp", "o_mm", "o_ev"))
    RING, GRP = 8, 4
    VG = PAGES // 2
    k_in = [sem(f"k_in{u}") for u in range(RING)]
    v_in = [sem(f"v_in{u}") for u in range(2)]
    q_in, kn_in, vn_in, pt_in, o_out, os_in, z_ok, t0, t1, t2 = (sem(n) for n in
        ("q_in", "kn_in", "vn_in", "pt_in", "o_out", "os_in", "z_ok", "t0", "t1", "t2"))
    dp_ok, pp_ok = sem("dp_ok"), sem("pp_ok")
    ks_ok, mx_ok, mx_tr, mr_ok, mb_mm, sh_ok, e_ok, l_ok, l_mm, l_ev, pv_mm, om_ok, or_mm, or_ev = (sem(n) for n in
        ("ks_ok", "mx_ok", "mx_tr", "mr_ok", "mb_mm", "sh_ok", "e_ok", "l_ok", "l_mm", "l_ev", "pv_mm", "om_ok",
         "or_mm", "or_ev"))
    NQ = SEQ // P
    C, CP = 2 * HB, 32
    NP = PAGES + 1
    base = 4608
    khr = view(m.R, base, NQ, P)
    qh = m.R[:, base + 512:base + 1024]
    kth = m.R[:, base + 1024:base + 1536]
    SP = [[m.R[:, base + 2080 + 512 * (2 * u + j):base + 2080 + 512 * (2 * u + j + 1)] for j in range(2)] for u in range(2)]
    ct = [m.R[:, base + 4128 + 512 * u:base + 4128 + 512 * (u + 1)] for u in range(2)]
    mx = [m.small[:, 40 + 2 * u:42 + 2 * u] for u in range(2)]
    ls = [m.small[:, 44 + 2 * u:46 + 2 * u] for u in range(2)]
    r1 = [m.small[:, 48 + i:49 + i] for i in range(NQ)]
    lm = m.small[:, 52:53]
    kp = [m.W[:, u * D:(u + 1) * D] for u in range(4)] + [m.lnr[:, 0, :], m.lnr[:, 1, :],
                                                        m.kk[:, NTT - 1, :], m.vv[:, NTT - 1, :]]
    vp = [m.W[:, (4 + u) * D:(5 + u) * D] for u in range(4)]
    xtf = m.xt[:, :, :].rearrange("p k t -> p (k t)")
    qb, kn = xtf[:, 0:D], xtf[:, D:2 * D]
    v_prod, g_prod = xtf[:, 2 * D:3 * D], [xtf[:, 3 * D:4 * D], m.v[:, NTT - 1, :]]
    g_pages = [j for j in range(PAGES) if j % 4]
    NV, NPOOL = NP - len(g_pages), len(g_pages)
    vn, bmask, om = m.mod[:, 0, 0, :], m.mod[:, 0, 1, :], m.mod[:, 1, 0, :]
    orow = m.mod[0:1, 1, 1, :]
    o1 = 23552
    S, BT = (view(m.W, o1 + j * NP * C, NP, C) for j in range(2))
    m1 = m.W[:, o1 + 2 * NP * C:o1 + 2 * NP * C + C]
    mr = m.W[0:C, o1 + 560:o1 + 561]
    cf = m.W[:, o1 + 561:o1 + 562]
    dg = m.W[0:C, o1 + 562:o1 + 562 + C]
    nd = m.W[:, o1 + 580:o1 + 580 + PAGES]
    lw = m.W[:, o1 + 600:o1 + 600 + GRP * CP].rearrange("p (g c) -> p g c", c=CP)
    lsum = m.W[:, o1 + 730:o1 + 730 + C]
    PR = view(m.R, base + 1536, NP, CP)
    pt = m.small[0:1, 128:128 + NS * PAGES].bitcast(I32)
    ks = a["cache_k"].rearrange("g p h d -> g p (h d)")
    vs = a["cache_v"].rearrange("g p h d -> g p (h d)")
    KT_B, SC_B, CT_B, O_B, PSO, MISC = m.ps[0], [m.ps[1], m.ps[2]], m.ps[3], m.ps[4], [m.ps[5], m.ps[6]], m.ps[7]

    def seqs(eng, body):
        body(0)
        body(1)
        with eng.Fori(2, NS - 1) as b:
            body(b)
        body(NS - 1)

    with nc.Block() as block:
        @block.sync
        def _(sp):
            sp.dma_start(pt, a["page_table"].rearrange("b j -> (b j)").unsqueeze(0)).then_inc(pt_in, 16)
            sp.wait_ge(pt_in, 16)

            def load_values(b, p):
                if isinstance(b, int) and b < 0:
                    return
                last_seq = isinstance(b, int) and b == NS - 1
                in_key_ring = last_seq and 2 <= p < 2 + RING // 2
                pages = [sp.value_load(pt[0:1, bass.ds(b * PAGES + 2 * p + g, 1)], min_val=0, max_val=ks.shape[0] - 1)
                         for g in range(2)]
                if last_seq and p >= 2 + RING // 2:
                    sp.wait_ge(pv_mm, VG * b + p % 2 + 1)
                elif not in_key_ring and not (isinstance(b, int) and VG * b + p < 2):
                    sp.wait_ge(pv_mm, VG * b + p - 1)
                for g, page in enumerate(pages):
                    buf, loaded = vp[2 * (p % 2) + g], v_in[p % 2]
                    if in_key_ring:
                        n = 2 * p - 4 + g
                        buf, loaded = kp[n], k_in[n]
                        sp.wait_ge(ks_ok, NP * b + PAGES - RING + n + 1)
                    sp.dma_start(buf, vs[bass.ds(page, 1)].rearrange("g p n -> p (g n)")).then_inc(loaded, 16)
                if p == (6 if last_seq else 2):
                    sp.dma_start(vn[0:1, :], m.newD[1][bass.ds(b, 1), :]).then_inc(vn_in, 16)

            LAG = 5

            def body(b):
                first = isinstance(b, int) and b == 0
                for j in range(PAGES):
                    page = sp.value_load(pt[0:1, bass.ds(b * PAGES + j, 1)], min_val=0, max_val=ks.shape[0] - 1)
                    if j >= RING:
                        wait(sp, ks_ok, NP * b + j - RING + 1)
                    elif not first:
                        sp.wait_ge(ks_ok, NP * b + (j - RING))
                    if j == (0 if first else RING - 1):
                        sp.dma_start(qb, m.qsD[bass.ds(b, 1), :].to_broadcast([P, D])).then_inc(q_in, 16)
                        if first:
                            sp.wait_ge(z_ok, 4)
                        sp.dma_start(kn[0:1, :], m.newD[0][bass.ds(b, 1), :]).then_inc(kn_in, 16)
                    sp.dma_start(kp[j % RING], ks[bass.ds(page, 1)].rearrange("g p n -> p (g n)")).then_inc(k_in[j % RING], 16)
                    if j % 2:
                        p = (j - LAG) // 2
                        load_values(b - 1 if p >= 0 else b - 2, p % VG)
            seqs(sp, body)
            for p in range(VG - (LAG - 1) // 2, 2 * VG):
                load_values(NS - 2 + p // VG, p % VG)
            sp.wait_ge(o_out, 16 * NS)
            sp.dma_start(m.v[0:NS, NTT - 1, :], m.osD).then_inc(os_in, 16)
            sp.wait_ge(os_in, 16)

        @block.gpsimd
        def _(g):
            G = nc.gpsimd
            G.memset(kn, 0.0).then_inc(z_ok, 1)
            G.memset(vn, 0.0).then_inc(z_ok, 1)
            G.memset(PR, 0.0).then_inc(z_ok, 1)
            G.memset(lw, 1.0).then_inc(z_ok, 1)
            G.memset(bmask, 1.0).then_inc(t0, 1)
            G.iota(nd, pattern=[[P, PAGES]], base=-PAST, channel_multiplier=1, allow_small_or_imprecise_dtypes=True).then_inc(t0, 1)
            G.memset(BT[:, PAGES:NP, :], 0.0).then_inc(t0, 1)
            g.wait_ge(t0, 3)
            G.affine_select(out=BT[:, PAGES:NP, :], in_=BT[:, PAGES:NP, :], compare_op=ALU.is_ge, fill=NEG, base=0,
                            pattern=[[0, 1], [0, C]], channel_multiplier=-1).then_inc(t1, 1)
            for n in range(GRP):
                b3 = bmask[n * CP:(n + 1) * CP, :].rearrange("r (h d) -> r h d", d=DVB)
                G.affine_select(out=b3, in_=b3, compare_op=ALU.is_ge, fill=0.0, base=0, pattern=[[-2, HB], [0, DVB]],
                                channel_multiplier=1).then_inc(t1, 1)
                g.wait_ge(t1, 2 * n + 2)
                G.affine_select(out=b3, in_=b3, compare_op=ALU.is_ge, fill=0.0, base=1, pattern=[[2, HB], [0, DVB]],
                                channel_multiplier=-1).then_inc(t1, 1)
                g.wait_ge(t1, 2 * n + 3)

            def body(b):
                g.wait_ge(q_in, 16 * b + 16)
                for n, j in enumerate(g_pages):
                    g.wait_ge(k_in[j % RING], 16 * (PAGES // RING) * b + 16 * (j // RING + 1))
                    wait(g, ks_ok, NP * b + (g_pages[n - 2] + 1 - (NP if n < 2 else 0)))
                    G.tensor_tensor(g_prod[n % 2], kp[j % RING], qb, ALU.mult).then_inc(pp_ok, 1)
            seqs(g, body)

        @block.tensor
        def _(pe):
            def k_transpose(h):
                pe.wait_ge(kr_ok, h + 1)
                wait(pe, kt_ok, h)
                for j in range(NQ):
                    last = nc.tensor.transpose(KT_B[:, j * P:(j + 1) * P], khr[:, j, :], m.ident[:, :])
                last.then_inc(k_tr, 1)

            def finish(u, i, h):
                pe.wait_ge(c_ok, u + 1)
                wait(pe, c_cp, u)
                for j in range(i + 1):
                    last = nc.tensor.transpose(CT_B[:, j * P:(j + 1) * P], SP[i % 2][0][:, j * P:(j + 1) * P], m.ident[:, :])
                last.then_inc(c_tr, 1)
                pe.wait_ge(c_cp, u + 1)
                wait(pe, o_ev, u)
                for j in range(i + 1):
                    last = nc.tensor.matmul(O_B[:, (i % 2) * DVB:(i % 2 + 1) * DVB], ct[i % 2][:, j * P:(j + 1) * P],
                                            m.vv[:, j, bass.ds(h * DVB, DVB)], start=(j == 0), stop=(j == i))
                last.then_inc(o_mm, 1)

            def values(b, p):
                half = p % 2
                if p == 0:
                    pe.wait_ge(e_ok, b + 1)
                    wait(pe, om_ok, b)
                bufs = vp[2 * half:2 * half + 2]
                if isinstance(b, int) and b == NS - 1 and 2 <= p < 2 + RING // 2:
                    bufs = kp[2 * p - 4:2 * p - 2]
                    for n in (2 * p - 4, 2 * p - 3):
                        pe.wait_ge(k_in[n], 16 * (PAGES // RING) * NS + 16)
                elif isinstance(b, int) and b == NS - 1 and p >= 2:
                    pe.wait_ge(v_in[half], 32 * (VG // 2 * b + 2))
                else:
                    pe.wait_ge(v_in[half], 32 * (VG // 2 * b + p // 2 + 1))
                for n in range(2):
                    c = slice(n * 512, (n + 1) * 512)
                    for j in (2 * p, 2 * p + 1):
                        g = j % GRP
                        last = nc.tensor.matmul(PSO[n][g * CP:(g + 1) * CP, :], PR[:, j, :], bufs[j % 2][:, c],
                                                start=(j < GRP), stop=(j >= PAGES - GRP and g > 0), tile_position=(0, g * CP))
                if p == VG - 1:
                    pe.wait_ge(vn_in, 16 * b + 16)
                    for n in range(2):
                        last = nc.tensor.matmul(PSO[n][0:CP, :], PR[:, PAGES, :], vn[:, n * 512:(n + 1) * 512],
                                                start=False, stop=True, tile_position=(0, 0))
                last.then_inc(pv_mm, 1)

            def row(b, u):
                pe.wait_ge(om_ok, b + 1)
                pe.wait_ge(sb_ok, 2 * u)
                for n in range(2):
                    last = nc.tensor.matmul(SC_B[n][:, :], m.ones[:, :], om[:, n * 512:(n + 1) * 512], start=True, stop=True)
                last.then_inc(or_mm, 1)

            def softmax(b):
                pe.wait_ge(mx_ok, b + 1)
                nc.tensor.transpose(MISC[0:C, 0:P], m1, m.ident[:, :]).then_inc(mx_tr, 1)
                pe.wait_ge(mr_ok, b + 1)
                nc.tensor.matmul(MISC[:, P:P + C], m.ones[0:C, :], dg, start=True, stop=True).then_inc(mb_mm, 1)
                pe.wait_ge(l_ok, b + 1)
                nc.tensor.matmul(MISC[:, 160:161], lw.rearrange("p g c -> p (g c)"), m.ones[:, 0:1], start=True, stop=True).then_inc(l_mm, 1)

            def body(b):
                st = isinstance(b, int)
                for i in range(NQ):
                    u = NQ * b + i
                    if i == 0:
                        pe.wait_ge(kt_ok, b + 1)
                    wait(pe, sb_ok, 2 * u)
                    if i == 2 and not (st and b < 2):
                        pe.wait_ge(or_ev, b - 1)
                    for j in range(2):
                        r = slice(j * DHB, (j + 1) * DHB)
                        last = nc.tensor.matmul(SC_B[j][:, 0:(i + 1) * P], qh[r, i * P:(i + 1) * P],
                                                kth[r, 0:(i + 1) * P], start=True, stop=True)
                    last.then_inc(sc_mm, 1)
                    if i == 2 and not (st and b == HB - 1):
                        k_transpose(b + 1)
                    if not (st and b == 0):
                        values(b - 1, 2 * i)
                    if i:
                        finish(u - 1, i - 1, b)
                    if not (st and b == 0):
                        values(b - 1, 2 * i + 1)
                    if i == 1 and not (st and b < 2):
                        row(b - 2, u + 1)
                softmax(b)
                finish(NQ * b + NQ - 1, NQ - 1, b)
            k_transpose(0)
            seqs(pe, body)
            row(NS - 2, HB * NQ)
            for p in range(VG):
                values(NS - 1, p)
            pe.wait_ge(or_ev, NS - 1)
            row(NS - 1, HB * NQ)

        @block.scalar
        def _(s):
            def stage(h):
                wait(s, k_tr, h)
                nc.scalar.copy(khr, m.kk[:, 0:NQ, bass.ds(h * P, P)]).then_inc(kr_ok, 1)

            def q_copy(h):
                wait(s, sc_mm, NQ * h)
                nc.scalar.copy(qh, m.qt[:, bass.ds(h, 1), :].rearrange("p a t -> p (a t)"))

            def k_copy(h):
                s.wait_ge(k_tr, h + 1)
                nc.scalar.copy(kth, KT_B[:, :]).then_inc(kt_ok, 1)

            def c_copy(u, i):
                s.wait_ge(c_tr, u + 1)
                wait(s, o_mm, u - 1)
                nc.scalar.copy(ct[i % 2][:, 0:(i + 1) * P], CT_B[:, 0:(i + 1) * P]).then_inc(c_cp, 1)

            def row_out(b):
                s.wait_ge(or_mm, b + 1)
                wait(s, o_out, 16 * b)
                for n in range(2):
                    last = nc.scalar.copy(orow[:, n * 512:(n + 1) * 512], SC_B[n][0:1, :])
                last.then_inc(or_ev, 1)
                s.wait_ge(or_ev, b + 1)
                s.dma_start(m.osD[bass.ds(b, 1), :], orow).then_inc(o_out, 16)

            def body(b):
                st = isinstance(b, int)
                for i in range(NQ):
                    u = NQ * b + i
                    if i:
                        c_copy(u - 1, i - 1)
                    s.wait_ge(nb_ok, u + 1)
                    for j in range(2):
                        x = SP[i % 2][j][:, 0:(i + 1) * P]
                        last = nc.scalar.activation(x, x, ACT.Exp, bias=mx[i % 2][:, j:j + 1], accum_out=ls[i % 2][:, j:j + 1])
                    last.then_inc(p_ok, 1)
                    if i == 1 and not (st and b == HB - 1):
                        stage(b + 1)
                    if i == NQ - 1 and not (st and b == HB - 1):
                        q_copy(b + 1)
                        k_copy(b + 1)
                    if i == 1 and not (st and b < 2):
                        row_out(b - 2)
                s.wait_ge(sh_ok, b + 1)
                wait(s, pv_mm, VG * b)
                nc.scalar.activation(PR[:, :, 0:C], S, ACT.Exp).then_inc(e_ok, 1)
                c_copy(NQ * b + NQ - 1, NQ - 1)
            s.wait_ge(z_ok, 4)
            stage(0)
            q_copy(0)
            k_copy(0)
            seqs(s, body)
            row_out(NS - 2)
            row_out(NS - 1)

        @block.vector
        def _(v):
            V = nc.vector
            v.wait_ge(t1, 2 * GRP + 1)
            for h in range(HB):
                V.tensor_scalar(BT[:, 0:PAGES, 2 * h:2 * h + 2], nd.unsqueeze(2).to_broadcast([P, PAGES, 2]),
                                2.0 ** (-8.0 * (h + 1) / HB), None, ALU.mult)

            def weigh(u, i):
                v.wait_ge(p_ok, u + 1)
                p1, p2 = (SP[i % 2][j][:, 0:(i + 1) * P] for j in range(2))
                V.reciprocal(r1[i], ls[i % 2][:, 1:2])
                V.tensor_scalar(lm, ls[i % 2][:, 0:1], m.lam, -1.0, ALU.mult, ALU.mult)
                v.drain()
                V.tensor_tensor(lm, lm, r1[i], ALU.mult)
                v.drain()
                V.reciprocal(r1[i], ls[i % 2][:, 0:1])
                V.scalar_tensor_tensor(out=p1, in0=p2, scalar=lm, in1=p1, op0=ALU.mult, op1=ALU.add).then_inc(c_ok, 1)

            def keep(u, i, h):
                v.wait_ge(o_mm, u + 1)
                V.tensor_scalar(m.v[:, i, bass.ds(h * DVB, DVB)], O_B[:, (i % 2) * DVB:(i % 2 + 1) * DVB], r1[i], None,
                                ALU.mult).then_inc(o_ev, 1)

            def unit(b, i):
                st = isinstance(b, int)
                u, w = NQ * b + i, (i + 1) * P
                v.wait_ge(sc_mm, u + 1)
                wait(v, c_tr, u - 1)
                for j in range(2):
                    V.scalar_tensor_tensor(out=SP[i % 2][j][:, 0:w], in0=m.dist[:, SEQ - w:SEQ], scalar=m.slope[:, bass.ds(b, 1)],
                                           in1=SC_B[j][:, 0:w], op0=ALU.mult, op1=ALU.add).then_inc(sb_ok, 1)
                v.drain()
                for j in range(2):
                    V.tensor_reduce(out=mx[i % 2][:, j:j + 1], in_=SP[i % 2][j][:, 0:w], axis=AX.X, op=ALU.max)
                v.drain()
                V.tensor_scalar(mx[i % 2], mx[i % 2], -1.0, None, ALU.mult).then_inc(nb_ok, 1)

            def multiply(b, j):
                if j < PAGES:
                    v.wait_ge(k_in[j % RING], 16 * (PAGES // RING) * b + 16 * (j // RING + 1))
                if j:
                    v.wait_ge(ks_ok, NP * b + j - 3)
                V.tensor_tensor(v_prod, kp[j % RING] if j < PAGES else kn, qb, ALU.mult).then_inc(dp_ok, 1)

            def sum_page(b, j):
                if j % 4:
                    n = g_pages.index(j)
                    v.wait_ge(pp_ok, NPOOL * b + n + 1)
                    prod = g_prod[n % 2]
                else:
                    v.wait_ge(dp_ok, NV * b + j // 4 + 1)
                    prod = v_prod
                V.tensor_reduce(out=S[:, j, :], in_=prod.rearrange("p (c d) -> p c d", d=DHB),
                                axis=AX.X, op=ALU.add).then_inc(ks_ok, 1)

            def fold(b):
                v.wait_ge(pv_mm, VG * (b + 1))
                wait(v, or_mm, b)
                for n in range(2):
                    c = slice(n * 512, (n + 1) * 512)
                    last = V.scalar_tensor_tensor(out=om[:, c], in0=PSO[n][:, :], scalar=cf, in1=bmask[:, c], op0=ALU.mult, op1=ALU.mult)
                last.then_inc(om_ok, 1)

            def body(b):
                st = isinstance(b, int)
                v.wait_ge(q_in, 16 * b + 16)
                v.wait_ge(kn_in, 16 * b + 16)
                multiply(b, 0)
                for i in range(NQ):
                    sum_page(b, 4 * i)
                    sum_page(b, 4 * i + 1)
                    if i:
                        weigh(NQ * b + i - 1, i - 1)
                    if i > 1:
                        keep(NQ * b + i - 2, i - 2, b)
                    elif i == 1 and not (st and b == 0):
                        keep(NQ * b - 1, NQ - 1, b - 1)
                    sum_page(b, 4 * i + 2)
                    multiply(b, 4 * i + 4)
                    sum_page(b, 4 * i + 3)
                    unit(b, i)
                sum_page(b, PAGES)
                v.drain()
                V.tensor_tensor(S, S, BT, ALU.add)
                v.drain()
                V.tensor_reduce(out=m1, in_=S.rearrange("p j c -> p c j"), axis=AX.X, op=ALU.max).then_inc(mx_ok, 1)
                weigh(NQ * b + NQ - 1, NQ - 1)
                v.wait_ge(mx_tr, b + 1)
                V.tensor_reduce(out=mr, in_=MISC[0:C, 0:P], axis=AX.X, op=ALU.max)
                v.drain()
                V.tensor_scalar(dg, m.ident[0:C, 0:C], mr, None, ALU.mult).then_inc(mr_ok, 1)
                keep(NQ * b + NQ - 2, NQ - 2, b)
                v.wait_ge(mb_mm, b + 1)
                V.tensor_tensor(S, S, MISC[:, P:P + C].unsqueeze(1).to_broadcast([P, NP, C]), ALU.subtract).then_inc(sh_ok, 1)
                if not (st and b == 0):
                    fold(b - 1)
                v.wait_ge(e_ok, b + 1)
                V.tensor_reduce(out=lsum, in_=PR[:, :, 0:C].rearrange("p j c -> p c j"), axis=AX.X, op=ALU.add)
                v.drain()
                V.tensor_copy(lw[:, :, 0:C], lsum.unsqueeze(1).to_broadcast([P, GRP, C])).then_inc(l_ok, 1)
                v.wait_ge(l_mm, b + 1)
                V.reciprocal(cf, MISC[:, 160:161])
                v.drain()
                V.tensor_tensor(cf, cf, m.coef, ALU.mult)
                v.drain()
            seqs(v, body)
            keep(HB * NQ - 1, NQ - 1, HB - 1)
            fold(NS - 1)
            v.drain()
            V.memset(m.xt[:, :, TOK:SEQ + 32], 0.0)


OUTS = [("y_prompt", (1, SEQ, D)), ("y_sample", (NS, 1, D)), ("s_prompt", (1, 1, HA, DKA, DVA)),
        ("s_sample", (1, NS, HA, DKA, DVA)), ("k_prompt", (1, SEQ // PAGE, PAGE, HB, 2 * DHB)),
        ("v_prompt", (1, SEQ // PAGE, PAGE, HB, DVB)), ("k_sample", (NS, 1, HB, 2 * DHB)),
        ("v_sample", (NS, 1, HB, DVB))]


def build(nc, a):
    held.clear()
    with ExitStack() as ctx:
        m = allocate(nc, ctx)
        stage_constants(nc, ctx, m)
        stage_ada(nc, ctx, m, a)
        w_first = first_chunks(nc, ctx, m, "glap", a["w_in_a"][0])
        stage_modulate(nc, ctx, m, "mix0", 0, 3, load_x=(a["x_prompt"], a["x_sample"]), ahead=w_first)
        stage_ln_rows(nc, ctx, m, "lnm0", a["ln_mix_g"][0], a["ln_mix_b"][0])
        stage_gla_project(nc, ctx, m, a, w_first)
        stage_gla_prompt(nc, ctx, m, a)
        stage_gla_sample(nc, ctx, m, a)
        stage_mix_output(nc, ctx, m, "glao", HA, a["gn_a"][0], True, 1.0, a["w_o_a"][0])
        stage_modulate(nc, ctx, m, "ffn0", 3, 3, keep_rows=True)
        weights = expert_weights(nc, ctx, m, 0, a)
        stage_route(nc, ctx, m, 0, a, weights)
        stage_experts(nc, ctx, m, 0, weights)
        stage_combine(nc, ctx, m, 0)
        free_semaphores(nc)
        w_first = first_chunks(nc, ctx, m, "kv", a["w_kv"])
        stage_modulate(nc, ctx, m, "kvm", 12, 2, ahead=w_first)
        stage_shared_kv(nc, ctx, m, a, w_first)
        w_first = first_chunks(nc, ctx, m, "q", a["w_q_b"][0])
        stage_modulate(nc, ctx, m, "mix1", 6, 3, ahead=w_first)
        stage_queries(nc, ctx, m, a, w_first)
        stage_attention(nc, ctx, m, a)
        free_semaphores(nc)
        stage_ln_rows(nc, ctx, m, "lnm1", a["ln_mix_g"][1], a["ln_mix_b"][1])
        stage_mix_output(nc, ctx, m, "diffo", HB, a["subln_b"][0], False, 1.0 - LAM_INIT, a["w_o_b"][0])
        stage_modulate(nc, ctx, m, "ffn1", 9, 3, keep_rows=True)
        weights = expert_weights(nc, ctx, m, 1, a)
        stage_route(nc, ctx, m, 1, a, weights)
        stage_experts(nc, ctx, m, 1, weights)
        stage_combine(nc, ctx, m, 1, stores=(a["y_prompt"], a["y_sample"]))


def kernel(**inputs):
    import numpy as _np
    import concourse.bacc as _bacc
    from concourse import mybir as _mybir
    from concourse.bass_utils import run_bass_kernel_spmd as _run

    nc = _bacc.Bacc("TRN2", target_bir_lowering=False, num_devices=1)
    arrays, a = {}, {}
    for name, value in inputs.items():
        x = _np.ascontiguousarray(value)
        arrays[f"in_{name}_dram"] = x
        a[name] = nc.dram_tensor(f"in_{name}_dram", x.shape, _mybir.dt.from_np(x.dtype), kind="ExternalInput").ap()
    for name, shape in OUTS:
        a[name] = nc.dram_tensor(f"out_{name}_dram", shape, F32, kind="ExternalOutput").ap()
    build(nc, a)
    r = _run(nc, [arrays], core_ids=[0])
    return tuple(r.results[0][f"out_{name}_dram"] for name, _ in OUTS)
```
